# Optimizing a Trainium2 kernel written in Bass

```python
import math
import jax, jax.numpy as jnp
from jax import lax
import numpy as np
import jax
import jax.numpy as jnp

D_MODEL = 2048
BATCH = 1
SEQ = 256
DEPTH = 1

N_MIXERS = 4
GROUP_WIDTH = D_MODEL // N_MIXERS
N_HEADS_GLA = 4
N_HEADS_GDN = 4
N_POOL_GROUPS = 4
N_HEADS_FOX = 4
HEAD_DIM = GROUP_WIDTH // 4
GLA_KEY_DIM = HEAD_DIM // 2
GLA_GATE_RANK = 16
GLA_GATE_TAU = 16.0
GDN_CONV = 4
POOL_WINDOWS = (2, 4, 8, 16)
POOL_GROUP_DIM = GROUP_WIDTH // N_POOL_GROUPS
CHUNK = 64
FOX_BLOCK = 128
D_FF = 256 * int(math.ceil(8 * D_MODEL / 3 / 256))
FFN_CONV = 3
EPS = 1e-6

IN_SPLITS = (
    N_HEADS_GLA * GLA_KEY_DIM,
    N_HEADS_GLA * GLA_KEY_DIM,
    GROUP_WIDTH,
    GROUP_WIDTH,
    GLA_GATE_RANK,
    3 * GROUP_WIDTH,
    GROUP_WIDTH,
    N_HEADS_GDN,
    N_HEADS_GDN,
    GROUP_WIDTH,
    GROUP_WIDTH,
    GROUP_WIDTH,
    GROUP_WIDTH,
    N_HEADS_FOX,
)
IN_WIDTH = sum(IN_SPLITS)
SPLIT_IDX = tuple(sum(IN_SPLITS[:i + 1]) for i in range(len(IN_SPLITS) - 1))


def rmsnorm(x, w):
    xf = x.astype(jnp.float32)
    y = xf * lax.rsqrt(jnp.mean(xf * xf, axis=-1, keepdims=True) + EPS)
    return (y * w.astype(jnp.float32)).astype(x.dtype)

def l2norm(x):
    return x * lax.rsqrt(jnp.sum(x * x, axis=-1, keepdims=True) + EPS)

def causal_dwconv(x, w):
    width, T = w.shape[0], x.shape[1]
    xp = jnp.pad(x, ((0, 0), (width - 1, 0), (0, 0)))
    return sum(xp[:, j:j + T] * w[j] for j in range(width))

def gla_mixer(q, k, v, g_out, g_lr, w_lr, b_lr, norm_w):
    B, T, _ = q.shape
    H, dk, dv, C = N_HEADS_GLA, GLA_KEY_DIM, HEAD_DIM, CHUNK
    N = T // C
    logg = jax.nn.log_sigmoid(g_lr @ w_lr + b_lr) / GLA_GATE_TAU
    to_c = lambda t, d: jnp.transpose(t.reshape(B, N, C, H, d), (1, 0, 3, 2, 4))
    qc, kc, vc = to_c(q * dk ** -0.5, dk), to_c(k, dk), to_c(v, dv)
    bcum = jnp.cumsum(to_c(logg, dk), axis=3)
    causal = jnp.tril(jnp.ones((C, C), bool))[:, :, None]

    def step(S, inp):
        qi, ki, vi, bi = inp
        diff = bi[:, :, :, None, :] - bi[:, :, None, :, :]
        decay = jnp.exp(jnp.where(causal, diff, -jnp.inf))
        att = jnp.einsum('bhtd,bhsd,bhtsd->bhts', qi, ki, decay)
        o = jnp.einsum('bhts,bhsv->bhtv', att, vi) + jnp.einsum('bhtd,bhdv->bhtv', qi * jnp.exp(bi), S)
        blast = bi[:, :, -1:, :]
        S = S * jnp.exp(blast)[:, :, 0, :, None] + jnp.einsum('bhsd,bhsv->bhdv', ki * jnp.exp(blast - bi), vi)
        return S, o

    S0 = jnp.zeros((B, H, dk, dv), jnp.float32)
    _, o = lax.scan(step, S0, (qc, kc, vc, bcum))
    o = jnp.transpose(o, (1, 0, 3, 2, 4)).reshape(B, T, H, dv)
    o = rmsnorm(o, norm_w) * jax.nn.silu(g_out.reshape(B, T, H, dv))
    return o.reshape(B, T, H * dv)

def gated_deltanet_mixer(qkv, g_out, beta_in, a_in, conv_w, a_log, dt_bias, norm_w):
    B, T, _ = qkv.shape
    H, d, C = N_HEADS_GDN, HEAD_DIM, CHUNK
    N = T // C
    qkv = jax.nn.silu(causal_dwconv(qkv, conv_w))
    q, k, v = jnp.split(qkv, 3, axis=-1)
    q = l2norm(q.reshape(B, T, H, d)) * d ** -0.5
    k = l2norm(k.reshape(B, T, H, d))
    v = v.reshape(B, T, H, d)
    beta = jax.nn.sigmoid(beta_in)
    g = -jnp.exp(a_log) * jax.nn.softplus(a_in + dt_bias)
    to_c = lambda t: jnp.moveaxis(t.reshape(B, N, C, H, -1), 3, 1)
    qc, kc, vc = to_c(q), to_c(k), to_c(v)
    bc = to_c(beta[..., None])
    gcum = jnp.cumsum(to_c(g[..., None])[..., 0], axis=-1)
    incl = jnp.tril(jnp.ones((C, C), bool))
    strict = jnp.tril(jnp.ones((C, C), bool), -1)
    decay = jnp.exp(jnp.where(incl, gcum[..., :, None] - gcum[..., None, :], -jnp.inf))
    kbeta = kc * bc
    lmat = jnp.where(strict, jnp.einsum('bhnid,bhnjd->bhnij', kbeta, kc) * decay, 0.0)
    rhs = jnp.concatenate([vc * bc, kbeta * jnp.exp(gcum)[..., None]], axis=-1)
    sol = lax.linalg.triangular_solve(lmat + jnp.eye(C, dtype=lmat.dtype), rhs,
                                      left_side=True, lower=True, unit_diagonal=True)
    u, w = sol[..., :d], sol[..., d:]
    attn = jnp.einsum('bhnid,bhnjd->bhnij', qc, kc) * decay

    def step(S, inp):
        q_i, k_i, u_i, w_i, a_i, g_i = inp
        v_new = u_i - jnp.einsum('bhck,bhkv->bhcv', w_i, S)
        o = (jnp.einsum('bhck,bhkv->bhcv', q_i * jnp.exp(g_i)[..., None], S)
             + jnp.einsum('bhij,bhjv->bhiv', a_i, v_new))
        g_last = g_i[..., -1:]
        S = S * jnp.exp(g_last)[..., None] + jnp.einsum(
            'bhck,bhcv->bhkv', k_i * jnp.exp(g_last - g_i)[..., None], v_new)
        return S, o

    xs = tuple(jnp.moveaxis(t, 2, 0) for t in (qc, kc, u, w, attn, gcum))
    S0 = jnp.zeros((B, H, d, d), jnp.float32)
    _, o = lax.scan(step, S0, xs)
    o = jnp.moveaxis(jnp.moveaxis(o, 0, 2), 1, 3).reshape(B, T, H, d)
    o = rmsnorm(o, norm_w) * jax.nn.silu(g_out.reshape(B, T, H, d))
    return o.reshape(B, T, H * d)

def pool_mixer(u, w_grp, scale):
    B, T, Cw = u.shape
    cs = jnp.pad(jnp.cumsum(u, axis=1), ((0, 0), (1, 0), (0, 0)))
    pos = jnp.arange(1, T + 1, dtype=jnp.float32)
    outs = []
    for gi, win in enumerate(POOL_WINDOWS):
        sl = slice(gi * POOL_GROUP_DIM, (gi + 1) * POOL_GROUP_DIM)
        csg = cs[:, :, sl]
        lower = jnp.pad(csg[:, :T - win + 1], ((0, 0), (win - 1, 0), (0, 0)))
        mean = (csg[:, 1:] - lower) / jnp.minimum(pos, float(win))[None, :, None]
        outs.append(mean - u[:, :, sl])
    dlt = jnp.stack(outs, axis=2)
    y = jnp.einsum('btgc,gcd->btgd', dlt, w_grp).reshape(B, T, Cw)
    return y * scale

def forgetting_attention(q, k, v, f_in, f_bias):
    B, T, _ = q.shape
    H, d = N_HEADS_FOX, HEAD_DIM
    heads = lambda t: jnp.moveaxis(t.reshape(B, T, H, d), 2, 1)
    q, k, v = heads(q) * d ** -0.5, heads(k), heads(v)
    F = jnp.cumsum(jnp.moveaxis(jax.nn.log_sigmoid(f_in + f_bias), 2, 1), axis=-1)
    outs = []
    for i in range(T // FOX_BLOCK):
        s0, e = i * FOX_BLOCK, (i + 1) * FOX_BLOCK
        logits = (jnp.einsum('bhqd,bhkd->bhqk', q[:, :, s0:e], k[:, :, :e])
                  + F[:, :, s0:e, None] - F[:, :, None, :e])
        mask = jnp.arange(s0, e)[:, None] >= jnp.arange(e)[None, :]
        p = jax.nn.softmax(jnp.where(mask, logits, -jnp.inf), axis=-1)
        outs.append(jnp.einsum('bhqk,bhkd->bhqd', p, v[:, :, :e]))
    o = jnp.concatenate(outs, axis=2)
    return jnp.moveaxis(o, 1, 2).reshape(B, T, H * d)

def conv_ffn(h, w_gate, w_up, conv_w, conv_b, w_down):
    gate = causal_dwconv(h @ w_gate, conv_w) + conv_b
    return (jax.nn.silu(gate) * (h @ w_up)) @ w_down

def first_inputs(seed: int = 0) -> dict:
    key = jax.random.key(seed)
    ks = iter(jax.random.split(key, 32))
    nrm = lambda shape, s: jax.random.normal(next(ks), shape, jnp.float32) * s
    L, D, F = DEPTH, D_MODEL, D_FF
    x = nrm((BATCH, SEQ, D), 1.0)
    c = nrm((BATCH, D), 1.0)
    w_mod = nrm((L, D, 6 * D), 0.5 * D ** -0.5)
    b_mod = nrm((L, 6 * D), 0.02)
    norm_mix = 1.0 + nrm((L, D), 0.1)
    norm_ffn = 1.0 + nrm((L, D), 0.1)
    w_in = nrm((L, D, IN_WIDTH), D ** -0.5)
    gla_w_lr = nrm((L, GLA_GATE_RANK, N_HEADS_GLA * GLA_KEY_DIM), GLA_GATE_RANK ** -0.5)
    gla_b_lr = nrm((L, N_HEADS_GLA * GLA_KEY_DIM), 0.1)
    gla_norm = 1.0 + nrm((L, HEAD_DIM), 0.1)
    gdn_conv = nrm((L, GDN_CONV, 3 * GROUP_WIDTH), GDN_CONV ** -0.5)
    gdn_a_log = jnp.log(jax.random.uniform(next(ks), (L, N_HEADS_GDN), jnp.float32, 1.0, 16.0))
    dt = jnp.exp(jax.random.uniform(next(ks), (L, N_HEADS_GDN), jnp.float32, math.log(1e-3), math.log(1e-1)))
    gdn_dt_bias = dt + jnp.log(-jnp.expm1(-dt))
    gdn_norm = 1.0 + nrm((L, HEAD_DIM), 0.1)
    pool_w = nrm((L, N_POOL_GROUPS, POOL_GROUP_DIM, POOL_GROUP_DIM), POOL_GROUP_DIM ** -0.5)
    pool_scale = 1.0 + nrm((L, GROUP_WIDTH), 0.1)
    fox_f_bias = 2.0 + nrm((L, N_HEADS_FOX), 0.5)
    w_out = nrm((L, D, D), D ** -0.5)
    ffn_w_gate = nrm((L, D, F), D ** -0.5)
    ffn_w_up = nrm((L, D, F), D ** -0.5)
    ffn_conv_w = nrm((L, FFN_CONV, F), FFN_CONV ** -0.5)
    ffn_conv_b = nrm((L, F), 0.02)
    ffn_w_down = nrm((L, F, D), F ** -0.5)
    norm_final = 1.0 + nrm((D,), 0.1)
    return {"x": x, "c": c, "w_mod": w_mod, "b_mod": b_mod, "norm_mix": norm_mix, "norm_ffn": norm_ffn,
            "w_in": w_in, "gla_w_lr": gla_w_lr, "gla_b_lr": gla_b_lr, "gla_norm": gla_norm,
            "gdn_conv": gdn_conv, "gdn_a_log": gdn_a_log, "gdn_dt_bias": gdn_dt_bias, "gdn_norm": gdn_norm,
            "pool_w": pool_w, "pool_scale": pool_scale, "fox_f_bias": fox_f_bias, "w_out": w_out,
            "ffn_w_gate": ffn_w_gate, "ffn_w_up": ffn_w_up, "ffn_conv_w": ffn_conv_w,
            "ffn_conv_b": ffn_conv_b, "ffn_w_down": ffn_w_down, "norm_final": norm_final}

def first_block(x, c, w_mod, b_mod, norm_mix, norm_ffn, w_in, gla_w_lr, gla_b_lr, gla_norm,
              gdn_conv, gdn_a_log, gdn_dt_bias, gdn_norm, pool_w, pool_scale, fox_f_bias, w_out,
              ffn_w_gate, ffn_w_up, ffn_conv_w, ffn_conv_b, ffn_w_down, norm_final):
    B, T, D = x.shape
    f32 = lambda t: t.astype(jnp.float32)
    cond = jax.nn.silu(c)
    for l in range(DEPTH):
        mod = (cond @ w_mod[l] + b_mod[l]).reshape(B, 6, D)
        sh1, sc1, g1, sh2, sc2, g2 = [mod[:, i, None, :] for i in range(6)]

        h = rmsnorm(x, norm_mix[l]) * (1.0 + sc1) + sh1
        proj = f32(h @ w_in[l])
        (gla_q, gla_k, gla_v, gla_g, gla_lr, gdn_qkv, gdn_g, gdn_b, gdn_a,
         pool_u, fox_q, fox_k, fox_v, fox_f) = jnp.split(proj, SPLIT_IDX, axis=-1)
        y_a = gla_mixer(gla_q, gla_k, gla_v, gla_g, gla_lr, f32(gla_w_lr[l]), f32(gla_b_lr[l]), gla_norm[l])
        y_b = gated_deltanet_mixer(gdn_qkv, gdn_g, gdn_b, gdn_a, f32(gdn_conv[l]), f32(gdn_a_log[l]),
                                   f32(gdn_dt_bias[l]), gdn_norm[l])
        y_c = pool_mixer(pool_u, f32(pool_w[l]), f32(pool_scale[l]))
        y_d = forgetting_attention(fox_q, fox_k, fox_v, fox_f, f32(fox_f_bias[l]))
        y = jnp.concatenate([y_a, y_b, y_c, y_d], axis=-1).astype(x.dtype) @ w_out[l]
        x = x + g1 * y

        h = rmsnorm(x, norm_ffn[l]) * (1.0 + sc2) + sh2
        x = x + g2 * conv_ffn(h, ffn_w_gate[l], ffn_w_up[l], ffn_conv_w[l], ffn_conv_b[l], ffn_w_down[l])
    return rmsnorm(x, norm_final)


HEAD_DIM_2 = 64
NSA_HEADS = 16
NSA_KV_HEADS = 2
NSA_HPG = NSA_HEADS // NSA_KV_HEADS
CMP_LEN = 32
CMP_STRIDE = 16
CMP_HIDDEN = 128
SLC_BLOCK = 64
N_SELECT = 16
NSA_WINDOW = 512
FORCE_BONUS = 1e4
SWA_HEADS = 16
SWA_KV_HEADS = 2
SWA_HPG = SWA_HEADS // SWA_KV_HEADS
SWA_WINDOW = 128
REL_BUCKETS = 32
REL_EXACT = 16
REL_MAX_DIST = 2048
PEER_HEADS = 8
PEER_NKEYS = 128
PEER_EXPERTS = PEER_NKEYS * PEER_NKEYS
PEER_QDIM = 256
PEER_TOPK = 16
PEER_CHUNK = 128

Q_BLOCK = 128
NEG = -1e30
RMS_EPS = 1e-6
NSA_Q_W = NSA_HEADS * HEAD_DIM_2
NSA_KV_W = NSA_KV_HEADS * HEAD_DIM_2
NSA_GATE_W = NSA_HEADS * 3
SWA_Q_W = SWA_HEADS * HEAD_DIM_2
SWA_KV_W = SWA_KV_HEADS * HEAD_DIM_2
MIX_WIDTH = NSA_Q_W + SWA_Q_W
PROJ_SPLITS = (NSA_Q_W, NSA_KV_W, NSA_KV_W, NSA_KV_W, NSA_KV_W, NSA_KV_W, NSA_KV_W, NSA_GATE_W, SWA_Q_W, SWA_KV_W, SWA_KV_W)
PROJ_WIDTH = sum(PROJ_SPLITS)
SLC_OFFSETS = (-1, 0, 1, 2, 3)
SLC_WEIGHTS = (1.0, 2.0, 2.0, 2.0, 1.0)


def rmsnorm_2(x, g):
    xf = x.astype(jnp.float32)
    y = xf * lax.rsqrt(jnp.mean(xf * xf, axis=-1, keepdims=True) + RMS_EPS)
    return (y * g.astype(jnp.float32)).astype(x.dtype)

def rel_bucket(dist):
    d = jnp.maximum(dist, 0)
    n_log = REL_BUCKETS - REL_EXACT
    large = REL_EXACT + (jnp.log(jnp.maximum(d, 1).astype(jnp.float32) / REL_EXACT)
                         / math.log(REL_MAX_DIST / REL_EXACT) * n_log).astype(jnp.int32)
    large = jnp.minimum(large, REL_BUCKETS - 1)
    return jnp.where(d < REL_EXACT, d, large)

def masked_softmax(logits, valid):
    p = jax.nn.softmax(jnp.where(valid, logits, NEG), axis=-1)
    return jnp.where(valid, p, 0.0)

def compress(k, pos, w1, w2):
    B, S, G, Dh = k.shape
    chunks = k.reshape(B, S // CMP_STRIDE, CMP_STRIDE, G, Dh)
    blocks = jnp.concatenate([chunks[:, :-1], chunks[:, 1:]], axis=2)
    blocks = blocks + pos[None, None, :, None, :]
    flat = jnp.moveaxis(blocks, 3, 2).reshape(B, blocks.shape[1], G, CMP_LEN * Dh)
    return jax.nn.gelu(flat @ w1) @ w2

def hybrid_mixer(xn, w_in, cmp_pos_k, cmp_w1_k, cmp_w2_k, cmp_pos_v, cmp_w1_v, cmp_w2_v,
                 sinks, rel_bias, w_out):
    B, S, _ = xn.shape
    f32 = jnp.float32
    GA, GB = NSA_KV_HEADS, SWA_KV_HEADS
    NS = S // SLC_BLOCK
    n_sel = min(N_SELECT, NS)
    scale = HEAD_DIM_2 ** -0.5
    offs = [int(c) for c in np.cumsum(PROJ_SPLITS)[:-1]]
    (q_a, kc, vc, ks, vs, kw, vw, gate_a, q_b, k_b, v_b) = jnp.split(xn @ w_in, offs, axis=-1)

    q_a = q_a.reshape(B, S, GA, NSA_HPG, HEAD_DIM_2)
    q_b = q_b.reshape(B, S, GB, SWA_HPG, HEAD_DIM_2)
    gate_a = jax.nn.sigmoid(gate_a).reshape(B, S, GA, NSA_HPG, 3)
    kc_c = compress(kc.reshape(B, S, GA, HEAD_DIM_2), cmp_pos_k, cmp_w1_k, cmp_w2_k)
    vc_c = compress(vc.reshape(B, S, GA, HEAD_DIM_2), cmp_pos_v, cmp_w1_v, cmp_w2_v)
    n_cmp = kc_c.shape[1]
    cmp_end = jnp.arange(n_cmp) * CMP_STRIDE + CMP_LEN - 1
    ks_blk = ks.reshape(B, NS, SLC_BLOCK, GA, HEAD_DIM_2).transpose(0, 3, 1, 2, 4)
    vs_blk = vs.reshape(B, NS, SLC_BLOCK, GA, HEAD_DIM_2).transpose(0, 3, 1, 2, 4)
    pad_a = ((0, 0), (NSA_WINDOW, 0), (0, 0), (0, 0))
    kw_pad = jnp.pad(kw.reshape(B, S, GA, HEAD_DIM_2), pad_a)
    vw_pad = jnp.pad(vw.reshape(B, S, GA, HEAD_DIM_2), pad_a)
    pad_b = ((0, 0), (SWA_WINDOW, 0), (0, 0), (0, 0))
    kb_pad = jnp.pad(k_b.reshape(B, S, GB, HEAD_DIM_2), pad_b)
    vb_pad = jnp.pad(v_b.reshape(B, S, GB, HEAD_DIM_2), pad_b)

    bias_a = rel_bias[:, :NSA_HEADS].reshape(REL_BUCKETS, GA, NSA_HPG).astype(f32)
    bias_b = rel_bias[:, NSA_HEADS:].reshape(REL_BUCKETS, GB, SWA_HPG).astype(f32)
    sink = sinks.astype(f32).reshape(1, GB, SWA_HPG, 1, 1)
    b_idx = jnp.arange(B)[:, None, None, None]
    g_idx = jnp.arange(GA)[None, :, None, None]
    blk_ids = jnp.arange(NS)
    slc_tok = jnp.arange(SLC_BLOCK)

    def token_bias(table, dist):
        return table[rel_bucket(dist)].transpose(2, 3, 0, 1)

    def query_block(i):
        q0 = i * Q_BLOCK
        pos_q = q0 + jnp.arange(Q_BLOCK)
        qa = lax.dynamic_slice_in_dim(q_a, q0, Q_BLOCK, axis=1)
        dt = qa.dtype

        dist_c = pos_q[:, None] - cmp_end[None, :]
        lg_c = jnp.einsum('bqghd,bcgd->bghqc', qa, kc_c, preferred_element_type=f32) * scale
        p_cmp = masked_softmax(lg_c + token_bias(bias_a, dist_c), dist_c >= 0)
        o_cmp = jnp.einsum('bghqc,bcgd->bqghd', p_cmp.astype(dt), vc_c)

        imp = jnp.pad(p_cmp.sum(axis=2), ((0, 0), (0, 0), (0, 0), (1, 1)))
        imp_s = jnp.zeros(imp.shape[:-1] + (NS,), f32)
        for r, w in zip(SLC_OFFSETS, SLC_WEIGHTS):
            imp_s = imp_s + w * imp[..., r + 1: r + 2 + 4 * (NS - 1): 4]
        cb = pos_q[:, None] // SLC_BLOCK
        j = blk_ids[None, :]
        forced = (j == 0) | (j == cb) | (j == cb - 1)
        score = jnp.where(j > cb, NEG, imp_s + jnp.where(forced, FORCE_BONUS, 0.0))
        _, sel = lax.top_k(score, n_sel)
        ks_g = ks_blk[b_idx, g_idx, sel].reshape(B, GA, Q_BLOCK, n_sel * SLC_BLOCK, HEAD_DIM_2)
        vs_g = vs_blk[b_idx, g_idx, sel].reshape(B, GA, Q_BLOCK, n_sel * SLC_BLOCK, HEAD_DIM_2)
        kpos = (sel[..., None] * SLC_BLOCK + slc_tok).reshape(B, GA, Q_BLOCK, n_sel * SLC_BLOCK)
        dist_s = pos_q[:, None] - kpos
        bias_s = jnp.moveaxis(bias_a[rel_bucket(dist_s), g_idx], -1, 2)
        lg_s = jnp.einsum('bqghd,bgqkd->bghqk', qa, ks_g, preferred_element_type=f32) * scale
        p_s = masked_softmax(lg_s + bias_s, (dist_s >= 0)[:, :, None])
        o_slc = jnp.einsum('bghqk,bgqkd->bqghd', p_s.astype(dt), vs_g)

        La = Q_BLOCK + NSA_WINDOW
        kwin = lax.dynamic_slice_in_dim(kw_pad, q0, La, axis=1)
        vwin = lax.dynamic_slice_in_dim(vw_pad, q0, La, axis=1)
        kpos_w = q0 - NSA_WINDOW + jnp.arange(La)
        dist_w = pos_q[:, None] - kpos_w[None, :]
        valid_w = (dist_w >= 0) & (dist_w < NSA_WINDOW) & (kpos_w[None, :] >= 0)
        lg_w = jnp.einsum('bqghd,blgd->bghql', qa, kwin, preferred_element_type=f32) * scale
        p_w = masked_softmax(lg_w + token_bias(bias_a, dist_w), valid_w)
        o_win = jnp.einsum('bghql,blgd->bqghd', p_w.astype(dt), vwin)

        g = lax.dynamic_slice_in_dim(gate_a, q0, Q_BLOCK, axis=1)
        o_a = g[..., 0:1] * o_cmp + g[..., 1:2] * o_slc + g[..., 2:3] * o_win

        qb = lax.dynamic_slice_in_dim(q_b, q0, Q_BLOCK, axis=1)
        Lb = Q_BLOCK + SWA_WINDOW
        kbw = lax.dynamic_slice_in_dim(kb_pad, q0, Lb, axis=1)
        vbw = lax.dynamic_slice_in_dim(vb_pad, q0, Lb, axis=1)
        kpos_b = q0 - SWA_WINDOW + jnp.arange(Lb)
        dist_b = pos_q[:, None] - kpos_b[None, :]
        valid_b = (dist_b >= 0) & (dist_b < SWA_WINDOW) & (kpos_b[None, :] >= 0)
        lg_b = jnp.einsum('bqghd,blgd->bghql', qb, kbw, preferred_element_type=f32) * scale
        lg_b = jnp.where(valid_b, lg_b + token_bias(bias_b, dist_b), NEG)
        m = jnp.maximum(lg_b.max(axis=-1, keepdims=True), sink)
        e = jnp.exp(lg_b - m)
        p_b = e / (e.sum(axis=-1, keepdims=True) + jnp.exp(sink - m))
        o_b = jnp.einsum('bghql,blgd->bqghd', p_b.astype(dt), vbw)

        return jnp.concatenate([o_a.reshape(B, Q_BLOCK, NSA_Q_W),
                                o_b.reshape(B, Q_BLOCK, SWA_Q_W)], axis=-1)

    out = lax.map(query_block, jnp.arange(S // Q_BLOCK))
    out = out.transpose(1, 0, 2, 3).reshape(B, S, MIX_WIDTH)
    return out @ w_out

def peer(xn, wq, subkeys, u, v):
    B, S, D = xn.shape
    T = B * S
    xt = xn.reshape(T, D)
    q = (xt @ wq).reshape(T, PEER_HEADS, 2, PEER_QDIM // 2).astype(jnp.float32)
    s1 = jnp.einsum('thd,nd->thn', q[:, :, 0], subkeys[0].astype(jnp.float32))
    s2 = jnp.einsum('thd,nd->thn', q[:, :, 1], subkeys[1].astype(jnp.float32))
    v1, i1 = lax.top_k(s1, PEER_TOPK)
    v2, i2 = lax.top_k(s2, PEER_TOPK)
    cand = (v1[..., :, None] + v2[..., None, :]).reshape(T, PEER_HEADS, PEER_TOPK * PEER_TOPK)
    sc, ci = lax.top_k(cand, PEER_TOPK)
    e1 = jnp.take_along_axis(i1, ci // PEER_TOPK, axis=-1)
    e2 = jnp.take_along_axis(i2, ci % PEER_TOPK, axis=-1)
    idx = e1 * PEER_NKEYS + e2
    gate = jax.nn.softmax(sc, axis=-1).astype(xn.dtype)
    n_ch = T // PEER_CHUNK

    def chunk(args):
        xc, ic, gc = args
        h = jax.nn.gelu(jnp.einsum('cd,chkd->chk', xc, u[ic]))
        return jnp.einsum('chk,chkd->cd', gc * h, v[ic])

    out = lax.map(chunk, (xt.reshape(n_ch, PEER_CHUNK, D),
                          idx.reshape(n_ch, PEER_CHUNK, PEER_HEADS, PEER_TOPK),
                          gate.reshape(n_ch, PEER_CHUNK, PEER_HEADS, PEER_TOPK)))
    return out.reshape(B, S, D)

def second_inputs(seed: int = 0) -> dict:
    key = jax.random.key(seed)
    ks = jax.random.split(key, 18)

    def nrm(k, shape, s):
        return jax.random.normal(k, shape, jnp.float32) * s

    return {
        'x': nrm(ks[0], (BATCH, SEQ, D_MODEL), 1.0),
        'attn_norm': 1.0 + nrm(ks[1], (DEPTH, D_MODEL), 0.02),
        'w_in': nrm(ks[2], (DEPTH, D_MODEL, PROJ_WIDTH), D_MODEL ** -0.5),
        'cmp_pos_k': nrm(ks[3], (DEPTH, CMP_LEN, HEAD_DIM_2), 0.1),
        'cmp_w1_k': nrm(ks[4], (DEPTH, CMP_LEN * HEAD_DIM_2, CMP_HIDDEN), (CMP_LEN * HEAD_DIM_2) ** -0.5),
        'cmp_w2_k': nrm(ks[5], (DEPTH, CMP_HIDDEN, HEAD_DIM_2), CMP_HIDDEN ** -0.5),
        'cmp_pos_v': nrm(ks[6], (DEPTH, CMP_LEN, HEAD_DIM_2), 0.1),
        'cmp_w1_v': nrm(ks[7], (DEPTH, CMP_LEN * HEAD_DIM_2, CMP_HIDDEN), (CMP_LEN * HEAD_DIM_2) ** -0.5),
        'cmp_w2_v': nrm(ks[8], (DEPTH, CMP_HIDDEN, HEAD_DIM_2), CMP_HIDDEN ** -0.5),
        'sinks': nrm(ks[9], (DEPTH, SWA_HEADS), 0.5),
        'w_out': nrm(ks[10], (DEPTH, MIX_WIDTH, D_MODEL), MIX_WIDTH ** -0.5),
        'ffn_norm': 1.0 + nrm(ks[11], (DEPTH, D_MODEL), 0.02),
        'peer_wq': nrm(ks[12], (DEPTH, D_MODEL, PEER_HEADS * PEER_QDIM), D_MODEL ** -0.5),
        'peer_subkeys': nrm(ks[13], (DEPTH, 2, PEER_NKEYS, PEER_QDIM // 2), (PEER_QDIM // 2) ** -0.5),
        'peer_u': nrm(ks[14], (DEPTH, PEER_EXPERTS, D_MODEL), D_MODEL ** -0.5),
        'peer_v': nrm(ks[15], (DEPTH, PEER_EXPERTS, D_MODEL), (PEER_HEADS * PEER_TOPK) ** -0.5),
        'rel_bias': nrm(ks[16], (REL_BUCKETS, NSA_HEADS + SWA_HEADS), 0.5),
        'final_norm': 1.0 + nrm(ks[17], (D_MODEL,), 0.02),
    }

def second_block(x, attn_norm, w_in, cmp_pos_k, cmp_w1_k, cmp_w2_k, cmp_pos_v, cmp_w1_v, cmp_w2_v,
              sinks, w_out, ffn_norm, peer_wq, peer_subkeys, peer_u, peer_v, rel_bias, final_norm):
    h = x
    for l in range(DEPTH):
        h = h + hybrid_mixer(rmsnorm_2(h, attn_norm[l]), w_in[l],
                             cmp_pos_k[l], cmp_w1_k[l], cmp_w2_k[l],
                             cmp_pos_v[l], cmp_w1_v[l], cmp_w2_v[l],
                             sinks[l], rel_bias, w_out[l])
        h = h + peer(rmsnorm_2(h, ffn_norm[l]), peer_wq[l], peer_subkeys[l], peer_u[l], peer_v[l])
    return rmsnorm_2(h, final_norm)


def setup_inputs(seed=0):
    out = dict(first_inputs(seed))
    for name, value in second_inputs(seed + 1).items():
        if name != "x":
            out[name + "_2"] = value
    return out


def reference(
    x, c, w_mod, b_mod, norm_mix, norm_ffn, w_in, gla_w_lr, gla_b_lr, gla_norm, gdn_conv,
    gdn_a_log, gdn_dt_bias, gdn_norm, pool_w, pool_scale, fox_f_bias, w_out, ffn_w_gate,
    ffn_w_up, ffn_conv_w, ffn_conv_b, ffn_w_down, norm_final, attn_norm_2, w_in_2, cmp_pos_k_2,
    cmp_w1_k_2, cmp_w2_k_2, cmp_pos_v_2, cmp_w1_v_2, cmp_w2_v_2, sinks_2, w_out_2, ffn_norm_2,
    peer_wq_2, peer_subkeys_2, peer_u_2, peer_v_2, rel_bias_2, final_norm_2,
):
    x = first_block(
        x, c, w_mod, b_mod, norm_mix, norm_ffn, w_in, gla_w_lr, gla_b_lr, gla_norm, gdn_conv,
        gdn_a_log, gdn_dt_bias, gdn_norm, pool_w, pool_scale, fox_f_bias, w_out, ffn_w_gate,
        ffn_w_up, ffn_conv_w, ffn_conv_b, ffn_w_down, norm_final,
    )
    return second_block(
        x, attn_norm_2, w_in_2, cmp_pos_k_2, cmp_w1_k_2, cmp_w2_k_2, cmp_pos_v_2, cmp_w1_v_2,
        cmp_w2_v_2, sinks_2, w_out_2, ffn_norm_2, peer_wq_2, peer_subkeys_2, peer_u_2, peer_v_2,
        rel_bias_2, final_norm_2,
    )


_drawn_inputs = setup_inputs


def setup_inputs(seed=0):
    import zlib

    import numpy as np

    out = dict(_drawn_inputs(seed))
    spreads = {}
    factors = {'gla_w_lr': 3.4,
     'gla_b_lr': 8.0,
     'gla_norm': 4.491,
     'gdn_a_log': 6.163,
     'gdn_norm': 5.134,
     'pool_scale': 3.726,
     'fox_f_bias': 116.848,
     'ffn_conv_b': 8.0,
     'attn_norm_2': 7.218,
     'cmp_pos_k_2': 8.0,
     'sinks_2': 38.136,
     'ffn_norm_2': 41.7,
     'final_norm_2': 22.082,
     'cmp_pos_v_2': 8.0}
    for name, (base, spread) in spreads.items():
        noise = np.random.default_rng([zlib.crc32(name.encode()), seed]).standard_normal(out[name].shape)
        drawn = base * np.exp(spread * noise) if base else spread * noise
        out[name] = jnp.asarray(drawn.astype(out[name].dtype))
    for name, factor in factors.items():
        out[name] = (out[name] * factor).astype(out[name].dtype)
    return out
```

```python
from contextlib import ExitStack

import concourse.bass as bass
import numpy as np
from concourse import mybir

ALU = mybir.AluOpType
ACT = mybir.ActivationFunctionType
F32 = mybir.dt.float32
I32 = mybir.dt.int32
U32 = mybir.dt.uint32
X_AXIS = mybir.AxisListType.X

P = 128
T = 256
NT = T // P
D = 2048
KT = D // P
NB = 512
SLOTS = 4
KS = KT // SLOTS
HD = 128
DK = 64
CH = 64
FF = 5632
EPS = 1e-6
BIG = 1e30

GLA_Q, GLA_K, GLA_V, GLA_G, GLA_LR = 0, 256, 512, 1024, 1536
GDN_QKV, GDN_G, GDN_B, GDN_A = 1552, 3088, 3600, 3604
POOL_U, FOX_Q, FOX_K, FOX_V, FOX_F, W1 = 3608, 4120, 4632, 5144, 5656, 5660
QA, KC, VC, KSL, VSL, KW, VW, GATE, QB, KB, VB, W2 = 0, 1024, 1152, 1280, 1408, 1536, 1664, 1792, 1840, 2864, 2992, 3120
NCMP = 15
WINS = (2, 4, 8, 16)

BLK = {}
_b = 0
for _n, _c in (("mod", 24), ("in1", 12), ("out1", 4), ("up", 22), ("down", 11), ("in2", 7), ("out2", 4), ("wq", 4)):
    BLK[_n] = _b
    _b += _c
EVB = {"in1": 0, "out1": 12, "in2": 16, "out2": 23}

VEC = {
    "norm_mix": (0, 0, 16), "norm_ffn": (0, 16, 16), "attn_norm": (0, 32, 16), "ffn_norm2": (0, 48, 16),
    "gdn_conv": (0, 64, 48), "gla_b": (0, 112, 2), "gla_norm": (0, 114, 1), "gdn_norm": (0, 115, 1), "pool_scale": (0, 116, 4),
    "conv01": (1, 0, 88), "pos_k": (1, 88, 16), "pos_v": (1, 104, 16),
    "conv2": (2, 0, 44), "conv_b": (2, 44, 44), "b_mod1": (2, 88, 32),
    "b_mod2": (3, 0, 32),
}
VROWS = (120, 120, 120, 32)

LEVELS = (1, 2, 4, 8, 16, 32)


def tables():
    i = np.arange(P)
    same = (i[:, None] // CH) == (i[None, :] // CH)
    tri = i[:, None] <= i[None, :]
    cols = {}
    cols["ident"] = np.eye(P)
    cols["anti"] = np.eye(P)[::-1]
    cols["ones"] = np.ones((P, P))
    cols["tri"] = tri
    cols["tri_chunk"] = tri & same
    cols["strict_chunk"] = (i[:, None] < i[None, :]) & same
    cols["neg_tri"] = BIG * (i[None, :] > i[:, None])
    for n in LEVELS:
        cols[f"level{n}"] = (i[:, None] // (2 * n) == i[None, :] // (2 * n)) & (i[:, None] // n % 2 == 0) & (i[None, :] // n % 2 == 1)
    cols["level1_t"] = cols["level1"].T
    cols["gla_mask"] = (i[:, None] % CH) <= np.arange(CH)[None, :]
    pick = np.zeros((P, 192))
    pick[:CH, CH - 1] = 1
    pick[CH:, P - 1] = 1
    cols["pick"] = pick
    inv = np.array([[1.0 / min(t + 1, w) for t in range(16)] for w in WINS])
    cols["pool_inv"] = np.broadcast_to(inv.reshape(1, 64), (P, 64))
    reset = np.ones((P, T))
    reset[:, ::CH] = 0
    cols["scan_reset"] = reset
    dist = 255 - np.arange(384)
    f = np.float32
    large = 16 + (np.log(np.maximum(dist, 1).astype(f) / f(16)) / f(np.log(2048 / 16)) * f(16)).astype(np.int32)
    bucket = np.where(dist < 16, dist, np.minimum(large, 31))
    hot = np.zeros((P, 384))
    for m in range(256):
        hot[bucket[m], m] = 1
    cols["bucket"] = hot
    neg = np.zeros((P, 384))
    neg[:, dist < 0] = -BIG
    neg[16:32, dist >= 128] = -BIG
    cols["bias_neg"] = neg
    t = i[:, None] + P * np.arange(NT)[None, :]
    cols["cmp_valid"] = t >= 31
    cols["iota16"] = np.broadcast_to(np.arange(16.0), (P, 16))
    at, off = {}, 0
    for name, c in cols.items():
        at[name] = (off, c.shape[1])
        off += c.shape[1]
    return at, np.concatenate([np.asarray(c, np.float32) for c in cols.values()], axis=1)


TAB_AT, TAB = tables()

STEPS = {
    "fox_vec": (("fox_lf", 1), ("fox_cum_out", 1), ("fox_logit", 4), ("fox_max", 1), ("fox_p", 2)),
    "gla_vec": (("gla_z_out", 1), ("gla_b", 1), ("gla_kd", 1), ("gla_ke", 1)),
    "gla_act": (("gla_eb", 1), ("gla_ekd", 1)),
    "gdn_pe": (("qk_sum", 1), ("gdn_cum", 1), ("gdn_rows", 1), ("gdn_kk", 1), ("k_turned", 1), ("v_turned", 1), ("inv_turned", 1)),
    "gdn_act": (("gdn_beta", 1), ("gdn_alog", 1), ("conv0", 1), ("conv_silu", 1), ("qk_sq", 1), ("qk_root", 1), ("gdn_ecum", 1),
                ("gdn_erows", 1), ("gdn_dT", 1), ("gdn_fac", 1), ("k_scaled", 1), ("inv_out", 1)),
    "gdn_vec": (("gdn_g", 1), ("conv_sum", 1), ("qk_eps", 1), ("gdn_cum_out", 1), ("qk_norm", 2), ("gdn_rows_out", 1), ("kb_out", 2),
                ("gdn_diff", 1), ("gdn_bg", 1), ("attn_out", 1)),
}
STEP_OF = {name: (shared, sum(n for _, n in steps[:j])) for shared, steps in STEPS.items() for j, (name, _) in enumerate(steps)}


class Chain:

    def __init__(self, eng, at, own):
        self.eng, self.at, self.own, self.n, self.turn = eng, at, own, {}, None

    def __call__(self, ins, name=None, wait=True):
        name = name or self.own
        ins.then_inc(self.at(name, 0)[0], 1)
        self.n[name] = self.n.get(name, 0) + 1
        if wait:
            turn = self.turn * self.per[name] if self.turn is not None and self.per[name] != 1 else self.turn
            self.eng.wait_ge(*self.at(name, self.n[name] if self.turn is None else turn + self.n[name]))

    def begin(self, i, **per):
        self.per, self.turn, self.before = per, i, dict(self.n)

    def end(self, turns):
        for name, n in self.n.items():
            passed = n - self.before.get(name, 0)
            assert passed == self.per.get(name, 0), (name, passed)
            self.n[name] = n + (turns - 1) * passed
        self.turn = None


def build(nc, a, out, scratch, dbg):
    ctx = ExitStack()
    sb = lambda n, s, d=F32: ctx.enter_context(nc.sbuf_tensor(n, s, d))
    sems = {}

    def sem(name):
        name = STEP_OF[name][0] if name in STEP_OF else name
        if name not in sems:
            sems[name] = ctx.enter_context(nc.semaphore(name))
        return sems[name]

    def at(name, n):
        return sem(name), n + STEP_OF[name][1] if name in STEP_OF else n

    tab = sb("tab", [P, TAB.shape[1]])
    tb = lambda name, w=None: tab[:, TAB_AT[name][0]:TAB_AT[name][0] + (w or TAB_AT[name][1])]
    ident = tb("ident")
    ones = tb("ones")
    vrows = sb("vrows", [P, 4, P])
    vcols = sb("vcols", [P, 4, P])
    vc = lambda name, k=0, n=1: vcols[:, VEC[name][0], VEC[name][1] + k:VEC[name][1] + k + n]
    small = sb("small", [P, 4 + 4 + 4 + 16])
    x = sb("x", [P, NT, D])
    ring = sb("ring", [P, SLOTS, KS, NB])
    hT = sb("hT", [P, KT, T])
    yT = sb("yT", [P, KT, T])
    xs = yT[:].rearrange("p k t -> p (k t)").rearrange("p (t d) -> p t d", t=NT)
    gates = sb("gates", [P, 2, D])
    proj = sb("proj", [P, NT, W1])
    c_col = sb("c_col", [P, KT])
    c_wide = hT[:, 0:KT // 2, :].rearrange("p k t -> p (k t)").rearrange("p (k m) -> p k m", m=P)
    mod_raw = sb("mod_raw", [P, 64])
    mod_col = sb("mod_col", [P, 64])
    stat = sb("stat", [P, 32])
    arena = sb("arena", [P, 12800])
    ps = ctx.enter_context(nc.psum_tensor("ps", [P, 8, NB], F32))

    flat_proj = proj[:].rearrange("p t n -> p (t n)")

    def carve(base, sizes):
        views, off = {}, 0
        for name, shape in sizes.items():
            n = int(np.prod(shape))
            v = base[:, off:off + n]
            if len(shape) == 2:
                v = v.rearrange("p (a b) -> p a b", b=shape[1])
            elif len(shape) == 3:
                v = v.rearrange("p (a b c) -> p a b c", b=shape[1], c=shape[2])
            views[name] = v
            off += n
        assert off <= base.shape[1], (off, base.shape)
        return views

    fox = carve(arena[:], {
        "q": (4, T), "k": (4, T), "z": (1, 8), "e": (1, 8), "l": (1, 8), "cum": (1, 8), "decay": (4, 384), "logit": (4, 384),
        "max": (1, 8), "sum": (1, 8), "rec": (1, 8), "pT": (4, 384)})
    pool = carve(hT[:].rearrange("p k t -> p (k t)"), {"u": (4, T + 16), "w": (4, T + 16), "w2": (4, T + 16), "pw": (4, P), "w_lr": (1, T)})
    act_store = flat_proj[:, 0:44 * T].rearrange("p (k t) -> p k t", t=T)
    w1v = {n: a[n].rearrange("(k p) n -> p k n", p=P) for n in ("w_in", "w_out", "ffn_w_gate", "ffn_w_up", "w_in_2", "w_out_2", "peer_wq_2")}
    w_mod = a["w_mod"].rearrange("(p k) n -> p k n", k=KT)
    w_down = a["ffn_w_down"].rearrange("(k p) n -> p k n", p=P)
    w_lr = pool["w_lr"][0:16, 0, :]
    gla = carve(arena[:], {
        "q": (2, T), "k": (2, T), "gate": (4, T), "lr": (1, T), "z": (2, T), "e": (2, T), "b": (2, T), "pair": (2, 2048),
        "v": (4, 512), "att": (2, T), "qe": (2, T), "ke": (2, T), "ke_tok": (8, P), "state": (2, P)})
    TURNS = [(FOX_Q, P, 2, "act"), (FOX_Q + 256, P, 2, "act"), (FOX_K, P, 2, "vec"), (FOX_K + 256, P, 2, "vec"),
             (POOL_U, P, 2, "vec"), (POOL_U + 256, P, 2, "vec"),
             (GLA_Q, P, 2, "act"), (GLA_K, P, 2, "vec"), (GLA_G, P, 2, "act"), (GLA_G + 256, P, 2, "act"), (GLA_LR, 16, 1, "vec")]
    TURNS += [(GDN_QKV + 256 * j, P, 2, "vec") for j in range(6)] + [(GDN_G, P, 2, "act"), (GDN_G + 256, P, 2, "act")]
    FOX_T, POOL_T, GLA_T, GDN_T = 0, 4, 6, 11

    def turn_taken(g):
        who = TURNS[g][3]
        return sem("turn_" + who), sum(t[3] == who for t in TURNS[:g + 1])

    gdn = carve(arena[:], {
        "in": (12, 260), "conv": (12, T), "gate": (4, T), "sq": (8, T), "beta": (1, 8), "z": (1, 8), "e": (1, 8), "l": (1, 8), "u1": (1, 8),
        "g": (1, 8), "cum": (1, 8), "ecum": (1, 8), "fac": (2, 8), "decay": (1, 4), "state": (4, P), "new": (4, P), "u": (8, P)})
    gdn |= carve(flat_proj, {"rows": (8, P), "erows": (8, P), "dT": (8, P), "LT": (8, P), "off": (8, P), "inv": (8, P), "invT": (8, P),
                             "X": (8, P), "attnT": (8, P), "wT": (8, P), "kb": (4, T)})
    gdn |= carve(hT[:].rearrange("p k t -> p (k t)"), {"k_end": (2, 8, P), "k_w": (8, P), "v_b": (8, P)})
    ffn = carve(arena[:], {"y": (1, NB), "y2": (2, NB), "gate": (4, T), "act": (2, 4, T)})
    p2 = flat_proj[:, 0:NT * W2].rearrange("p (t n) -> p t n", t=NT)
    DOWN = FF // P // SLOTS
    BRANCHES = ("slc", "win", "cmp", "ban")
    UNITS = [(t, br) for t in range(NT) for br in BRANCHES]
    NU = len(UNITS)
    OUT_AT = {"a": UNITS.index((1, "cmp")) + 1, "b": NU}
    hyb = carve(arena[:], {"bias": (32, T), "v": (3, 4, 192), "p": (2, 2, T), "pT": (2, 4, P)})
    hyb |= carve(hT[:].rearrange("p k t -> p (k t)"), {"xk": (4, T), "kT": (6, T), "q": (2, 2, T), "hid": (2, 30), "kc": (2, 15)})
    hyb |= carve(flat_proj[:, NT * W2:], {"w1": (2, 16, P), "v_cmp": (2, 192), "q_in": (2, NT, P)})
    hst = carve(vrows[:].rearrange("p a b -> p (a b)"), {
        "w2": (2, P), "gate": (6, 16), "max": (NU, 2), "sum": (NU, 2), "sink": (NU, 2), "esink": (NU, 2), "hb": (1, 2)})
    kv_twice = yT[:].rearrange("p k t -> p (k t)")[:, 0:20 * P].rearrange("p (s m) -> p s m", m=P)
    TWICE = (KC, VC, KSL, KW, KB)
    rel = sb("rel", [32, 32])
    bias_rows = arena[0:32, 1024:1024 + 384]
    KCOL = (KSL, KW, KB)
    VCOL = (VSL, VW, VB)
    HEADS, TOP = 8, 16
    PICKS = HEADS * TOP
    SIDES = 2 * HEADS
    peer = carve(arena[:], {"q": (SIDES, T), "score": (2, SIDES, P), "sum": (2, SIDES // 2, 256)})
    peer |= carve(arena[:], {"hot": (PICKS, TOP)})
    peer |= carve(hT[:].rearrange("p k t -> p (k t)"), {
        "val": (2 * SIDES, TOP), "at_f": (2 * SIDES, TOP), "hi_f": (2, PICKS), "lo_f": (2, PICKS), "e1": (2, PICKS), "e2": (2, PICKS), "total": (1, 2 * HEADS)})
    spare = flat_proj[:, 4 * D:]
    peer |= carve(spare, {"best": (2 * HEADS, TOP), "h": (2, PICKS), "weight": (2, PICKS), "keys": (2, P), "keysT": (2, P), "h16": (1, 16),
                          "at_u": (2 * SIDES, TOP), "pick_u": (2 * HEADS, TOP), "expert": (2, PICKS), "now": (2, 8)})
    row_slots = [ring[:, s].rearrange("p k n -> p (k n)") for s in range(4)] + [flat_proj[:, D * s:D * (s + 1)] for s in range(4)]
    ROWS = len(row_slots)
    at_u, pick_u = peer["at_u"].bitcast(U32), peer["pick_u"].bitcast(U32)
    part_u = carve(hst["w2"].rearrange("p a b -> p (a b)"), {"x": (1, PICKS)})["x"][:, 0, :].bitcast(U32)
    expert = peer["expert"].bitcast(I32)
    expert_now = peer["now"].bitcast(I32)
    WQ_END = SLOTS * (BLK["wq"] + 4)
    block = ctx.enter_context(nc.Block())

    @block.sync
    def _(sp):
        def load(name, dst, src):
            sp.dma_start(dst, src).then_inc(sem(name), 16)

        load("x_in", x[:], a["x"].rearrange("(t p) d -> p t d", p=P))
        load("c_in", c_col[:], a["c"].rearrange("(p k) -> p k", k=KT))
        load("tab_in", tab[:], a["tab"])
        load("rel_in", rel[:], a["rel_bias_2"])

        def slot_load(view, u, s, first, cols, w, turn=0):
            if not first:
                sp.wait_ge(*at("unit_used", turn + (u + s - SLOTS + 1)))
            sp.dma_start(ring[:, s, :, 0:w], view[:, KS * s:KS * (s + 1), cols]).then_inc(sem(f"slot{s}"), 16)

        for s in range(SLOTS):
            slot_load(w_mod, 0, s, True, slice(0, NB), NB)
        for name, (tile, r0, n) in VEC.items():
            src = {"norm_mix": "norm_mix", "norm_ffn": "norm_ffn", "attn_norm": "attn_norm_2", "ffn_norm2": "ffn_norm_2",
                   "gdn_conv": "gdn_conv", "gla_b": "gla_b_lr", "gla_norm": "gla_norm", "gdn_norm": "gdn_norm",
                   "pool_scale": "pool_scale", "conv01": "ffn_conv_w", "pos_k": "cmp_pos_k_2", "pos_v": "cmp_pos_v_2",
                   "conv2": "ffn_conv_w", "conv_b": "ffn_conv_b", "b_mod1": "b_mod", "b_mod2": "b_mod"}[name]
            skip = {"conv2": 88, "b_mod2": 48}.get(name, 0)
            load("rows_in", vrows[r0:r0 + n, tile, :], a[src].rearrange("(r c) -> r c", c=P)[skip:skip + n, :])
        for j, (src, n) in enumerate((("fox_f_bias", 4), ("gdn_dt_bias", 4), ("gdn_a_log", 4), ("sinks_2", 16))):
            load("small_in", small[:, 4 * j:4 * j + n], a[src].partition_broadcast(P))
        for g in range(2):
            load("gate_bias_in", gates[:, g, :], a["b_mod"][(2 + 3 * g) * D:(3 + 3 * g) * D].partition_broadcast(P))
        sp.wait_ge(*at("bias_rows", 1))
        sp.dma_start(scratch, bias_rows).then_inc(sem("bias_saved"), 16)
        with sp.Fori(1, 24) as i:
            for s in range(SLOTS):
                slot_load(w_mod, 0, s, False, bass.ds(i * NB, NB), NB, i * SLOTS)

        def stream(view, blk, n, tail):
            with sp.Fori(0, n) as i:
                for s in range(SLOTS):
                    slot_load(view, blk * SLOTS, s, False, bass.ds(i * NB, NB), NB, i * SLOTS)
            if tail:
                for s in range(SLOTS):
                    slot_load(view, (blk + n) * SLOTS, s, False, slice(n * NB, n * NB + tail), tail)

        stream(w1v["w_in"], BLK["in1"], 11, W1 - 11 * NB)
        sp.wait_ge(*at("unit_used", SLOTS * BLK["out1"]))
        load("w_lr_in", w_lr, a["gla_w_lr"])
        load("pool_w_in", pool["pw"], a["pool_w"].rearrange("g c d -> c g d"))
        sp.wait_ge(*at("fox_out", 4))
        for half in range(2):
            for c in range(4):
                load("gla_v_in", gla["v"][CH * half:CH * (half + 1), c, :],
                     proj[CH * (c % 2):CH * (c % 2 + 1), c // 2, GLA_V:GLA_V + 512])
        stream(w1v["w_out"], BLK["out1"], 4, 0)
        sp.wait_ge(*at("x_done", 1))
        load("norm_in", gates[:, 0, :], a["norm_final"].partition_broadcast(P))
        with sp.Fori(0, 11) as i:
            for m, name in enumerate(("ffn_w_gate", "ffn_w_up")):
                for s in range(SLOTS):
                    slot_load(w1v[name], (BLK["up"] + m) * SLOTS, s, False, bass.ds(i * NB, NB), NB, i * (2 * SLOTS))
        wd = a["ffn_w_down"].rearrange("(j s p) n -> p j s n", s=SLOTS, p=P)
        with sp.Fori(0, DOWN) as i:
            for s in range(SLOTS):
                sp.wait_ge(*at("unit_used", i * SLOTS + (BLK["down"] * SLOTS + s - SLOTS + 1)))
                sp.dma_start(ring[:, s, :, :], wd[:, bass.ds(i, 1), s, :].rearrange("p o (k n) -> p (o k) n", n=NB)).then_inc(sem(f"slot{s}"), 16)
        sp.wait_ge(*at("x_done", 2))
        load("norm_in", gates[:, 1, :], a["final_norm_2"].partition_broadcast(P))
        stream(w1v["w_in_2"], BLK["in2"], 6, W2 - 6 * NB)
        sp.wait_ge(*at("x_done", 3))
        load("norm_in", gates[:, 0, :], a["ffn_norm_2"].partition_broadcast(P))
        for m, name in enumerate(("cmp_w1_k_2", "cmp_w1_v_2")):
            load("cmp_w_in", hyb["w1"][:, m], a[name].rearrange("(j p) n -> p j n", p=P))
        for m, name in enumerate(("cmp_w2_k_2", "cmp_w2_v_2")):
            for c in range(2):
                load("cmp_w_in", hst["w2"][:, m, DK * c:DK * (c + 1)], a[name])
        sp.wait_ge(*at("bias_saved", 16))
        load("bias_in", hyb["bias"], bass.AP(scratch.tensor, 0, [[1, P], [384, 32], [1, T]]))
        stream(w1v["w_out_2"], BLK["out2"], 4, 0)
        stream(w1v["peer_wq_2"], BLK["wq"], 4, 0)
        for t in range(NT):
            sp.wait_ge(*at("out_row", t + 1))
            sp.dma_start(out[0, P * t:P * (t + 1), :], x[:, t]).then_inc(sem("out_saved"), 16)
        sp.wait_ge(*at("out_saved", 32))

    @block.gpsimd
    def _(pool_eng):
        pool_eng.wait_ge(*at("cond", 1))
        pool_eng.tensor_copy(c_wide, c_col[:].unsqueeze(2).to_broadcast([P, KT, P])).then_inc(sem("c_wide"), 1)
        plink = Chain(pool_eng, at, "pool_chain")
        pool_eng.wait_ge(*at("unit_used", SLOTS * BLK["out1"]))
        pu, pw, pw2 = pool["u"], pool["w"], pool["w2"]
        N = T + 16
        for buf in (pu, pw, pw2):
            ins = pool_eng.memset(buf[:, :, 0:16], 0.0)
            plink(ins, "pool_zero")
        g0, n0 = turn_taken(POOL_T + 1)
        pool_eng.wait_ge(g0, n0)
        plink(pool_eng.tensor_tensor(pw[:, :, 1:N], pu[:, :, 1:N], pu[:, :, 0:N - 1], ALU.add))
        plink(pool_eng.tensor_tensor(pw2[:, 1:4, 2:N], pw[:, 1:4, 2:N], pw[:, 1:4, 0:N - 2], ALU.add))
        plink(pool_eng.tensor_tensor(pw[:, 2:4, 4:N], pw2[:, 2:4, 4:N], pw2[:, 2:4, 0:N - 4], ALU.add))
        plink(pool_eng.tensor_tensor(pw2[:, 3:4, 8:N], pw[:, 3:4, 8:N], pw[:, 3:4, 0:N - 8], ALU.add))
        inv = tb("pool_inv").rearrange("p (g n) -> p g n", n=16)
        for g, win in enumerate(WINS):
            src = (pw, pw2)[g % 2]
            plink(pool_eng.tensor_tensor(src[:, g, 16:32], src[:, g, 16:32], inv[:, g, :], ALU.mult))
            plink(pool_eng.tensor_scalar(src[:, g, 32:N], src[:, g, 32:N], 1.0 / win, None, ALU.mult))
            plink(pool_eng.tensor_tensor(src[:, g, 16:N], src[:, g, 16:N], pu[:, g, 16:N], ALU.subtract), "pool_delta")
        for n in range(16):
            g, sblk = n // 8, n % 8
            t0 = 8 * sblk
            d = gla["pair"][:, n % 2, 0:32 * (CH - t0)].rearrange("p (c s t) -> p c s t", c=4, s=8)
            pool_eng.wait_ge(*at("pair_diff", n + 1))
            plink(pool_eng.tensor_scalar(d, d, 0.0, None, ALU.min), "pair_min", wait=False)
            pool_eng.wait_ge(*at("pair_k", n + 1))
            qv = gla["q"][:, g, :].rearrange("p (c t) -> p c t", c=4)[:, :, t0:CH].unsqueeze(2).to_broadcast([P, 4, 8, CH - t0])
            plink(pool_eng.tensor_tensor(d, d, qv, ALU.mult), "pair_q", wait=False)
        for phase, table in enumerate((a["peer_u_2"], a["peer_v_2"])):
            for t in range(NT):
                pool_eng.wait_ge(*at("experts", t + 1))
                base = PICKS * (NT * phase + t)
                with pool_eng.Fori(0, PICKS // (2 * ROWS)) as i:
                    for half in range(2):
                        pool_eng.wait_ge(*at("row_used", i * (2 * ROWS) + (base + ROWS * half + 1)))
                        pool_eng.tensor_copy(expert_now[:, half, :], expert[:, t, bass.ds(i * (2 * ROWS) + ROWS * half, ROWS)]).then_inc(sem("experts_now"), 1)
                        for s in range(ROWS):
                            if s == 0:
                                pool_eng.wait_ge(*at("experts_now", i * 2 + (base // ROWS + half + 1)))
                            pool_eng.wait_ge(*at("row_used", i * (2 * ROWS) + (base + ROWS * half + s + 1)))
                            pool_eng.sem_inc(sem("row_free"), 1)
                            pool_eng.indirect_dma_start(row_slots[s], None, table, bass.IndirectOffsetOnAxis(expert_now[:, half, s:s + 1], 0))\
                                    .then_inc(sem(f"row{s}"), 16)

    @block.scalar
    def _(act):
        link = Chain(act, at, "act_chain")
        act.wait_ge(*at("c_in", 16))
        act.activation(c_col[:], c_col[:], ACT.Silu).then_inc(sem("cond"), 1)
        act.wait_ge(*at("vec_T", 1))
        turned = ps[:, 7, :].rearrange("p (a b) -> p a b", b=P)
        act.copy(vcols[:, 0:3, 0:120], turned[:, 0:3, 0:120]).then_inc(sem("vcols"), 1)
        act.copy(vcols[:, 3, 0:32], turned[:, 3, 0:32]).then_inc(sem("vcols"), 1)

        def norm(n, scaled=True):
            for t in range(NT):
                act.activation(xs[:, t], x[:, t], ACT.Square, accum_out=stat[:, t:t + 1]).then_inc(sem("squares"), 1)
            act.wait_ge(*at("mean_sq", n + 1))
            act.activation(stat[:, 4:6], stat[:, 2:4], ACT.Sqrt).then_inc(sem("root"), 1)
            if not scaled:
                return
            act.wait_ge(*at("squares", 2 * n + 2))
            act.wait_ge(*at("rstd", n + 1))
            act.activation(xs[:, 1], x[:, 1], ACT.Copy, scale=stat[:, 7:8]).then_inc(sem("xs_act"), 1)

        def norm_cols(n, scale, shift):
            for g in range(0, 8, 2):
                act.wait_ge(*at("hT_turned", n * 8 + g + 1))
                for k in range(2):
                    f = 2 * g + k
                    ins = act.activation(hT[:, f, :], ps[:, g % 4, T * k:T * (k + 1)], ACT.Identity, scale=scale[:, f:f + 1],
                                         bias=shift[:, f:f + 1] if shift is not None else 0.0)
                ins.then_inc(sem("hT_act"), 1)

        def evac(blk, n, dst, tail):
            with act.Fori(0, n) as i:
                act.wait_ge(*at("unit_used", i * SLOTS + SLOTS * (blk + 1)))
                act.copy(dst[:, 0, bass.ds(i * NB, NB)], ps[:, 0, :]).then_inc(sem("evac_act"), 1)
            if tail:
                act.wait_ge(*at("unit_used", SLOTS * (blk + n + 1)))
                act.copy(dst[:, 0, n * NB:n * NB + tail], ps[:, 0, 0:tail]).then_inc(sem("evac_act"), 1)

        act.wait_ge(*at("x_in", 16))
        norm(0)
        act.wait_ge(*at("mod_cols", 1))
        norm_cols(0, mod_col[:, 16:32], mod_col[:, 0:16])
        evac(BLK["in1"], 11, proj, W1 - 11 * NB)
        def taken(g):
            act.wait_ge(*at("turned", g + 1))
            return ps[:, g % 4, :]

        act_turn = lambda ins: ins.then_inc(sem("turn_act"), 1)

        def log1p_exp(n, e, out):
            act.wait_ge(*at("abs_z", n + 1))
            link(act.activation(e, e, ACT.Exp, scale=-1.0), "exp_z")
            link(act.activation(out, e, ACT.Ln, bias=1.0), "ln_z")

        for j in range(2):
            act_turn(act.activation(fox["q"][:, 2 * j:2 * j + 2, :], taken(FOX_T + j).rearrange("p (h t) -> p h t", h=2), ACT.Copy, scale=HD ** -0.5))
        log1p_exp(0, fox["e"], fox["l"])
        act.wait_ge(*at("fox_max", 1))
        fm, fs = fox["max"][:, 0, :], fox["sum"][:, 0, :]
        for h in range(4):
            for t in range(NT):
                part = fox["logit"][:, h, (0, P)[t]:(P, 3 * P)[t]]
                act.activation(part, part, ACT.Exp, bias=fm[:, 4 * t + h:4 * t + h + 1], accum_out=fs[:, 4 * t + h:4 * t + h + 1])\
                   .then_inc(sem("fox_exp"), 1)
        for h in range(4):
            act.wait_ge(*at("fox_pT", h + 1))
            act.copy(fox["pT"][:, h, :], ps[:, 5 + h % 2, 0:384]).then_inc(sem("fox_pT_out"), 1)
        for g in range(4):
            act.wait_ge(*at("pool_y", 1))
            act.activation(yT[:, 8 + g, :], ps[:, 5 + g // 2, T * (g % 2):T * (g % 2 + 1)], ACT.Copy, scale=vc("pool_scale", g))\
               .then_inc(sem("pool_out"), 1)
        act.wait_ge(*at("fox_out", 4))
        act.wait_ge(*at("fox_pT_out", 4))
        act_turn(act.activation(gla["q"], taken(GLA_T).rearrange("p (h t) -> p h t", h=2), ACT.Copy, scale=DK ** -0.5))
        for j in range(2):
            act_turn(act.activation(gla["gate"][:, 2 * j:2 * j + 2, :], taken(GLA_T + 2 + j).rearrange("p (h t) -> p h t", h=2), ACT.Silu))
        log1p_exp(1, gla["e"], gla["e"])
        act.wait_ge(*at("gla_b", 1))
        act.activation(gla["z"], gla["b"], ACT.Exp).then_inc(sem("gla_eb"), 1)
        act.wait_ge(*at("gla_kd", 1))
        act.activation(gla["e"], gla["e"], ACT.Exp).then_inc(sem("gla_ekd"), 1)
        for b in range(2):
            act.wait_ge(*at("ke_turned", b + 1))
            act.copy(gla["ke_tok"][0:CH, 4 * b:4 * b + 4, :], ps[0:CH, 5 + b, :].rearrange("p (n d) -> p n d", d=P)).then_inc(sem("ke_tok"), 1)
        for n in range(16):
            d = gla["pair"][:, n % 2, 0:32 * (CH - 8 * (n % 8))]
            act.wait_ge(*at("pair_min", n + 1))
            act.activation(d, d, ACT.Exp).then_inc(sem("pair_exp"), 1)

        def head_norm(m, sq):
            act.wait_ge(*at("mix_o", m + 1))
            for j in range(2):
                act.activation(sq[:, NB * j:NB * (j + 1)], ps[:, 6 + j, :], ACT.Square).then_inc(sem("o_sq"), 1)
            act.wait_ge(*at("o_mean", m + 1))
            act.activation(sq, sq, ACT.Sqrt).then_inc(sem("o_root"), 1)

        head_norm(0, gla["pair"].rearrange("p a b -> p (a b)")[:, 0:1024])
        act.wait_ge(*at("mix_out", 2))
        gsm = lambda name: gdn[name][:, 0, :]
        by_tile = lambda v: v.rearrange("p (t h) -> p t h", t=NT)
        act.activation(by_tile(gsm("beta")), proj[:, :, GDN_B:GDN_B + 4], ACT.Sigmoid).then_inc(sem("gdn_beta"), 1)
        for j in range(2):
            act_turn(act.activation(gdn["gate"][:, 2 * j:2 * j + 2, :], taken(GDN_T + 6 + j).rearrange("p (h t) -> p h t", h=2), ACT.Silu))
        link(act.activation(gdn["decay"][:, 0, :], small[:, 8:12], ACT.Exp), "gdn_alog")
        log1p_exp(2, gdn["e"], gdn["l"])
        g0, n0 = turn_taken(GDN_T + 5)
        act.wait_ge(g0, n0)
        for i in range(12):
            ins = act.activation(gdn["conv"][:, i, :], gdn["in"][:, i, 1:T + 1], ACT.Copy, scale=vc("gdn_conv", i))
        link(ins, "conv0")
        act.wait_ge(*at("conv_sum", 1))
        link(act.activation(gdn["conv"], gdn["conv"], ACT.Silu), "conv_silu")
        act.activation(gdn["sq"], gdn["conv"][:, 0:8, :], ACT.Square).then_inc(sem("qk_sq"), 1)
        act.wait_ge(*at("qk_eps", 1))
        act.activation(gdn["sq"], gdn["sq"], ACT.Sqrt).then_inc(sem("qk_root"), 1)
        act.wait_ge(*at("gdn_cum_out", 1))
        act.activation(gdn["ecum"], gdn["cum"], ACT.Exp).then_inc(sem("gdn_ecum"), 1)
        act.wait_ge(*at("gdn_rows_out", 1))
        act.activation(gdn["erows"], gdn["rows"], ACT.Exp).then_inc(sem("gdn_erows"), 1)
        act.wait_ge(*at("gdn_diff", 1))
        act.activation(gdn["dT"], gdn["dT"], ACT.Exp).then_inc(sem("gdn_dT"), 1)
        for c2 in range(2):
            r = slice(CH * c2, CH * (c2 + 1))
            ins = act.activation(gdn["fac"][r, c2, :], gdn["fac"][r, c2, :], ACT.Exp)
        link(ins, "gdn_fac")
        act.wait_ge(*at("k_turned", 1))
        act.wait_ge(*at("gdn_bg", 1))
        for n in range(8):
            src = ps[:, n // 4, P * (n % 4):P * (n % 4 + 1)]
            for c2 in range(2):
                act.activation(gdn["k_end"][:, c2, n, :], src, ACT.Copy, scale=gdn["fac"][:, c2, n:n + 1])
            ins = act.activation(gdn["k_w"][:, n, :], src, ACT.Copy, scale=gsm("u1")[:, n:n + 1])
        ins.then_inc(sem("k_scaled"), 1)
        flat = lambda name: gdn[name].rearrange("p n c -> p (n c)")
        act.wait_ge(*at("inv_turned", 1))
        act.copy(flat("inv")[:, 0:NB], ps[:, 4, :])
        act.copy(flat("inv")[:, NB:2 * NB], ps[:, 5, :]).then_inc(sem("inv_out"), 1)
        for lv in range(1, len(LEVELS)):
            act.wait_ge(*at("inv_x", lv))
            act.copy(flat("X")[:, 0:NB], ps[:, 4, :])
            act.copy(flat("X")[:, NB:2 * NB], ps[:, 5, :]).then_inc(sem("inv_x_out"), 1)
        act.wait_ge(*at("gdn_w", 1))
        act.copy(flat("wT")[:, 0:NB], ps[:, 6, :])
        act.copy(flat("wT")[:, NB:2 * NB], ps[:, 7, :]).then_inc(sem("gdn_w_out"), 1)
        head_norm(1, gdn["sq"].rearrange("p a b -> p (a b)")[:, 0:1024])
        def residual_evac(blk, ev):
            for i in range(4):
                act.wait_ge(*at("unit_used", SLOTS * (blk + i + 1)))
                if i or ev > 12:
                    act.wait_ge(*at("added", ev // 23 * 4 + i))
                act.copy(ffn["y"][:, 0, :], ps[:, 0, :]).then_inc(sem("evac_act"), 1)

        act.wait_ge(*at("mix_out", 4))
        residual_evac(BLK["out1"], EVB["out1"])
        act.wait_ge(*at("x_done", 1))
        norm(1)
        norm_cols(1, mod_col[:, 48:64], mod_col[:, 32:48])
        act.wait_ge(*at("ffn_credit", 1))
        with act.Fori(0, 11) as i:
            act.wait_ge(*at("unit_used", i * 8 + SLOTS * (BLK["up"] + 1)))
            act.wait_ge(*at("up_free", i + 1))
            for f in range(4):
                act.activation(ffn["gate"][:, f, :], ps[:, f, 0:T], ACT.Identity, scale=vcols[:, 2, bass.ds(i * 4 + f, 1)],
                               bias=vcols[:, 2, bass.ds(i * 4 + (44 + f), 1)]).then_inc(sem("conv_tap2"), 1)
            act.wait_ge(*at("gate_free", i + 2))
            act.activation(ffn["gate"], ffn["gate"], ACT.Silu).then_inc(sem("gate_silu"), 1)
        act.wait_ge(*at("up_free", 12))
        for j in range(2):
            act.copy(ffn["act"][:, j], act_store[:, 4 * j:4 * j + 4, :]).then_inc(sem("staged"), 1)
        with act.Fori(2, DOWN - 1, 2) as i:
            for par in range(2):
                act.wait_ge(*at("unit_used", i * SLOTS + SLOTS * (BLK["down"] - 1 + par)))
                act.copy(ffn["act"][:, par], act_store[:, bass.ds(i * 4 + 4 * par, 4), :]).then_inc(sem("staged"), 1)
        act.wait_ge(*at("unit_used", SLOTS * (BLK["down"] + DOWN - 2)))
        act.copy(ffn["act"][:, 0], act_store[:, 4 * (DOWN - 1):4 * DOWN, :]).then_inc(sem("staged"), 1)
        act.wait_ge(*at("x_done", 2))
        norm(2, scaled=False)
        act.wait_ge(*at("x_done", 3))
        norm(3)
        norm_cols(2, vc("attn_norm", 0, 16), None)
        evac(BLK["in2"], 6, p2, W2 - 6 * NB)
        act.wait_ge(*at("evac_vec", EVB["out2"] + 1))
        act.wait_ge(*at("evac_act", EVB["out2"] + 1))
        for t in range(NT):
            act.activation(hst["gate"][:, 3 * t:3 * t + 3, :], p2[:, t, GATE:GATE + 48].rearrange("p (h b) -> p b h", b=3), ACT.Sigmoid)\
               .then_inc(sem("gate_sig"), 1)
        for m in range(2):
            act.wait_ge(*at("cmp_hid", m + 1))
            act.wait_ge(*at("cmp_hb", m + 1))
            act.activation(hyb["hid"][:, m, :], ps[:, 2 + m, 0:30], ACT.Gelu_apprx_tanh, bias=hst["hb"][:, 0, m:m + 1]).then_inc(sem("cmp_gelu"), 1)

        def softmax_exp(i, g, u):
            t, br = UNITS[u]
            n = {"cmp": (7, 15)[t]}.get(br, P * (t + 1))
            act.wait_ge(*at("att_max", i * NU + (4 * NU * g + u + 1)))
            act.wait_ge(*at("att_turned", i * NU + (4 * NU * g + max(u - 1, 0) + 1)))
            if br == "ban":
                act.activation(hst["esink"][:, u, :], hst["sink"][:, u, :], ACT.Exp)
            for h in range(2):
                ins = act.activation(hyb["p"][:, u % 2, h, 0:n], ps[:, 1 + u % 3, T * h:T * h + n], ACT.Exp, bias=hst["max"][:, u, h:h + 1],
                                     accum_out=hst["sum"][:, u, h:h + 1])
            ins.then_inc(sem("att_exp"), 1)

        def turned_out(i, g, u):
            t, br = UNITS[u]
            act.wait_ge(*at("att_turned", i * NU + (4 * NU * g + u + 2)))
            act.wait_ge(*at("att_pv", i * NU + (4 * NU * g + max(u - 1, 0) + 1)))
            r, n = {"cmp": ((7, 15)[t], 2)}.get(br, (P, 2 * (t + 1)))
            act.copy(hyb["pT"][0:r, u % 2, 0:n, :], ps[0:r, 4 + u % 2, 0:P * n].rearrange("p (a b) -> p a b", b=P)).then_inc(sem("att_pT"), 1)

        act.wait_ge(*at("q_zero", 1))
        for g in range(2):
            with act.Fori(0, 4) as i:
                act.wait_ge(*at("q_turned", i + (4 * g + 1)))
                for h in range(2):
                    r = slice(DK * h, DK * (h + 1))
                    ins = act.activation(hyb["q"][r, :, h, :], ps[r, 0, :].rearrange("p (k t) -> p k t", k=2), ACT.Copy, scale=DK ** -0.5)
                ins.then_inc(sem("q_out"), 1)
                softmax_exp(i, g, 0)
                for u in range(NU):
                    if u + 1 < NU:
                        softmax_exp(i, g, u + 1)
                    turned_out(i, g, u)
        residual_evac(BLK["out2"], EVB["out2"])
        act.wait_ge(*at("x_done", 4))
        act.dma_start(peer["keys"], a["peer_subkeys_2"].rearrange("s n d -> n s d")).then_inc(sem("keys_in"), 16)
        norm(4)
        norm_cols(3, vc("ffn_norm2", 0, 16), None)
        with act.Fori(0, 4) as i:
            act.wait_ge(*at("unit_used", i * SLOTS + SLOTS * (BLK["wq"] + 1)))
            act.copy(peer["q"][:, bass.ds(i * 4, 4), :], ps[:, 0:4, 0:T]).then_inc(sem("wq_out"), 1)
        for t in range(NT):
            for b in range(4):
                act.wait_ge(*at("keys_scored", t * 4 + b + 1))
                act.copy(peer["score"][:, t, 4 * b:4 * b + 4, :], ps[:, (4 - 4 * t) + b, :].rearrange("p (a b) -> p a b", b=P)).then_inc(sem("score_out"), 1)
        for t in range(NT):
            act.wait_ge(*at("best_shift", t + 1))
            best = peer["best"][:, HEADS * t:HEADS * (t + 1), :]
            act.activation(best, best, ACT.Exp).then_inc(sem("best_exp"), 1)
        for t in range(NT):
            act.wait_ge(*at("h_done", t + 1))
            act.activation(peer["h"][:, t, :], peer["h"][:, t, :], ACT.Gelu_apprx_tanh).then_inc(sem("h_gelu"), 1)
        act.wait_ge(*at("x_done", 5))
        norm(5, scaled=False)

    @block.tensor
    def _(pe):
        pe.wait_ge(*at("tab_in", 16))
        pe.wait_ge(*at("rows_in", 16 * len(VEC)))
        for j, n in enumerate(VROWS):
            ins = pe.transpose(ps[:, 7, P * j:P * j + n], vrows[0:n, j, :], ident[0:n, 0:n])
        ins.then_inc(sem("vec_T"), 1)

        pe.wait_ge(*at("rel_in", 16))
        pe.matmul(ps[0:32, 6, 0:384], rel[:], tb("bucket")[0:32, :], start=True, stop=True).then_inc(sem("bias_rows_ps"), 1)
        pe.wait_ge(*at("c_wide", 1))

        def mod_block(i, bank, extra):
            if extra is not None:
                pe.wait_ge(*at("mod_evac", i - 1))
            for s in range(SLOTS):
                pe.wait_ge(sem(f"slot{s}"), i * 16 + 16)
                for k in range(KS):
                    ins = pe.matmul(ps[:, bank, :], c_wide[:, KS * s + k, :], ring[:, s, k, :],
                                    start=(s == 0 and k == 0), stop=(s == SLOTS - 1 and k == KS - 1))
                ins.then_inc(sem("unit_used"), 1)

        mod_block(0, 0, None)
        mod_block(1, 1, None)
        with pe.Fori(1, 12) as i:
            mod_block(i * 2, 0, True)
            mod_block(i * 2 + 1, 1, True)

        def norm_turn(n):
            pe.wait_ge(*at("xs_vec", n + 1))
            pe.wait_ge(*at("xs_act", n + 1))
            for g in range(8):
                if g >= 4:
                    pe.wait_ge(sem("hT_vec" if g % 2 else "hT_act"), n * 4 + (g - 4) // 2 + 1)
                for k in range(2):
                    for t in range(NT):
                        f = 2 * g + k
                        ins = pe.transpose(ps[:, g % 4, (NT * k + t) * P:(NT * k + t + 1) * P], xs[:, t, P * f:P * (f + 1)], ident)
                ins.then_inc(sem("hT_turned"), 1)
            pe.wait_ge(*at("hT_act", n * 4 + 4))
            pe.wait_ge(*at("hT_vec", n * 4 + 4))

        def project(lhs, blk, ev, n, tail):
            def one(turn, b, e, w):
                pe.wait_ge(*at("evac_act", turn + (e + 1)))
                pe.wait_ge(*at("evac_vec", turn + (e + 1)))
                for s in range(SLOTS):
                    pe.wait_ge(sem(f"slot{s}"), turn * 16 + (b * 16 + 16))
                    for k in range(KS):
                        for t in range(NT):
                            ins = pe.matmul(ps[:, t, 0:w], lhs[:, KS * s + k, P * t:P * (t + 1)], ring[:, s, k, 0:w],
                                            start=(s == 0 and k == 0), stop=(s == SLOTS - 1 and k == KS - 1))
                    ins.then_inc(sem("unit_used"), 1)
            with pe.Fori(0, n) as i:
                one(i, blk, ev, NB)
            if tail:
                one(0, blk + n, ev + n, tail)

        pe.wait_ge(*at("mod_evac", 24))
        norm_turn(0)
        project(hT, BLK["in1"], EVB["in1"], 11, W1 - 11 * NB)
        def turn(g):
            col, w, tiles, _ = TURNS[g]
            if g >= 4:
                pe.wait_ge(*turn_taken(g - 4))
            for k in range(tiles):
                for t in range(NT):
                    ins = pe.transpose(ps[0:w, g % 4, (NT * k + t) * P:(NT * k + t + 1) * P],
                                       proj[:, t, col + w * k:col + w * (k + 1)], ident)
            ins.then_inc(sem("turned"), 1)

        pe.wait_ge(*at("evac_act", EVB["out1"] + 1))
        pe.wait_ge(*at("evac_vec", EVB["out1"] + 1))
        for g in range(FOX_T, GLA_T):
            turn(g)
        pe.wait_ge(*at("fox_lf", 1))
        lf = fox["z"][:, 0, :]
        pe.matmul(ps[:, 4, 0:8], tb("tri"), lf, start=True, stop=False, skip_group_check=True)
        pe.matmul(ps[:, 4, 4:8], ones, lf[:, 0:4], start=False, stop=True, skip_group_check=True).then_inc(sem("fox_cum"), 1)
        pe.wait_ge(*at("fox_cum_out", 1))
        for h in range(4):
            for t in range(NT):
                ins = pe.transpose(ps[:, 5 + h // 2, (NT * (h % 2) + t) * P:(NT * (h % 2) + t + 1) * P],
                                   fox["cum"][:, 0, 4 * t + h:4 * t + h + 1].to_broadcast([P, P]), ident)
        ins.then_inc(sem("fox_rows"), 1)
        for g in range(FOX_T, POOL_T):
            pe.wait_ge(*turn_taken(g))
        for h in range(4):
            bank = (4, 7)[h % 2]
            if h >= 2:
                pe.wait_ge(*at("fox_logit", h - 1))
            pe.matmul(ps[:, bank, 0:P], fox["q"][:, h, 0:P], fox["k"][:, h, 0:P], start=True, stop=True)
            pe.matmul(ps[:, bank, P:3 * P], fox["q"][:, h, P:T], fox["k"][:, h, :], start=True, stop=True).then_inc(sem("fox_score"), 1)

        def fox_values(h):
            bank = (4, 7)[h % 2]
            pe.wait_ge(*at("fox_pT_out", h + 1))
            if h >= 2:
                pe.wait_ge(*at("fox_out", h - 1))
            v = [proj[:, t, FOX_V + P * h:FOX_V + P * (h + 1)] for t in range(NT)]
            pT = fox["pT"][:, h, :]
            pe.matmul(ps[:, bank, 0:P], v[0], pT[:, 0:P], start=True, stop=True)
            pe.matmul(ps[:, bank, P:T], v[0], pT[:, P:2 * P], start=True, stop=False)
            pe.matmul(ps[:, bank, P:T], v[1], pT[:, 2 * P:3 * P], start=False, stop=True).then_inc(sem("fox_o"), 1)

        pe.wait_ge(*at("fox_p", 2))
        for h in range(4):
            if h >= 2:
                pe.wait_ge(*at("fox_pT_out", h - 1))
            for j in range(3):
                ins = pe.transpose(ps[:, 5 + h % 2, P * j:P * (j + 1)], fox["logit"][:, h, P * j:P * (j + 1)], ident)
            ins.then_inc(sem("fox_pT"), 1)
            if h >= 1:
                fox_values(h - 1)
        fox_values(3)
        pe.wait_ge(*at("pool_delta", 4))
        pe.wait_ge(*at("pool_w_in", 16))
        pe.wait_ge(*at("fox_pT_out", 4))
        for g in range(4):
            src = (pool["w"], pool["w2"])[g % 2]
            ins = pe.matmul(ps[:, 5 + g // 2, T * (g % 2):T * (g % 2 + 1)], pool["pw"][:, g, :], src[:, g, 16:T + 16], start=True, stop=True)
        ins.then_inc(sem("pool_y"), 1)
        for g in range(GLA_T, GDN_T):
            turn(g)
        pe.wait_ge(*turn_taken(GLA_T + 4))
        pe.wait_ge(*at("w_lr_in", 16))
        pe.wait_ge(*at("fox_out", 4))
        for g in range(2):
            ins = pe.matmul(ps[:, 4, T * g:T * (g + 1)], w_lr[:, P * g:P * (g + 1)], gla["lr"][0:16, 0, :], start=True, stop=True)
        ins.then_inc(sem("gla_z"), 1)
        pe.wait_ge(*at("gla_ke", 1))
        pe.wait_ge(*at("pool_out", 4))
        for c in range(4):
            for g in range(2):
                ins = pe.transpose(ps[0:CH, 5 + c // 2, P * (2 * (c % 2) + g):P * (2 * (c % 2) + g + 1)], gla["ke"][:, g, CH * c:CH * (c + 1)], ident)
            if c % 2:
                ins.then_inc(sem("ke_turned"), 1)
        pe.wait_ge(*at("gla_z_out", 1))
        pe.wait_ge(*at("ke_tok", 2))
        for n in range(16):
            g, sblk = n // 8, n % 8
            t0 = 8 * sblk
            d = gla["pair"][:, n % 2, 0:32 * (CH - t0)].rearrange("p (c s t) -> p c s t", c=4, s=8)
            dst = ps[:, 4 + g, 0:T].rearrange("p (c t) -> p c t", c=4)[:, :, t0:CH]
            pe.wait_ge(*at("pair_q", n + 1))
            for s in range(8):
                key = 8 * sblk + s
                ins = pe.matmul(dst, tb("pick")[:, CH - 1 - key:CH - 1 - key + P], d[:, :, s, :],
                                start=(key == 0), stop=(key == CH - 1), skip_group_check=True)
            ins.then_inc(sem("pair_used"), 1)
        pe.wait_ge(*at("gla_att", 2))
        pe.wait_ge(*at("gla_v_in", 16 * 8))
        pe.wait_ge(*at("fox_out", 4))
        for c in range(4):
            for h in range(4):
                g, r = h // 2, slice(CH * (h % 2), CH * (h % 2) + CH)
                dst = ps[:, 6 + h % 2, T * g + CH * c:T * g + CH * (c + 1)]
                ins = pe.matmul(dst, gla["v"][r, c, P * h:P * (h + 1)], gla["att"][r, g, CH * c:CH * (c + 1)],
                                start=True, stop=(c == 0), skip_group_check=True)
                if c > 0:
                    if h == 0:
                        pe.wait_ge(*at("gla_state", c))
                    ins = pe.matmul(dst, gla["state"][r, g, :], gla["qe"][r, g, CH * c:CH * (c + 1)],
                                    start=False, stop=True, skip_group_check=True)
            if c < 3:
                for g in range(2):
                    ins2 = pe.matmul(ps[:, 4, T * g:T * (g + 1)], gla["ke_tok"][0:CH, 2 * c + g, :], gla["v"][0:CH, c, T * g:T * (g + 1)],
                                     start=True, stop=True)
                ins2.then_inc(sem("gla_dstate"), 1)
        ins.then_inc(sem("mix_o"), 1)

        def head_norm(m, sq):
            pe.wait_ge(*at("o_sq", 2 * m + 2))
            for j in range(2):
                ins = pe.matmul(ps[:, 4 + j, :], ones, sq[:, NB * j:NB * (j + 1)], start=True, stop=True)
            ins.then_inc(sem("o_sum"), 1)

        head_norm(0, gla["pair"].rearrange("p a b -> p (a b)")[:, 0:1024])
        for g in range(GDN_T, len(TURNS)):
            turn(g)
        gsm = lambda name: gdn[name][:, 0, :]
        tok = lambda n: slice(P * (n // 4), P * (n // 4 + 1))
        pe.wait_ge(*at("qk_sq", 1))
        pe.wait_ge(*at("mix_out", 2))
        for j in range(4):
            ins = pe.matmul(ps[:, 4 + j, :], ones, gdn["sq"][:, 2 * j:2 * j + 2, :], start=True, stop=True)
        ins.then_inc(sem("qk_sum"), 1)
        pe.wait_ge(*at("gdn_g", 1))
        for g in (len(TURNS) - 4, len(TURNS) - 3, len(TURNS) - 2, len(TURNS) - 1):
            pe.wait_ge(*turn_taken(g))
        pe.matmul(ps[:, 0, 0:8], tb("tri_chunk"), gsm("g"), start=True, stop=True).then_inc(sem("gdn_cum"), 1)
        pe.wait_ge(*at("gdn_cum_out", 1))
        pe.wait_ge(*at("gdn_beta", 1))
        pe.wait_ge(*at("qk_eps", 1))
        for i, name in enumerate(("cum", "beta")):
            for n in range(8):
                ins = pe.transpose(ps[:, 2 + 2 * i + n // 4, P * (n % 4):P * (n % 4 + 1)], gsm(name)[:, n:n + 1].to_broadcast([P, P]), ident)
        ins.then_inc(sem("gdn_rows"), 1)
        pe.wait_ge(*at("kb_out", 2))
        pe.wait_ge(*at("qk_norm", 2))
        pe.wait_ge(*at("gdn_rows_out", 1))
        for n in range(8):
            h, t = n % 4, tok(n)
            pe.matmul(ps[:, 4 + n // 4, P * h:P * (h + 1)], gdn["conv"][:, 4 + h, t], gdn["kb"][:, h, t], start=True, stop=True)
            ins = pe.matmul(ps[:, 6 + n // 4, P * h:P * (h + 1)], gdn["conv"][:, 4 + h, t], gdn["conv"][:, h, t], start=True, stop=True)
        ins.then_inc(sem("gdn_kk"), 1)
        for n in range(8):
            ins = pe.transpose(ps[:, n // 4, P * (n % 4):P * (n % 4 + 1)], gdn["conv"][:, 4 + n % 4, tok(n)], ident)
        ins.then_inc(sem("k_turned"), 1)
        for n in range(8):
            ins = pe.transpose(ps[:, 2 + n // 4, P * (n % 4):P * (n % 4 + 1)], gdn["conv"][:, 8 + n % 4, tok(n)], ident)
        ins.then_inc(sem("v_turned"), 1)
        pe.wait_ge(*at("invT_out", 1))
        for n in range(8):
            ins = pe.transpose(ps[:, 4 + n // 4, P * (n % 4):P * (n % 4 + 1)], gdn["invT"][:, n, :], ident)
        ins.then_inc(sem("inv_turned"), 1)
        for lv in range(1, len(LEVELS)):
            last = lv == len(LEVELS) - 1
            pe.wait_ge(*at("inv_off", lv))
            if lv == 1:
                pe.wait_ge(*at("inv_out", 1))
                pe.wait_ge(*at("k_scaled", 1))
                pe.wait_ge(*at("v_scaled", 1))
                pe.wait_ge(*at("attn_out", 1))
            else:
                pe.wait_ge(*at("inv_new", lv - 1))
                pe.wait_ge(*at("invT_out", lv))
            for n in range(8):
                ins = pe.matmul(ps[:, 4 + n // 4, P * (n % 4):P * (n % 4 + 1)], gdn["off"][:, n, :], gdn["inv"][:, n, :], start=True, stop=True)
            ins.then_inc(sem("inv_x"), 1)
            pe.wait_ge(*at("inv_x_out", lv))
            for n in range(8):
                ins = pe.matmul(ps[:, n // 4, P * (n % 4):P * (n % 4 + 1)], gdn["X"][:, n, :], gdn["invT"][:, n, :], start=True, stop=True)
            ins.then_inc(sem("invT_delta"), 1)
            if not last:
                for n in range(8):
                    ins = pe.matmul(ps[:, 6 + n // 4, P * (n % 4):P * (n % 4 + 1)], gdn["invT"][:, n, :], gdn["X"][:, n, :], start=True, stop=True)
                ins.then_inc(sem("inv_delta"), 1)
        pe.wait_ge(*at("invT_out", len(LEVELS)))
        for n in range(8):
            dst = slice(P * (n % 4), P * (n % 4 + 1))
            pe.matmul(ps[:, 4 + n // 4, dst], gdn["invT"][:, n, :], gdn["v_b"][:, n, :], start=True, stop=True)
            ins = pe.matmul(ps[:, 6 + n // 4, dst], gdn["k_w"][:, n, :], gdn["invT"][:, n, :], start=True, stop=True)
        ins.then_inc(sem("gdn_w"), 1)
        pe.wait_ge(*at("gdn_u_out", 1))
        pe.wait_ge(*at("gdn_w_out", 1))
        pe.wait_ge(*at("q_decayed", 2))
        for c in range(4):
            t, c2 = c // 2, c % 2
            if c > 0:
                pe.wait_ge(*at("gdn_state", c))
                for h in range(4):
                    ins = pe.matmul(ps[:, 4, P * h:P * (h + 1)], gdn["wT"][:, 4 * t + h, :], gdn["state"][:, h, :], start=True, stop=True)
                ins.then_inc(sem("gdn_ws"), 1)
                pe.wait_ge(*at("gdn_new", c))
            new = gdn["u"] if c == 0 else gdn["new"]
            if c < 3:
                for h in range(4):
                    ins = pe.matmul(ps[:, 5, P * h:P * (h + 1)], gdn["k_end"][:, c2, 4 * t + h, :], new[:, h, :], start=True, stop=True)
                ins.then_inc(sem("gdn_dstate"), 1)
            for h in range(4):
                dst = ps[:, 6 + h % 2, T * (h // 2) + CH * c:T * (h // 2) + CH * (c + 1)]
                ins = pe.matmul(dst, new[:, h, :], gdn["attnT"][:, 4 * t + h, CH * c2:CH * (c2 + 1)], start=True, stop=(c == 0), skip_group_check=True)
                if c > 0:
                    ins = pe.matmul(dst, gdn["state"][:, h, :], gdn["conv"][:, h, CH * c:CH * (c + 1)], start=False, stop=True, skip_group_check=True)
            if c < 3:
                ins.then_inc(sem("gdn_o"), 1)
        ins.then_inc(sem("mix_o"), 1)
        head_norm(1, gdn["sq"].rearrange("p a b -> p (a b)")[:, 0:1024])
        pe.wait_ge(*at("mix_out", 4))
        project(yT, BLK["out1"], EVB["out1"], 4, 0)
        norm_turn(1)
        pe.wait_ge(*at("ffn_credit", 1))
        with pe.Fori(0, 11) as i:
            for m, free in enumerate(("gate_free", "up_free")):
                pe.wait_ge(sem(free), i + 1)
                for s in range(SLOTS):
                    pe.wait_ge(sem(f"slot{s}"), i * 32 + 16 * (BLK["up"] + m + 1))
                    for k in range(KS):
                        for f in range(4):
                            ins = pe.matmul(ps[:, 4 * m + f, 0:T], ring[:, s, k, P * f:P * (f + 1)], hT[:, KS * s + k, :],
                                            start=(s == 0 and k == 0), stop=(s == SLOTS - 1 and k == KS - 1))
                    ins.then_inc(sem("unit_used"), 1)
        pe.wait_ge(*at("gate_free", 12))
        pe.wait_ge(*at("up_free", 12))

        def down_group(i, j, par, start, stop):
            pe.wait_ge(*at("staged", i + (j + 1)))
            for s in range(SLOTS):
                pe.wait_ge(sem(f"slot{s}"), i * 16 + 16 * (BLK["down"] + j + 1))
                for t in range(NT):
                    for n in range(4):
                        ins = pe.matmul(ps[:, 2 * n + t, :], ffn["act"][:, par, s, P * t:P * (t + 1)], ring[:, s, n, :],
                                        start=(start and s == 0), stop=(stop and s == SLOTS - 1))
                ins.then_inc(sem("unit_used"), 1)

        down_group(0, 0, 0, True, False)
        with pe.Fori(1, DOWN - 2, 2) as i:
            down_group(i, 0, 1, False, False)
            down_group(i, 1, 0, False, False)
        down_group(0, DOWN - 2, 1, False, False)
        down_group(0, DOWN - 1, 0, False, True)
        pe.wait_ge(*at("x_done", 2))
        norm_turn(2)
        project(hT, BLK["in2"], EVB["in2"], 6, W2 - 6 * NB)
        pe.wait_ge(*at("evac_act", EVB["out2"] + 1))
        pe.wait_ge(*at("evac_vec", EVB["out2"] + 1))

        pe.wait_ge(*at("kv_twice", 1))
        for i, bank in enumerate((0, 1, 4, 5, 6)):
            for g in range(2):
                for t in range(NT):
                    ins = pe.transpose(ps[:, bank, T * g + P * t:T * g + P * (t + 1)], kv_twice[:, 4 * i + 2 * t + g, :], ident)
            ins.then_inc(sem("kv_turned"), 1)
        pe.wait_ge(*at("cmp_w_in", 16 * 6))
        for m in range(2):
            pe.wait_ge(*at("xk", 2 * m + 2))
            for j in range(16):
                pe.matmul(ps[:, 2 + m, 0:30], hyb["w1"][:, m, j, :], hyb["xk"][:, 2 * m:2 * m + 2, 2 * j:2 * j + 225:16], start=(j == 0), stop=(j == 15))
            for j in range(16):
                ins = pe.matmul(ps[:, 7, m:m + 1], hyb["w1"][:, m, j, :], vc(("pos_k", "pos_v")[m], j), start=(j == 0), stop=(j == 15), skip_group_check=True)
            ins.then_inc(sem("cmp_hid"), 1)
            pe.wait_ge(*at("cmp_hb", m + 1))
        pe.wait_ge(*at("cmp_gelu", 2))
        pe.matmul(ps[:, 0, 0:30], hst["w2"][:, 0, :], hyb["hid"][:, 0, :], start=True, stop=True)
        for g in range(2):
            ins = pe.matmul(ps[0:NCMP, 1, DK * g:DK * (g + 1)], hyb["hid"][:, 1, NCMP * g:NCMP * (g + 1)], hst["w2"][:, 1, 0:DK], start=True, stop=True)
        ins.then_inc(sem("cmp_kv"), 1)
        pe.wait_ge(*at("kv_out", 1))
        pe.wait_ge(*at("bias_in", 16))

        def score(i, g, u):
            t, br = UNITS[u]
            pe.wait_ge(*at("att_exp", i * NU + (4 * NU * g + max(u - 2, 0) + 1)))
            if u == 0:
                pe.wait_ge(*at("q_out", i + (4 * g + 1)))
            off = P * (1 - t)
            for h in range(2):
                head = bass.ds(i * 2 + (8 * g + h + (16 if br == "ban" else 0)), 1)
                if br == "cmp":
                    n = (7, 15)[t]
                    keys, cols = hyb["kc"][:, g, 0:n], slice(off + 31, T, 16)
                else:
                    n = P * (t + 1)
                    keys, cols = hyb["kT"][:, 2 * ("slc", "win", "ban").index(br) + g, 0:n], slice(off, off + n)
                dst = ps[:, 1 + u % 3, T * h:T * h + n]
                pe.matmul(dst, hyb["q"][:, int(br == "ban"), h, P * t:P * (t + 1)], keys, start=True, stop=False)
                ins = pe.matmul(dst, tb("anti"), hyb["bias"][:, head, cols], start=False, stop=True)
            ins.then_inc(sem("att_score"), 1)

        def turn_p(i, g, u):
            t, br = UNITS[u]
            pe.wait_ge(*at("att_p", i * NU + (4 * NU * g + u + 1)))
            pe.wait_ge(*at("att_pT", i * NU + (4 * NU * g + max(u - 1, 0) + 1)))
            for h in range(2):
                for k in range(1 if br == "cmp" else t + 1):
                    n = (7, 15)[t] if br == "cmp" else P
                    q = h if br == "cmp" else (t + 1) * h + k
                    ins = pe.transpose(ps[0:n, 4 + u % 2, P * q:P * (q + 1)], hyb["p"][:, u % 2, h, P * k:P * k + n], ident)
            ins.then_inc(sem("att_turned"), 1)

        def values(i, g, u):
            t, br = UNITS[u]
            pe.wait_ge(*at("att_pT", i * NU + (4 * NU * g + u + 2)))
            if u == 0:
                pe.wait_ge(*at("att_out", i * 2 + (8 * g + 1)))
            dst = ps[:, 7 if br == "ban" else 6, P * t:P * (t + 1)]
            for h in range(2):
                cols = slice(DK * (1 - h), DK * (1 - h) + P)
                for k in range(1 if br == "cmp" else t + 1):
                    first = br in ("slc", "ban") and h == 0 and k == 0
                    if br == "cmp":
                        n = (7, 15)[t]
                        v, w = hyb["v_cmp"][0:n, g, cols], hyb["pT"][0:n, u % 2, h, :]
                    else:
                        v, w = hyb["v"][:, ("slc", "win", "ban").index(br), 2 * k + g, cols], hyb["pT"][:, u % 2, (t + 1) * h + k, :]
                    ins = pe.matmul(dst, v, w, start=first, stop=(br in ("cmp", "ban") and h == 1 and (br == "cmp" or k == t)))
            ins.then_inc(sem("att_pv"), 1)

        for g in range(2):
            with pe.Fori(0, 4) as i:
                pe.wait_ge(*at("q_in", i + (4 * g + 1)))
                for k in range(2):
                    for t in range(NT):
                        ins = pe.transpose(ps[:, 0, T * k + P * t:T * k + P * (t + 1)], hyb["q_in"][:, k, t, :], ident)
                ins.then_inc(sem("q_turned"), 1)
                score(i, g, 0)
                score(i, g, 1)
                for u in range(NU):
                    turn_p(i, g, u)
                    if u + 2 < NU:
                        score(i, g, u + 2)
                    if u:
                        values(i, g, u - 1)
                values(i, g, NU - 1)
        pe.wait_ge(*at("att_out", 17))
        project(yT, BLK["out2"], EVB["out2"], 4, 0)
        pe.wait_ge(*at("x_done", 4))
        norm_turn(3)
        pe.wait_ge(*at("keys_in", 16))
        for s in range(2):
            ins = pe.transpose(ps[:, 4, P * s:P * (s + 1)], peer["keys"][:, s, :], ident)
        ins.then_inc(sem("keys_turned"), 1)
        with pe.Fori(0, 4) as i:
            pe.wait_ge(*at("wq_out", i + 1))
            for s in range(SLOTS):
                pe.wait_ge(sem(f"slot{s}"), i * 16 + 16 * (BLK["wq"] + 1))
                for k in range(KS):
                    for f in range(4):
                        ins = pe.matmul(ps[:, f, 0:T], ring[:, s, k, P * f:P * (f + 1)], hT[:, KS * s + k, :],
                                        start=(s == 0 and k == 0), stop=(s == SLOTS - 1 and k == KS - 1))
                ins.then_inc(sem("unit_used"), 1)
        pe.wait_ge(*at("wq_out", 5))
        pe.wait_ge(*at("keys_out", 1))
        for t in range(NT):
            for c in range(SIDES):
                ins = pe.matmul(ps[:, 4 - 4 * t + c // 4, P * (c % 4):P * (c % 4 + 1)], peer["q"][:, c, P * t:P * (t + 1)], peer["keysT"][:, c % 2, :],
                                start=True, stop=True)
                if c % 4 == 3:
                    ins.then_inc(sem("keys_scored"), 1)

    @block.vector
    def _(vec):
        link = Chain(vec, at, "vec_chain")
        vec.memset(stat[:, 14:15], 0.0).then_inc(sem("evac_vec"), 1)
        vec.memset(stat[:, 15:16], 0.0).then_inc(sem("evac_act"), 1)

        def norm(n, scaled=True):
            vec.wait_ge(*at("squares", 2 * n + 2))
            vec.tensor_scalar(stat[:, 2:4], stat[:, 0:2], 1.0 / D, EPS, ALU.mult, ALU.add).then_inc(sem("mean_sq"), 1)
            vec.wait_ge(*at("root", n + 1))
            vec.reciprocal(stat[:, 6:8], stat[:, 4:6]).then_inc(sem("rstd"), 1)
            vec.wait_ge(*at("rstd", n + 1))
            if scaled:
                vec.tensor_scalar(xs[:, 0], x[:, 0], stat[:, 6:7], None, ALU.mult).then_inc(sem("xs_vec"), 1)

        def norm_cols(n, scale, shift):
            for g in range(1, 8, 2):
                vec.wait_ge(*at("hT_turned", n * 8 + g + 1))
                for k in range(2):
                    f = 2 * g + k
                    bank = ps[:, g % 4, T * k:T * (k + 1)]
                    if shift is not None:
                        ins = vec.tensor_scalar(hT[:, f, :], bank, scale[:, f:f + 1], shift[:, f:f + 1], ALU.mult, ALU.add)
                    else:
                        ins = vec.tensor_scalar(hT[:, f, :], bank, scale[:, f:f + 1], None, ALU.mult)
                ins.then_inc(sem("hT_vec"), 1)

        def evac(blk, n, dst, tail):
            with vec.Fori(0, n) as i:
                vec.wait_ge(*at("unit_used", i * SLOTS + SLOTS * (blk + 1)))
                vec.tensor_copy(dst[:, 1, bass.ds(i * NB, NB)], ps[:, 1, :]).then_inc(sem("evac_vec"), 1)
            if tail:
                vec.wait_ge(*at("unit_used", SLOTS * (blk + n + 1)))
                vec.tensor_copy(dst[:, 1, n * NB:n * NB + tail], ps[:, 1, 0:tail]).then_inc(sem("evac_vec"), 1)

        vec.wait_ge(*at("bias_rows_ps", 1))
        link(vec.tensor_tensor(bias_rows, ps[0:32, 6, 0:384], tb("bias_neg")[0:32, :], ALU.add), "bias_rows")
        norm(0)
        diag = arena[:, 0:NB].rearrange("p (a b) -> p a b", b=P)
        vec.wait_ge(*at("gate_bias_in", 32))
        for half in range(2):
            with vec.Fori(0, 4) as i:
                link.begin(i, vec_chain=2, mod_evac=2)
                for par in range(2):
                    vec.wait_ge(*at("unit_used", i * 8 + (half * 48 + 4 * par + 4)))
                    link(vec.tensor_tensor(diag, ps[:, par, :].rearrange("p (a b) -> p a b", b=P),
                                           ident.unsqueeze(1).to_broadcast([P, 4, P]), ALU.mult))
                    link(vec.tensor_reduce(mod_raw[:, bass.ds(i * 8 + (half * 32 + 4 * par), 4)], diag, X_AXIS, ALU.add),
                         "mod_evac")
            link.end(4)
            with vec.Fori(0, 2) as i:
                link.begin(i, mod_evac=2)
                for par in range(2):
                    vec.wait_ge(*at("unit_used", i * 8 + (half * 48 + 32 + 4 * par + 4)))
                    g = gates[:, half, bass.ds(i * 1024 + par * NB, NB)]
                    link(vec.tensor_tensor(g, ps[:, par, :], g, ALU.add), "mod_evac", wait=False)
            link.end(2)
        vec.wait_ge(*at("vcols", 2))
        vec.wait_ge(*at("mod_evac", 24))
        link(vec.tensor_tensor(mod_col[:, 0:32], mod_raw[:, 0:32], vc("b_mod1", 0, 32), ALU.add))
        link(vec.tensor_tensor(mod_col[:, 32:64], mod_raw[:, 32:64], vc("b_mod2", 0, 32), ALU.add))
        for o, nm in ((16, "norm_mix"), (48, "norm_ffn")):
            ins = vec.scalar_tensor_tensor(out=mod_col[:, o:o + 16], in0=mod_col[:, o:o + 16], scalar=1.0, in1=vc(nm, 0, 16),
                                           op0=ALU.add, op1=ALU.mult)
            ins.then_inc(sem("mod_cols"), 1) if o == 48 else link(ins)
        vec.wait_ge(*at("mod_cols", 1))
        norm_cols(0, mod_col[:, 16:32], mod_col[:, 0:16])
        evac(BLK["in1"], 11, proj, W1 - 11 * NB)
        vec.wait_ge(*at("small_in", 64))
        vec.wait_ge(*at("evac_act", EVB["out1"] + 1))
        vec.wait_ge(*at("evac_vec", EVB["out1"] + 1))

        def taken(g):
            vec.wait_ge(*at("turned", g + 1))
            return ps[:, g % 4, :]

        vec_turn = lambda ins, wait=False: link(ins, "turn_vec", wait)
        z2 = fox["z"][:, 0, :].rearrange("p (t h) -> p t h", t=NT)
        link(vec.tensor_tensor(z2, proj[:, :, FOX_F:FOX_F + 4], small[:, 0:4].unsqueeze(1).to_broadcast([P, NT, 4]), ALU.add))
        link(vec.scalar_tensor_tensor(out=fox["e"], in0=fox["z"], scalar=-1.0, in1=fox["z"], op0=ALU.mult, op1=ALU.max), "abs_z")
        for j in range(2):
            vec_turn(vec.tensor_copy(fox["k"][:, 2 * j:2 * j + 2, :], taken(FOX_T + 2 + j).rearrange("p (h t) -> p h t", h=2)))
        vec.wait_ge(*at("pool_zero", 3))
        for j in range(2):
            vec_turn(vec.tensor_copy(pool["u"][:, 2 * j:2 * j + 2, 16:T + 16], taken(POOL_T + j).rearrange("p (h t) -> p h t", h=2)))
        vec.wait_ge(*at("ln_z", 1))
        link(vec.scalar_tensor_tensor(out=fox["z"], in0=fox["z"], scalar=0.0, in1=fox["l"], op0=ALU.min, op1=ALU.subtract), "fox_lf")
        vec.wait_ge(*at("fox_cum", 1))
        link(vec.tensor_copy(fox["cum"][:, 0, :], ps[:, 4, 0:8]), "fox_cum_out")
        vec.wait_ge(*at("fox_rows", 1))
        neg2 = tb("neg_tri").unsqueeze(1).to_broadcast([P, 2, P])
        for b in range(2):
            rows = ps[:, 5 + b, :].rearrange("p (h t k) -> p h t k", h=2, t=2)
            hh = slice(2 * b, 2 * b + 2)
            vec.tensor_tensor(fox["decay"][:, hh, 0:P], rows[:, :, 0, :], neg2, ALU.add)
            vec.tensor_copy(fox["decay"][:, hh, P:2 * P], rows[:, :, 0, :])
            link(vec.tensor_tensor(fox["decay"][:, hh, 2 * P:3 * P], rows[:, :, 1, :], neg2, ALU.add))
        for h in range(4):
            bank = (4, 7)[h % 2]
            vec.wait_ge(*at("fox_score", h + 1))
            for t in range(NT):
                r = slice((0, P)[t], (P, 3 * P)[t])
                ins = vec.scalar_tensor_tensor(out=fox["logit"][:, h, r], in0=ps[:, bank, r], scalar=fox["cum"][:, 0, 4 * t + h:4 * t + h + 1],
                                               in1=fox["decay"][:, h, r], op0=ALU.add, op1=ALU.subtract)
            link(ins, "fox_logit")
        fm = fox["max"][:, 0, :]
        vec.tensor_reduce(fm[:, 0:4], fox["logit"][:, :, 0:P], X_AXIS, ALU.max)
        link(vec.tensor_reduce(fm[:, 4:8], fox["logit"][:, :, P:3 * P], X_AXIS, ALU.max))
        link(vec.tensor_scalar(fm, fm, -1.0, None, ALU.mult), "fox_max")
        vec.wait_ge(*at("fox_exp", 8))
        link(vec.reciprocal(fox["rec"], fox["sum"]))
        for t in range(NT):
            r = slice((0, P)[t], (P, 3 * P)[t])
            rec = fox["rec"][:, 0, 4 * t:4 * t + 4].unsqueeze(2).to_broadcast([P, 4, P * (t + 1)])
            link(vec.tensor_tensor(fox["logit"][:, :, r], fox["logit"][:, :, r], rec, ALU.mult), "fox_p")
        for h in range(4):
            vec.wait_ge(*at("fox_o", h + 1))
            link(vec.tensor_copy(yT[:, 12 + h, :], ps[:, (4, 7)[h % 2], 0:T]), "fox_out")
        gv = lambda name: gla[name].rearrange("p a b -> p (a b)")
        vec.wait_ge(*at("fox_pT_out", 4))
        vec_turn(vec.tensor_copy(gla["k"], taken(GLA_T + 1).rearrange("p (h t) -> p h t", h=2)))
        vec_turn(vec.tensor_copy(gla["lr"][0:16, 0, :], taken(GLA_T + 4)[0:16, 0:T]), True)
        vec.wait_ge(*at("gla_z", 1))
        for g in range(2):
            ins = vec.tensor_scalar(gla["z"][:, g, :], ps[:, 4, T * g:T * (g + 1)], vc("gla_b", g), None, ALU.add)
        link(ins, "gla_z_out")
        link(vec.scalar_tensor_tensor(out=gla["e"], in0=gla["z"], scalar=-1.0, in1=gla["z"], op0=ALU.mult, op1=ALU.max), "abs_z")
        vec.wait_ge(*at("ln_z", 2))
        link(vec.scalar_tensor_tensor(out=gla["z"], in0=gla["z"], scalar=0.0, in1=gla["e"], op0=ALU.min, op1=ALU.subtract))
        for g in range(2):
            ins = vec.tensor_tensor_scan(gla["b"][:, g, :], tb("scan_reset"), gla["z"][:, g, :], 0.0, ALU.mult, ALU.add)
        link(ins)
        link(vec.tensor_scalar(gla["b"], gla["b"], 1.0 / 16.0, None, ALU.mult), "gla_b")
        bc = gv("b").rearrange("p (n t) -> p n t", t=CH)
        link(vec.tensor_tensor(gv("e").rearrange("p (n t) -> p n t", t=CH), bc[:, :, CH - 1:CH].to_broadcast([P, 8, CH]), bc, ALU.subtract), "gla_kd")
        vec.wait_ge(*at("gla_eb", 1))
        vec.wait_ge(turn_taken(GLA_T)[0], turn_taken(GLA_T)[1])
        link(vec.tensor_tensor(gla["qe"], gla["q"], gla["z"], ALU.mult))
        vec.wait_ge(*at("gla_ekd", 1))
        link(vec.tensor_tensor(gla["ke"], gla["k"], gla["e"], ALU.mult), "gla_ke")

        def pair(n):
            g, t0 = n // 8, 8 * (n % 8)
            d = gla["pair"][:, n % 2, 0:32 * (CH - t0)].rearrange("p (c s t) -> p c s t", c=4, s=8)
            chunks = lambda v: gla[v][:, g, :].rearrange("p (c t) -> p c t", c=4)
            shape = [P, 4, 8, CH - t0]
            return d, chunks("b")[:, :, t0:CH].unsqueeze(2).to_broadcast(shape), \
                chunks("b")[:, :, t0:t0 + 8].unsqueeze(3).to_broadcast(shape), chunks("k")[:, :, t0:t0 + 8].unsqueeze(3).to_broadcast(shape)

        def pair_diff(n):
            d, bt, bs, _ = pair(n)
            if n >= 2:
                vec.wait_ge(*at("pair_used", n - 1))
            vec.tensor_tensor(d, bt, bs, ALU.subtract).then_inc(sem("pair_diff"), 1)

        pair_diff(0)
        for n in range(16):
            if n < 15:
                pair_diff(n + 1)
            d, _, _, kb = pair(n)
            vec.wait_ge(*at("pair_exp", n + 1))
            vec.tensor_tensor(d, d, kb, ALU.mult).then_inc(sem("pair_k"), 1)
        mask = tb("gla_mask").unsqueeze(1).to_broadcast([P, 4, CH])
        vec.wait_ge(*at("pair_used", 16))
        for g in range(2):
            link(vec.tensor_tensor(gla["att"][:, g, :].rearrange("p (c t) -> p c t", c=4), ps[:, 4 + g, 0:T].rearrange("p (c t) -> p c t", c=4), mask, ALU.mult), "gla_att")
        for c in range(3):
            vec.wait_ge(*at("gla_dstate", c + 1))
            for h in range(4):
                g, r = h // 2, slice(CH * (h % 2), CH * (h % 2) + CH)
                st, ds = gla["state"][r, g, :], ps[r, 4, T * g + P * (h % 2):T * g + P * (h % 2 + 1)]
                if c == 0:
                    ins = vec.tensor_copy(st, ds)
                else:
                    last = CH * c + CH - 1
                    ins = vec.scalar_tensor_tensor(out=st, in0=st, scalar=gla["z"][r, g, last:last + 1], in1=ds, op0=ALU.mult, op1=ALU.add)
            link(ins, "gla_state")

        def head_norm(m, sq, gate, norm, y0):
            vec.wait_ge(*at("o_sum", m + 1))
            for j in range(2):
                ins = vec.tensor_scalar(sq[:, NB * j:NB * (j + 1)], ps[:, 4 + j, :], 1.0 / HD, EPS, ALU.mult, ALU.add)
            link(ins, "o_mean")
            vec.wait_ge(*at("o_root", m + 1))
            link(vec.reciprocal(sq, sq))
            for j in range(2):
                y, two = yT[:, y0 + j:y0 + j + 3:2, :], lambda v: v.rearrange("p (h t) -> p h t", h=2)
                link(vec.scalar_tensor_tensor(out=y, in0=two(ps[:, 6 + j, :]), scalar=vc(norm), in1=two(sq[:, NB * j:NB * (j + 1)]), op0=ALU.mult, op1=ALU.mult))
                link(vec.tensor_tensor(y, y, gate[:, j:j + 3:2, :], ALU.mult), "mix_out")

        vec.wait_ge(turn_taken(GLA_T + 3)[0], turn_taken(GLA_T + 3)[1])
        head_norm(0, gla["pair"].rearrange("p a b -> p (a b)")[:, 0:1024], gla["gate"], "gla_norm", 0)
        gsm = lambda name: gdn[name][:, 0, :]
        flat = lambda name: gdn[name].rearrange("p n c -> p (n c)")
        by_tile = lambda v: v.rearrange("p (t h) -> p t h", t=NT)
        link(vec.memset(gdn["in"][:, :, 0:4], 0.0))
        link(vec.memset(gdn["fac"], 0.0))
        link(vec.tensor_tensor(by_tile(gsm("z")), proj[:, :, GDN_A:GDN_A + 4], small[:, 4:8].unsqueeze(1).to_broadcast([P, NT, 4]), ALU.add))
        link(vec.scalar_tensor_tensor(out=gdn["e"], in0=gdn["z"], scalar=-1.0, in1=gdn["z"], op0=ALU.mult, op1=ALU.max), "abs_z")
        for j in range(6):
            vec_turn(vec.tensor_copy(gdn["in"][:, 2 * j:2 * j + 2, 4:T + 4], taken(GDN_T + j).rearrange("p (h t) -> p h t", h=2)), j == 5)
        vec.wait_ge(*at("ln_z", 3))
        link(vec.tensor_scalar(gdn["u1"], gdn["e"], 1.0, None, ALU.add))
        link(vec.tensor_scalar(gdn["g"], gdn["u1"], -1.0, None, ALU.add))
        link(vec.tensor_tensor(gdn["g"], gdn["e"], gdn["g"], ALU.subtract))
        link(vec.reciprocal(gdn["u1"], gdn["u1"]))
        link(vec.tensor_tensor(gdn["g"], gdn["g"], gdn["u1"], ALU.mult))
        link(vec.tensor_tensor(gdn["g"], gdn["g"], gdn["l"], ALU.add))
        link(vec.scalar_tensor_tensor(out=gdn["z"], in0=gdn["z"], scalar=0.0, in1=gdn["g"], op0=ALU.max, op1=ALU.add))
        vec.wait_ge(*at("gdn_alog", 1))
        link(vec.scalar_tensor_tensor(out=by_tile(gsm("g")), in0=by_tile(gsm("z")), scalar=-1.0,
                                      in1=gdn["decay"].to_broadcast([P, NT, 4]), op0=ALU.mult, op1=ALU.mult), "gdn_g")
        vec.wait_ge(*at("conv0", 1))
        for j in range(1, 4):
            for i in range(12):
                ins = vec.scalar_tensor_tensor(out=gdn["conv"][:, i, :], in0=gdn["in"][:, i, 1 + j:T + 1 + j], scalar=vc("gdn_conv", 12 * j + i),
                                               in1=gdn["conv"][:, i, :], op0=ALU.mult, op1=ALU.add)
            link(ins, "conv_sum" if j == 3 else None)
        vec.wait_ge(*at("qk_sum", 1))
        for j in range(4):
            ins = vec.tensor_scalar(gdn["sq"][:, 2 * j:2 * j + 2, :], ps[:, 4 + j, :].rearrange("p (h t) -> p h t", h=2), EPS, None, ALU.add)
        link(ins, "qk_eps")
        vec.wait_ge(*at("gdn_cum", 1))
        link(vec.tensor_copy(gsm("cum"), ps[:, 0, 0:8]), "gdn_cum_out")
        vec.wait_ge(*at("qk_root", 1))
        link(vec.reciprocal(gdn["sq"], gdn["sq"]))
        q4, k4 = gdn["conv"][:, 0:4, :], gdn["conv"][:, 4:8, :]
        link(vec.scalar_tensor_tensor(out=q4, in0=q4, scalar=HD ** -0.5, in1=gdn["sq"][:, 0:4, :], op0=ALU.mult, op1=ALU.mult), "qk_norm")
        link(vec.tensor_tensor(k4, k4, gdn["sq"][:, 4:8, :], ALU.mult), "qk_norm")
        vec.wait_ge(*at("gdn_rows", 1))
        vec.wait_ge(*at("turn_act", turn_taken(len(TURNS) - 1)[1]))
        for j in range(2):
            ins = vec.tensor_copy(flat("rows")[:, NB * j:NB * (j + 1)], ps[:, 2 + j, :])
        link(ins, "gdn_rows_out")
        for t in range(2):
            link(vec.tensor_tensor(gdn["kb"][:, :, P * t:P * (t + 1)], gdn["conv"][:, 4:8, P * t:P * (t + 1)],
                                   ps[:, 4 + t, :].rearrange("p (h t) -> p h t", h=4), ALU.mult), "kb_out")
        for n in range(8):
            ins = vec.tensor_scalar(gdn["dT"][:, n, :], gdn["rows"][:, n, :], gsm("cum")[:, n:n + 1], 0.0, ALU.subtract, ALU.min)
        for c2 in range(2):
            r = slice(CH * c2, CH * (c2 + 1))
            ins = vec.tensor_tensor(gdn["fac"][r, c2, :], gdn["rows"][r, :, CH * c2 + CH - 1], gsm("cum")[r, :], ALU.subtract)
        link(ins, "gdn_diff")
        vec.wait_ge(*at("gdn_ecum", 1))
        link(vec.tensor_tensor(gdn["u1"], gdn["beta"], gdn["ecum"], ALU.mult), "gdn_bg")
        vec.wait_ge(*at("gdn_dT", 1))
        wide = lambda name: tb(name).unsqueeze(1).to_broadcast([P, 8, P])
        link(vec.tensor_tensor(gdn["dT"], gdn["dT"], wide("tri_chunk"), ALU.mult))
        vec.wait_ge(*at("gdn_kk", 1))
        for j in range(2):
            r = slice(NB * j, NB * (j + 1))
            vec.tensor_tensor(flat("attnT")[:, r], ps[:, 6 + j, :], flat("dT")[:, r], ALU.mult)
            ins = vec.tensor_tensor(flat("LT")[:, r], ps[:, 4 + j, :], flat("dT")[:, r], ALU.mult)
        link(ins, "attn_out")
        link(vec.tensor_tensor(gdn["LT"], gdn["LT"], wide("strict_chunk"), ALU.mult))
        link(vec.tensor_tensor(gdn["off"], gdn["LT"], wide("level1"), ALU.mult))
        link(vec.tensor_tensor(gdn["invT"], wide("ident"), gdn["off"], ALU.subtract), "invT_out")
        vec.wait_ge(*at("v_turned", 1))
        for n in range(8):
            ins = vec.tensor_scalar(gdn["v_b"][:, n, :], ps[:, 2 + n // 4, P * (n % 4):P * (n % 4 + 1)], gsm("beta")[:, n:n + 1], None, ALU.mult)
        link(ins, "v_scaled")
        vec.wait_ge(*at("gdn_erows", 1))
        for t in range(2):
            r = slice(P * t, P * (t + 1))
            link(vec.tensor_tensor(gdn["conv"][:, 0:4, r], gdn["conv"][:, 0:4, r], gdn["erows"][:, 4 * t:4 * t + 4, :], ALU.mult), "q_decayed")
        for lv in range(1, len(LEVELS)):
            link(vec.tensor_tensor(gdn["off"], gdn["LT"], wide(f"level{LEVELS[lv]}"), ALU.mult), "inv_off")
            if lv < len(LEVELS) - 1:
                vec.wait_ge(*at("inv_delta", lv))
            vec.wait_ge(*at("invT_delta", lv))
            for j in range(2):
                r = slice(NB * j, NB * (j + 1))
                ins = vec.tensor_tensor(flat("invT")[:, r], flat("invT")[:, r], ps[:, j, :], ALU.subtract)
            link(ins, "invT_out")
            if lv < len(LEVELS) - 1:
                for j in range(2):
                    r = slice(NB * j, NB * (j + 1))
                    ins = vec.tensor_tensor(flat("inv")[:, r], flat("inv")[:, r], ps[:, 6 + j, :], ALU.subtract)
                link(ins, "inv_new")
        vec.wait_ge(*at("gdn_w", 1))
        for j in range(2):
            ins = vec.tensor_copy(flat("u")[:, NB * j:NB * (j + 1)], ps[:, 4 + j, :])
        link(ins, "gdn_u_out")
        for c in range(4):
            t, c2 = c // 2, c % 2
            if c > 0:
                vec.wait_ge(*at("gdn_ws", c))
                link(vec.tensor_tensor(flat("new"), flat("u")[:, NB * t:NB * (t + 1)], ps[:, 4, :], ALU.subtract), "gdn_new")
            if c < 3:
                vec.wait_ge(*at("gdn_dstate", c + 1))
                vec.wait_ge(*at("gdn_o", c + 1))
                for h in range(4):
                    st, ds = gdn["state"][:, h, :], ps[:, 5, P * h:P * (h + 1)]
                    if c == 0:
                        ins = vec.tensor_copy(st, ds)
                    else:
                        last = CH * c2 + CH - 1
                        ins = vec.scalar_tensor_tensor(out=st, in0=st, scalar=gdn["erows"][:, 4 * t + h, last:last + 1], in1=ds, op0=ALU.mult, op1=ALU.add)
                link(ins, "gdn_state")
        head_norm(1, gdn["sq"].rearrange("p a b -> p (a b)")[:, 0:1024], gdn["gate"], "gdn_norm", 4)
        vec.memset(stat[:, 13:14], 0.0).then_inc(sem("gate_free"), 1)
        vec.memset(stat[:, 12:13], 0.0).then_inc(sem("up_free"), 1)
        vec.memset(stat[:, 11:12], 0.0).then_inc(sem("ffn_credit"), 1)

        def residual_add(blk, ev, gate):
            for i in range(4):
                r = slice(NB * i, NB * (i + 1))
                vec.wait_ge(*at("unit_used", SLOTS * (blk + i + 1)))
                if gate is not None:
                    link(vec.tensor_tensor(ffn["y2"][:, 1, :], ps[:, 1, :], gate[:, r], ALU.mult), "evac_vec")
                    link(vec.tensor_tensor(x[:, 1, r], x[:, 1, r], ffn["y2"][:, 1, :], ALU.add))
                else:
                    link(vec.tensor_tensor(x[:, 1, r], x[:, 1, r], ps[:, 1, :], ALU.add), "evac_vec")
                vec.wait_ge(*at("evac_act", ev + i + 2))
                y = ffn["y"][:, 0, :]
                if gate is not None:
                    y = ffn["y2"][:, 0, :]
                    link(vec.tensor_tensor(y, ffn["y"][:, 0, :], gate[:, r], ALU.mult))
                link(vec.tensor_tensor(x[:, 0, r], x[:, 0, r], y, ALU.add), "added")

        link.n["evac_vec"] = EVB["out1"] + 1
        residual_add(BLK["out1"], EVB["out1"], gates[:, 0, :])
        link(vec.memset(stat[:, 10:11], 0.0), "x_done")
        norm(1)
        norm_cols(1, mod_col[:, 48:64], mod_col[:, 32:48])
        with vec.Fori(0, 11) as i:
            link.begin(i, vec_chain=1, gate_free=1, up_free=1)
            vec.wait_ge(*at("conv_tap2", i * 4 + 4))
            for f in range(4):
                ins = vec.scalar_tensor_tensor(out=ffn["gate"][:, f, 1:T], in0=ps[:, f, 0:T - 1], scalar=vcols[:, 1, bass.ds(i * 4 + (44 + f), 1)],
                                               in1=ffn["gate"][:, f, 1:T], op0=ALU.mult, op1=ALU.add)
            link(ins)
            for f in range(4):
                ins = vec.scalar_tensor_tensor(out=ffn["gate"][:, f, 2:T], in0=ps[:, f, 0:T - 2], scalar=vcols[:, 1, bass.ds(i * 4 + f, 1)],
                                               in1=ffn["gate"][:, f, 2:T], op0=ALU.mult, op1=ALU.add)
            link(ins, "gate_free", wait=False)
            vec.wait_ge(*at("gate_silu", i + 1))
            vec.wait_ge(*at("unit_used", i * 8 + SLOTS * (BLK["up"] + 2)))
            link(vec.tensor_tensor(act_store[:, bass.ds(i * 4, 4), :], ffn["gate"], ps[:, 4:8, 0:T], ALU.mult), "up_free", wait=False)
        link.end(11)
        vec.wait_ge(*at("unit_used", SLOTS * (BLK["down"] + DOWN)))
        for n in range(4):
            r = slice(NB * n, NB * (n + 1))
            for t in range(NT):
                ins = vec.tensor_tensor(ffn["y2"][:, t, :], ps[:, 2 * n + t, :], gates[:, 1, r], ALU.mult)
            link(ins)
            link(vec.tensor_tensor(x[:, :, r], x[:, :, r], ffn["y2"], ALU.add), "x_done" if n == 3 else None)
        norm(2, scaled=False)
        vec.wait_ge(*at("norm_in", 16))
        for t in range(NT):
            ins = vec.scalar_tensor_tensor(out=x[:, t], in0=x[:, t], scalar=stat[:, 6 + t:7 + t], in1=gates[:, 0, :], op0=ALU.mult, op1=ALU.mult)
        link(ins, "x_done")
        norm(3)
        norm_cols(2, vc("attn_norm", 0, 16), None)
        evac(BLK["in2"], 6, p2, W2 - 6 * NB)
        for k, name in enumerate(("att_exp", "att_turned", "att_pT", "att_pv", "att_out")):
            vec.memset(stat[:, 17 + k:18 + k], 0.0).then_inc(sem(name), 1)
        link.n["att_out"] = 1
        vec.wait_ge(*at("evac_act", EVB["out2"] + 1))
        vec.wait_ge(*at("evac_vec", EVB["out2"] + 1))
        for i, col in enumerate(TWICE):
            for t in range(NT):
                src = p2[:, t, col:col + 2 * DK].rearrange("p (g d) -> p g d", g=2).unsqueeze(2).to_broadcast([P, 2, 2, DK])
                ins = vec.tensor_copy(kv_twice[:, 4 * i + 2 * t:4 * i + 2 * t + 2, :].rearrange("p g (c d) -> p g c d", c=2), src)
        link(ins, "kv_twice")
        vec.memset(hyb["v"], 0.0)
        vec.memset(hyb["v_cmp"], 0.0)
        link(vec.memset(hyb["q"], 0.0), "q_zero")
        for kind in range(3):
            for t in range(NT):
                ins = vec.tensor_copy(hyb["v"][:, kind, 2 * t:2 * t + 2, DK:2 * DK], p2[:, t, VCOL[kind]:VCOL[kind] + 2 * DK].rearrange("p (g d) -> p g d", g=2))
        link(ins)
        for m in range(2):
            vec.wait_ge(*at("kv_turned", m + 1))
            src = ps[:, m, :].rearrange("p (g t) -> p g t", g=2)
            link(vec.tensor_copy(hyb["xk"][0:DK, 2 * m:2 * m + 2, :], src[0:DK]), "xk")
            link(vec.tensor_copy(hyb["xk"][DK:P, 2 * m:2 * m + 2, 0:T - 1], src[DK:P, :, 1:T]), "xk")
        for kind in range(3):
            vec.wait_ge(*at("kv_turned", kind + 3))
            ins = vec.tensor_copy(hyb["kT"][:, 2 * kind:2 * kind + 2, :], ps[:, 4 + kind, :].rearrange("p (g t) -> p g t", g=2))
        for m in range(2):
            vec.wait_ge(*at("cmp_hid", m + 1))
            link(vec.tensor_copy(hst["hb"][:, 0, m:m + 1], ps[:, 7, m:m + 1]), "cmp_hb")
        vec.wait_ge(*at("cmp_kv", 1))
        vec.tensor_copy(hyb["kc"], ps[:, 0, 0:30].rearrange("p (g c) -> p g c", g=2))
        link(vec.tensor_copy(hyb["v_cmp"][0:NCMP, :, DK:2 * DK], ps[0:NCMP, 1, 0:P].rearrange("p (g d) -> p g d", g=2)), "kv_out")
        vec.wait_ge(*at("gate_sig", 2))
        for t in range(NT):
            link(vec.tensor_scalar(hst["gate"][:, 3 * t, :], hst["gate"][:, 3 * t, :], tb("cmp_valid")[:, t:t + 1], None, ALU.mult))

        def row_max(i, g, u):
            t, br = UNITS[u]
            n = {"cmp": (7, 15)[t]}.get(br, P * (t + 1))
            vec.wait_ge(*at("att_score", i * NU + (4 * NU * g + u + 1)))
            m = hst["max"][:, u, :]
            link(vec.tensor_reduce(m, ps[:, 1 + u % 3, :].rearrange("p (h k) -> p h k", h=2)[:, :, 0:n], X_AXIS, ALU.max))
            if br == "ban":
                sink = small[:, bass.ds(i * 2 + (12 + 8 * g), 2)]
                link(vec.tensor_tensor(m, m, sink, ALU.max))
                link(vec.tensor_tensor(hst["sink"][:, u, :], sink, m, ALU.subtract))
            link(vec.tensor_scalar(m, m, -1.0, None, ALU.mult), "att_max")

        def weigh(i, g, u):
            t, br = UNITS[u]
            n = {"cmp": (7, 15)[t]}.get(br, P * (t + 1))
            vec.wait_ge(*at("att_exp", i * NU + (4 * NU * g + u + 2)))
            s = hst["sum"][:, u, :]
            if br == "ban":
                link(vec.tensor_tensor(s, s, hst["esink"][:, u, :], ALU.add))
            link(vec.reciprocal(s, s))
            if br != "ban":
                gate = hst["gate"][:, 3 * t + ("cmp", "slc", "win").index(br), bass.ds(i * 2 + 8 * g, 2)]
                link(vec.tensor_tensor(s, s, gate, ALU.mult))
            p = hyb["p"][:, u % 2, :, 0:n]
            link(vec.tensor_tensor(p, p, s.unsqueeze(2).to_broadcast([P, 2, n]), ALU.mult), "att_p", wait=False)

        nb = UNITS.count((0, "ban")) + UNITS.count((1, "ban"))
        for g in range(2):
            with vec.Fori(0, 4) as i:
                link.begin(i, vec_chain=NU + 2 * nb + NU + nb + (NU - nb), att_max=NU, att_p=NU, q_in=1, att_out=2)
                for k, col in enumerate((QA, QB)):
                    ins = vec.tensor_copy(hyb["q_in"][:, k], p2[:, :, bass.ds(i * P + (col + 512 * g), P)])
                link(ins, "q_in")
                row_max(i, g, 0)
                for u in range(NU):
                    if u + 1 < NU:
                        row_max(i, g, u + 1)
                    weigh(i, g, u)
                for k, kind in enumerate("ab"):
                    vec.wait_ge(*at("att_pv", i * NU + (4 * NU * g + OUT_AT[kind] + 1)))
                    link(vec.tensor_copy(yT[:, bass.ds(i + (4 * g + 8 * k), 1), :], ps[:, 6 + k, 0:T].unsqueeze(1)), "att_out")
            link.end(4)
        residual_add(BLK["out2"], EVB["out2"], None)
        link(vec.memset(stat[:, 22:23], 0.0), "x_done")
        link(vec.memset(stat[:, 24:25], 0.0), "wq_out")
        norm(4)
        norm_cols(3, vc("ffn_norm2", 0, 16), None)
        vec.wait_ge(*at("norm_in", 48))
        vec.wait_ge(*at("hT_turned", 32))
        for t in range(NT):
            ins = vec.tensor_tensor(xs[:, t], xs[:, t], gates[:, 0, :], ALU.mult)
        link(ins)
        vec.wait_ge(*at("keys_turned", 1))
        link(vec.tensor_copy(peer["keysT"], ps[:, 4, 0:2 * P].rearrange("p (s n) -> p s n", s=2)), "keys_out")

        def top16(n, scores, values, places):
            for half in range(2):
                r = slice(8 * half, 8 * half + 8)
                for c in range(n):
                    ins = vec.max(out=values(c)[:, r], in_=scores(c))
                link(ins)
                for c in range(n):
                    ins = vec.max_index(out=places(c)[:, r], in_max=values(c)[:, r], in_values=scores(c))
                link(ins)
                if half == 0:
                    for c in range(n):
                        ins = vec.match_replace(out=scores(c), in_to_replace=values(c)[:, r], in_values=scores(c), imm_value=-3.0e38)
                    link(ins)

        def choose(t):
            vec.wait_ge(*at("score_out", 4 * t + 4))
            side = lambda c: 16 * t + c
            top16(SIDES, lambda c: peer["score"][:, t, c, :], lambda c: peer["val"][:, side(c), :], lambda c: at_u[:, side(c), :])
            mine = slice(SIDES * t, SIDES * (t + 1))
            link(vec.tensor_copy(peer["at_f"][:, mine, :], at_u[:, mine, :]))
            val = peer["val"][:, mine, :].rearrange("p (h s) n -> p h s n", s=2)
            place = peer["at_f"][:, mine, :].rearrange("p (h s) n -> p h s n", s=2)
            wide = [P, HEADS, TOP, TOP]
            sums = peer["sum"][:, t].rearrange("p h (i j) -> p h i j", i=TOP)
            link(vec.tensor_tensor(sums, val[:, :, 0, :].unsqueeze(3).to_broadcast(wide), val[:, :, 1, :].unsqueeze(2).to_broadcast(wide), ALU.add))
            head = lambda h: HEADS * t + h
            top16(HEADS, lambda h: peer["sum"][:, t, h, :], lambda h: peer["best"][:, head(h), :], lambda h: pick_u[:, head(h), :])
            picks = pick_u[:, HEADS * t:HEADS * (t + 1), :].rearrange("p h k -> p (h k)")
            hot = peer["hot"].rearrange("p (h k) i -> p h k i", h=HEADS)
            for s, (op, arg, f, e) in enumerate(((ALU.logical_shift_right, 4, "hi_f", "e1"), (ALU.bitwise_and, 15, "lo_f", "e2"))):
                link(vec.tensor_scalar(part_u, picks, arg, None, op))
                link(vec.tensor_copy(peer[f][:, t, :], part_u))
                full = [P, PICKS, TOP]
                link(vec.tensor_tensor(peer["hot"], peer[f][:, t, :].unsqueeze(2).to_broadcast(full), tb("iota16").unsqueeze(1).to_broadcast(full), ALU.is_equal))
                link(vec.tensor_tensor(hot, hot, place[:, :, s, :].unsqueeze(2).to_broadcast(wide), ALU.mult))
                link(vec.tensor_reduce(peer[e][:, t, :], peer["hot"], X_AXIS, ALU.add))
            link(vec.scalar_tensor_tensor(out=peer["e1"][:, t, :], in0=peer["e1"][:, t, :], scalar=float(P), in1=peer["e2"][:, t, :], op0=ALU.mult, op1=ALU.add))
            link(vec.tensor_copy(expert[:, t, :], peer["e1"][:, t, :]), "experts")
            best = peer["best"][:, HEADS * t:HEADS * (t + 1), :]
            many = [P, HEADS, TOP]
            link(vec.tensor_tensor(peer["weight"][:, t, :].rearrange("p (h k) -> p h k", h=HEADS), best, best[:, :, 0:1].to_broadcast(many), ALU.subtract))
            link(vec.tensor_copy(best, peer["weight"][:, t, :].rearrange("p (h k) -> p h k", h=HEADS)), "best_shift")
            vec.wait_ge(*at("best_exp", t + 1))
            total = peer["total"][:, 0, HEADS * t:HEADS * (t + 1)]
            link(vec.tensor_reduce(total, best, X_AXIS, ALU.add))
            link(vec.reciprocal(total, total))
            link(vec.tensor_tensor(peer["weight"][:, t, :].rearrange("p (h k) -> p h k", h=HEADS), best, total.unsqueeze(2).to_broadcast(many), ALU.mult))

        def arrived(i, base, s):
            vec.wait_ge(sem(f"row{s % ROWS}"), i * 32 + 16 * (base // ROWS + s // ROWS + 1))

        for s in range(ROWS):
            link(vec.memset(stat[:, 25:26], 0.0), "row_used")
        vec.wait_ge(*at("score_out", 8))
        for t in range(NT):
            choose(t)
        for t in range(NT):
            with vec.Fori(0, PICKS // 16) as i:
                link.begin(i, vec_chain=1, row_used=16)
                for s in range(16):
                    arrived(i, PICKS * t, s)
                    slot = row_slots[s % ROWS]
                    link(vec.tensor_tensor_reduce(slot, slot, xs[:, t], 1.0, 0.0, ALU.mult, ALU.add, peer["h16"][:, 0, s:s + 1]), "row_used", wait=(s == 15))
                link(vec.tensor_copy(peer["h"][:, t, bass.ds(i * 16, 16)], peer["h16"][:, 0, :]))
            link.end(PICKS // 16)
            link(vec.memset(stat[:, 26 + t:27 + t], 0.0), "h_done")
        for t in range(NT):
            vec.wait_ge(*at("h_gelu", t + 1))
            link(vec.tensor_tensor(peer["weight"][:, t, :], peer["weight"][:, t, :], peer["h"][:, t, :], ALU.mult))
            with vec.Fori(0, PICKS // 16) as i:
                link.begin(i, row_used=16)
                for s in range(16):
                    arrived(i, PICKS * (NT + t), s)
                    link(vec.scalar_tensor_tensor(out=x[:, t], in0=row_slots[s % ROWS], scalar=peer["weight"][:, t, bass.ds(i * 16 + s, 1)], in1=x[:, t],
                                                  op0=ALU.mult, op1=ALU.add), "row_used")
            link.end(PICKS // 16)
        link(vec.memset(stat[:, 28:29], 0.0), "x_done")
        norm(5, scaled=False)
        for t in range(NT):
            link(vec.scalar_tensor_tensor(out=x[:, t], in0=x[:, t], scalar=stat[:, 6 + t:7 + t], in1=gates[:, 1, :], op0=ALU.mult, op1=ALU.mult), "out_row")
    ctx.close()


DBG = []
VECTORS = ("c", "b_mod", "norm_mix", "norm_ffn", "gla_b_lr", "gla_norm", "gdn_conv", "gdn_a_log", "gdn_dt_bias", "gdn_norm", "pool_scale", "fox_f_bias", "ffn_conv_w", "ffn_conv_b", "norm_final", "attn_norm_2", "cmp_pos_k_2", "cmp_pos_v_2", "sinks_2", "ffn_norm_2", "final_norm_2")


def kernel(**inputs):
    import concourse.bacc as bacc
    from concourse.bass_utils import run_bass_kernel_spmd

    nc = bacc.Bacc("TRN2", target_bir_lowering=False, num_devices=1)
    arrays, views = {}, {}
    for name, value in inputs.items():
        v = np.ascontiguousarray(value)
        shape = [n for n in v.shape if n != 1]
        if name in VECTORS:
            shape = [int(np.prod(v.shape))]
        arrays[f"in_{name}"] = v.reshape(shape)
    arrays["in_tab"] = TAB
    for name, v in arrays.items():
        views[name[3:]] = nc.dram_tensor(name, v.shape, mybir.dt.from_np(v.dtype), kind="ExternalInput").ap()
    out = nc.dram_tensor("out", (1, T, D), F32, kind="ExternalOutput").ap()
    dbg = [nc.dram_tensor(f"dbg{i}", s, F32, kind="ExternalOutput").ap() for i, s in enumerate(DBG)]
    scratch = nc.dram_tensor("bias_rows", (32, 384), F32, kind="Internal").ap()
    build(nc, views, out, scratch, dbg)
    got = run_bass_kernel_spmd(nc, [arrays], core_ids=[0]).results[0]
    if DBG:
        return tuple(got[f"dbg{i}"] for i in range(len(DBG)))
    return got["out"]
```

```python
from contextlib import ExitStack

import concourse.bass as bass
import numpy as np
from concourse import mybir

ALU = mybir.AluOpType
ACT = mybir.ActivationFunctionType
F32 = mybir.dt.float32
I32 = mybir.dt.int32
U32 = mybir.dt.uint32
X_AXIS = mybir.AxisListType.X

P = 128
T = 256
NT = T // P
D = 2048
KT = D // P
NB = 512
SLOTS = 4
KS = KT // SLOTS
HD = 128
DK = 64
CH = 64
FF = 5632
EPS = 1e-6
BIG = 1e30

GLA_Q, GLA_K, GLA_V, GLA_G, GLA_LR = 0, 256, 512, 1024, 1536
GDN_QKV, GDN_G, GDN_B, GDN_A = 1552, 3088, 3600, 3604
POOL_U, FOX_Q, FOX_K, FOX_V, FOX_F, W1 = 3608, 4120, 4632, 5144, 5656, 5660
QA, KC, VC, KSL, VSL, KW, VW, GATE, QB, KB, VB, W2 = 0, 1024, 1152, 1280, 1408, 1536, 1664, 1792, 1840, 2864, 2992, 3120
NCMP = 15
WINS = (2, 4, 8, 16)

BLK = {}
_b = 0
for _n, _c in (("in1", 12), ("out1", 4), ("up", 22), ("down", 11), ("in2", 7), ("out2", 4), ("wq", 8)):
    BLK[_n] = _b
    _b += _c
EVB = {"in1": 0, "out1": 12, "in2": 16, "out2": 23}

VEC = {
    "norm_mix": (0, 0, 16), "norm_ffn": (0, 16, 16), "attn_norm": (0, 32, 16), "ffn_norm2": (0, 48, 16),
    "gdn_conv": (0, 64, 48), "gla_b": (0, 112, 2), "gla_norm": (0, 114, 1), "gdn_norm": (0, 115, 1), "pool_scale": (0, 116, 4),
    "conv01": (1, 0, 88), "pos_k": (1, 88, 16), "pos_v": (1, 104, 16),
    "conv2": (2, 0, 44), "conv_b": (2, 44, 44), "b_mod1": (2, 88, 32),
    "b_mod2": (3, 0, 32),
}
VROWS = (120, 120, 120, 32)

LEVELS = (1, 2, 4, 8, 16, 32)


def tables():
    i = np.arange(P)
    same = (i[:, None] // CH) == (i[None, :] // CH)
    tri = i[:, None] <= i[None, :]
    cols = {}
    cols["ident"] = np.eye(P)
    cols["anti"] = np.eye(P)[::-1]
    cols["ones"] = np.ones((P, P))
    cols["tri"] = tri
    cols["tri_chunk"] = tri & same
    cols["strict_chunk"] = (i[:, None] < i[None, :]) & same
    cols["neg_tri"] = BIG * (i[None, :] > i[:, None])
    for n in LEVELS:
        cols[f"level{n}"] = (i[:, None] // (2 * n) == i[None, :] // (2 * n)) & (i[:, None] // n % 2 == 0) & (i[None, :] // n % 2 == 1)
    cols["level1_t"] = cols["level1"].T
    cols["gla_mask"] = (i[:, None] % CH) <= np.arange(CH)[None, :]
    pick = np.zeros((P, 192))
    pick[:CH, CH - 1] = 1
    pick[CH:, P - 1] = 1
    cols["pick"] = pick
    inv = np.array([[1.0 / min(t + 1, w) for t in range(16)] for w in WINS])
    cols["pool_inv"] = np.broadcast_to(inv.reshape(1, 64), (P, 64))
    reset = np.ones((P, T))
    reset[:, ::CH] = 0
    cols["scan_reset"] = reset
    dist = 255 - np.arange(384)
    f = np.float32
    large = 16 + (np.log(np.maximum(dist, 1).astype(f) / f(16)) / f(np.log(2048 / 16)) * f(16)).astype(np.int32)
    bucket = np.where(dist < 16, dist, np.minimum(large, 31))
    hot = np.zeros((P, 384))
    for m in range(256):
        hot[bucket[m], m] = 1
    cols["bucket"] = hot
    neg = np.zeros((P, 384))
    neg[:, dist < 0] = -BIG
    neg[16:32, dist >= 128] = -BIG
    cols["bias_neg"] = neg
    t = i[:, None] + P * np.arange(NT)[None, :]
    cols["cmp_valid"] = t >= 31
    cols["iota16"] = np.broadcast_to(np.arange(16.0), (P, 16))
    at, off = {}, 0
    for name, c in cols.items():
        at[name] = (off, c.shape[1])
        off += c.shape[1]
    return at, np.concatenate([np.asarray(c, np.float32) for c in cols.values()], axis=1)


TAB_AT, TAB = tables()

STEPS = {
    "fox_vec": (("fox_lf", 1), ("fox_cum_out", 1), ("fox_logit", 4), ("fox_max", 1), ("fox_p", 2)),
    "gla_vec": (("gla_z_out", 1), ("gla_b", 1), ("gla_kd", 1), ("gla_ke", 1)),
    "gla_act": (("gla_eb", 1), ("gla_ekd", 1)),
    "gdn_pe": (("qk_sum", 1), ("gdn_cum", 1), ("gdn_rows", 1), ("gdn_kk", 1), ("k_turned", 1), ("v_turned", 1), ("inv_turned", 1)),
    "gdn_act": (("gdn_beta", 1), ("gdn_alog", 1), ("conv0", 1), ("conv_silu", 1), ("qk_sq", 1), ("qk_root", 1), ("gdn_ecum", 1),
                ("gdn_erows", 1), ("gdn_dT", 1), ("gdn_fac", 1), ("k_scaled", 1), ("inv_out", 1)),
    "gdn_vec": (("gdn_g", 1), ("conv_sum", 1), ("qk_eps", 1), ("gdn_cum_out", 1), ("qk_norm", 2), ("gdn_rows_out", 1), ("kb_out", 2),
                ("gdn_diff", 1), ("gdn_bg", 1), ("attn_out", 1)),
    "start_pe": (("vec_T", 1), ("bias_rows_ps", 1), ("mod_sum", 2), ("gate_sum", 4)),
    "start_act": (("cond", 1), ("vcols", 2), ("gate_out", 4)),
}
STEPS |= {f"load{s}": ((f"mod_slot{s}", 12 * 2 * 16), (f"row{s}", 0)) for s in range(4)}
STEP_OF = {name: (shared, sum(n for _, n in steps[:j])) for shared, steps in STEPS.items() for j, (name, _) in enumerate(steps)}


class Chain:

    def __init__(self, eng, at, own):
        self.eng, self.at, self.own, self.n, self.turn = eng, at, own, {}, None

    def __call__(self, ins, name=None, wait=True):
        name = name or self.own
        ins.then_inc(self.at(name, 0)[0], 1)
        self.n[name] = self.n.get(name, 0) + 1
        if wait:
            turn = self.turn * self.per[name] if self.turn is not None and self.per[name] != 1 else self.turn
            self.eng.wait_ge(*self.at(name, self.n[name] if self.turn is None else turn + self.n[name]))

    def begin(self, i, **per):
        self.per, self.turn, self.before = per, i, dict(self.n)

    def end(self, turns):
        for name, n in self.n.items():
            passed = n - self.before.get(name, 0)
            assert passed == self.per.get(name, 0), (name, passed)
            self.n[name] = n + (turns - 1) * passed
        self.turn = None


def build(nc, a, out, scratch):
    ctx = ExitStack()
    sb = lambda n, s, d=F32: ctx.enter_context(nc.sbuf_tensor(n, s, d))
    sems = {}

    def sem(name):
        name = STEP_OF[name][0] if name in STEP_OF else name
        if name not in sems:
            sems[name] = ctx.enter_context(nc.semaphore(name))
        return sems[name]

    def at(name, n):
        return sem(name), n + STEP_OF[name][1] if name in STEP_OF else n

    tab = sb("tab", [P, TAB.shape[1]])
    tb = lambda name, w=None: tab[:, TAB_AT[name][0]:TAB_AT[name][0] + (w or TAB_AT[name][1])]
    ident = tb("ident")
    ones = tb("ones")
    vrows = sb("vrows", [P, 4, P])
    vcols = sb("vcols", [P, 4, P])
    vc = lambda name, k=0, n=1: vcols[:, VEC[name][0], VEC[name][1] + k:VEC[name][1] + k + n]
    small = sb("small", [P, 4 + 4 + 4 + 16])
    x = sb("x", [P, NT, D])
    ring = sb("ring", [P, SLOTS, KS, NB])
    hT = sb("hT", [P, KT, T])
    yT = sb("yT", [P, KT, T])
    xs = yT[:].rearrange("p k t -> p (k t)").rearrange("p (t d) -> p t d", t=NT)
    gates = sb("gates", [P, 2, D])
    proj = sb("proj", [P, NT, W1])
    c_col = sb("c_col", [P, KT])
    mod_col = sb("mod_col", [P, 64])
    stat = sb("stat", [P, 32])
    arena = sb("arena", [P, 12800])
    ps = ctx.enter_context(nc.psum_tensor("ps", [P, 8, NB], F32))

    flat_proj = proj[:].rearrange("p t n -> p (t n)")

    def carve(base, sizes):
        views, off = {}, 0
        for name, shape in sizes.items():
            n = int(np.prod(shape))
            v = base[:, off:off + n]
            if len(shape) == 2:
                v = v.rearrange("p (a b) -> p a b", b=shape[1])
            elif len(shape) == 3:
                v = v.rearrange("p (a b c) -> p a b c", b=shape[1], c=shape[2])
            views[name] = v
            off += n
        assert off <= base.shape[1], (off, base.shape)
        return views

    fox = carve(arena[:], {
        "q": (4, T), "k": (4, T), "z": (1, 8), "e": (1, 8), "l": (1, 8), "cum": (1, 8), "decay": (4, 384), "logit": (4, 384),
        "max": (1, 8), "sum": (1, 8), "rec": (1, 8), "pT": (4, 384)})
    pool = carve(hT[:].rearrange("p k t -> p (k t)"), {"u": (4, T + 16), "w": (4, T + 16), "w2": (4, T + 16), "pw": (4, P), "w_lr": (1, T)})
    act_store = flat_proj[:, 0:44 * T].rearrange("p (k t) -> p k t", t=T)
    w1v = {n: a[n].rearrange("(k p) n -> p k n", p=P) for n in ("w_in", "w_out", "ffn_w_gate", "ffn_w_up", "w_in_2", "w_out_2", "peer_wq_2")}
    w_mod = a["w_mod"].rearrange("(p k) n -> p k n", k=KT)
    MB = 1024
    mod = carve(arena[:], {"ring": (4, 2, MB), "acc": (4, MB)})
    MOD_BANK = (7, 3)
    MOD_UNITS = KT // 2
    pair_buf = lambda n: (gla["pair"][:, 0], gla["pair"][:, 1], hT[:].rearrange("p k t -> p (k t)"))[n % 3][:, 0:32 * (CH - 8 * (n % 8))]
    gate_pairs = gates[:].rearrange("p g (q b n) -> p (g q) b n", b=2, n=NB)
    w_lr = pool["w_lr"][0:16, 0, :]
    gla = carve(arena[:], {
        "q": (2, T), "k": (2, T), "gate": (4, T), "lr": (1, T), "z": (2, T), "e": (2, T), "b": (2, T), "pair": (2, 2048),
        "v": (4, 512), "att": (2, T), "qe": (2, T), "ke": (2, T), "ke_tok": (8, P), "state": (2, P)})
    TURNS = [(FOX_Q, P, 2, "act"), (FOX_Q + 256, P, 2, "act"), (FOX_K, P, 2, "vec"), (FOX_K + 256, P, 2, "vec"),
             (POOL_U, P, 2, "vec"), (POOL_U + 256, P, 2, "vec"),
             (GLA_Q, P, 2, "act"), (GLA_K, P, 2, "vec"), (GLA_G, P, 2, "act"), (GLA_G + 256, P, 2, "act"), (GLA_LR, 16, 1, "vec")]
    TURNS += [(GDN_QKV + 256 * j, P, 2, "vec") for j in range(6)] + [(GDN_G, P, 2, "act"), (GDN_G + 256, P, 2, "act")]
    FOX_T, POOL_T, GLA_T, GDN_T = 0, 4, 6, 11

    def turn_taken(g):
        who = TURNS[g][3]
        return sem("turn_" + who), sum(t[3] == who for t in TURNS[:g + 1])

    gdn = carve(arena[:], {
        "in": (12, 260), "conv": (12, T), "gate": (4, T), "sq": (8, T), "beta": (1, 8), "z": (1, 8), "e": (1, 8), "l": (1, 8), "u1": (1, 8),
        "g": (1, 8), "cum": (1, 8), "ecum": (1, 8), "fac": (2, 8), "decay": (1, 4), "state": (4, P), "new": (4, P), "u": (8, P)})
    gdn |= carve(flat_proj, {"rows": (8, P), "erows": (8, P), "dT": (8, P), "LT": (8, P), "off": (8, P), "inv": (8, P), "invT": (8, P),
                             "X": (8, P), "attnT": (8, P), "wT": (8, P), "kb": (4, T)})
    gdn |= carve(hT[:].rearrange("p k t -> p (k t)"), {"k_end": (2, 8, P), "k_w": (8, P), "v_b": (8, P)})
    ffn = carve(arena[:], {"y": (1, NB), "y2": (2, NB), "gate": (4, T), "act": (2, 4, T)})
    p2 = flat_proj[:, 0:NT * W2].rearrange("p (t n) -> p t n", t=NT)
    DOWN = FF // P // SLOTS
    BRANCHES = ("slc", "win", "cmp", "ban")
    UNITS = [(t, br) for t in range(NT) for br in BRANCHES]
    NU = len(UNITS)
    OUT_AT = {"a": UNITS.index((1, "cmp")) + 1, "b": NU}
    hyb = carve(arena[:], {"bias": (32, T), "v": (3, 4, 192), "p": (2, 2, T), "pT": (2, 4, P)})
    hyb |= carve(hT[:].rearrange("p k t -> p (k t)"), {"xk": (4, T), "kT": (6, T), "q": (2, 2, T), "hid": (2, 30), "kc": (2, 15)})
    hyb |= carve(flat_proj[:, NT * W2:], {"w1": (2, 16, P), "v_cmp": (2, 192), "q_in": (2, NT, P)})
    hst = carve(vrows[:].rearrange("p a b -> p (a b)"), {
        "w2": (2, P), "gate": (6, 16), "max": (NU, 2), "sum": (NU, 2), "sink": (NU, 2), "esink": (NU, 2), "hb": (1, 2)})
    kv_twice = yT[:].rearrange("p k t -> p (k t)")[:, 0:20 * P].rearrange("p (s m) -> p s m", m=P)
    TWICE = (KC, VC, KSL, KW, KB)
    rel = sb("rel", [32, 32])
    bias_rows = arena[0:32, 4 * 3 * MB:4 * 3 * MB + 384]
    KCOL = (KSL, KW, KB)
    VCOL = (VSL, VW, VB)
    HEADS, TOP = 8, 16
    PICKS = HEADS * TOP
    SIDES = 2 * HEADS
    peer = carve(arena[:], {"q": (SIDES, T), "score": (2, SIDES, P), "sum": (2, SIDES // 2, 256)})
    choice = [carve(base, {"hot": (PICKS, TOP), "val": (SIDES, TOP), "at_f": (SIDES, TOP), "hi_f": (1, PICKS), "lo_f": (1, PICKS), "e1": (1, PICKS), "e2": (1, PICKS)})
              for base in (flat_proj, arena[:])]
    spare = flat_proj[:, 4 * D:]
    peer |= carve(spare, {"best": (2 * HEADS, TOP), "h": (2, PICKS), "weight": (2, PICKS), "keys": (2, P), "keysT": (2, P), "h16": (1, 16), "total": (1, 2 * HEADS),
                          "at_u": (2 * SIDES, TOP), "pick_u": (2 * HEADS, TOP), "expert": (2, PICKS), "now": (2, 8)})
    row_slots = [flat_proj[:, D * s:D * (s + 1)] for s in range(4)] + [ring[:, s].rearrange("p k n -> p (k n)") for s in range(4)]
    ROWS = len(row_slots)
    at_u, pick_u = peer["at_u"].bitcast(U32), peer["pick_u"].bitcast(U32)
    part_u = carve(hst["w2"].rearrange("p a b -> p (a b)"), {"x": (1, PICKS)})["x"][:, 0, :].bitcast(U32)
    expert = peer["expert"].bitcast(I32)
    expert_now = peer["now"].bitcast(I32)
    block = ctx.enter_context(nc.Block())

    @block.sync
    def _(sp):
        def load(name, dst, src):
            sp.dma_start(dst, src).then_inc(sem(name), 16)

        load("c_in", c_col[:], a["c"].rearrange("(p k) -> p k", k=KT))
        load("x_in", x[:], a["x"].rearrange("(t p) d -> p t d", p=P))
        load("tab_in", tab[:], a["tab"])
        load("tab_in", rel[:], a["rel_bias_2"])

        def slot_load(view, u, s, first, cols, w, turn=0):
            if not first:
                sp.wait_ge(*at("unit_used", turn + (u + s - SLOTS + 1)))
            sp.dma_start(ring[:, s, :, 0:w], view[:, KS * s:KS * (s + 1), cols]).then_inc(sem(f"slot{s}"), 16)

        for name, (tile, r0, n) in VEC.items():
            src = {"norm_mix": "norm_mix", "norm_ffn": "norm_ffn", "attn_norm": "attn_norm_2", "ffn_norm2": "ffn_norm_2",
                   "gdn_conv": "gdn_conv", "gla_b": "gla_b_lr", "gla_norm": "gla_norm", "gdn_norm": "gdn_norm",
                   "pool_scale": "pool_scale", "conv01": "ffn_conv_w", "pos_k": "cmp_pos_k_2", "pos_v": "cmp_pos_v_2",
                   "conv2": "ffn_conv_w", "conv_b": "ffn_conv_b", "b_mod1": "b_mod", "b_mod2": "b_mod"}[name]
            skip = {"conv2": 88, "b_mod2": 48}.get(name, 0)
            load("rows_in", vrows[r0:r0 + n, tile, :], a[src].rearrange("(r c) -> r c", c=P)[skip:skip + n, :])
        for j, (src, n) in enumerate((("fox_f_bias", 4), ("gdn_dt_bias", 4), ("gdn_a_log", 4), ("sinks_2", 16))):
            load("small_in", small[:, 4 * j:4 * j + n], a[src].partition_broadcast(P))
        sp.wait_ge(*at("gates_zero", 1))
        for g in range(2):
            load("gate_bias_in", gates[0:1, g, :], a["b_mod"].rearrange("(g n) -> g n", n=D)[2 + 3 * g:3 + 3 * g, :])
        sp.wait_ge(*at("bias_rows", 1))
        sp.dma_start(scratch, bias_rows).then_inc(sem("bias_saved"), 16)

        def stream(view, blk, n, tail, first=0):
            with sp.Fori(first, n) as i:
                for s in range(SLOTS):
                    slot_load(view, blk * SLOTS, s, False, bass.ds(i * NB, NB), NB, i * SLOTS)
            if tail:
                for s in range(SLOTS):
                    slot_load(view, (blk + n) * SLOTS, s, False, slice(n * NB, n * NB + tail), tail)

        sp.wait_ge(*at("mod_used", 3 * MOD_UNITS))
        for s in range(SLOTS):
            slot_load(w1v["w_in"], 0, s, True, slice(0, NB), NB)
        stream(w1v["w_in"], BLK["in1"], 11, W1 - 11 * NB, first=1)
        sp.wait_ge(*at("unit_used", SLOTS * BLK["out1"]))
        load("mixer_w_in", w_lr, a["gla_w_lr"])
        load("mixer_w_in", pool["pw"], a["pool_w"].rearrange("g c d -> c g d"))
        sp.wait_ge(*at("fox_out", 4))
        for half in range(2):
            for c in range(4):
                load("gla_v_in", gla["v"][CH * half:CH * (half + 1), c, :],
                     proj[CH * (c % 2):CH * (c % 2 + 1), c // 2, GLA_V:GLA_V + 512])
        stream(w1v["w_out"], BLK["out1"], 4, 0)
        sp.wait_ge(*at("x_done", 1))
        load("norm_in", gates[:, 0, :], a["norm_final"].partition_broadcast(P))
        with sp.Fori(0, 11) as i:
            for m, name in enumerate(("ffn_w_gate", "ffn_w_up")):
                for s in range(SLOTS):
                    slot_load(w1v[name], (BLK["up"] + m) * SLOTS, s, False, bass.ds(i * NB, NB), NB, i * (2 * SLOTS))
        wd = a["ffn_w_down"].rearrange("(j s p) n -> p j s n", s=SLOTS, p=P)
        with sp.Fori(0, DOWN) as i:
            for s in range(SLOTS):
                sp.wait_ge(*at("unit_used", i * SLOTS + (BLK["down"] * SLOTS + s - SLOTS + 1)))
                sp.dma_start(ring[:, s, :, :], wd[:, bass.ds(i, 1), s, :].rearrange("p o (k n) -> p (o k) n", n=NB)).then_inc(sem(f"slot{s}"), 16)
        sp.wait_ge(*at("x_done", 2))
        load("norm_in", gates[:, 1, :], a["final_norm_2"].partition_broadcast(P))
        for m, name in enumerate(("cmp_w1_k_2", "cmp_w1_v_2")):
            load("cmp_w_in", hyb["w1"][:, m], a[name].rearrange("(j p) n -> p j n", p=P))
        for m, name in enumerate(("cmp_w2_k_2", "cmp_w2_v_2")):
            for c in range(2):
                load("cmp_w_in", hst["w2"][:, m, DK * c:DK * (c + 1)], a[name])
        sp.wait_ge(*at("bias_saved", 16))
        load("bias_in", hyb["bias"], bass.AP(scratch.tensor, 0, [[1, P], [384, 32], [1, T]]))
        stream(w1v["w_in_2"], BLK["in2"], 6, W2 - 6 * NB)
        sp.wait_ge(*at("x_done", 3))
        load("norm_in", gates[:, 0, :], a["ffn_norm_2"].partition_broadcast(P))
        stream(w1v["w_out_2"], BLK["out2"], 4, 0)
        for t in range(NT):
            stream(w1v["peer_wq_2"], BLK["wq"] + 4 * t, 4, 0)
        for t in range(NT):
            sp.wait_ge(*at("out_row", t + 1))
            sp.dma_start(out[0, P * t:P * (t + 1), :], x[:, t]).then_inc(sem("out_saved"), 16)
        sp.wait_ge(*at("out_saved", 32))

    @block.gpsimd
    def _(pool_eng):
        def mod_load(cols, j):
            pool_eng.dma_start(mod["ring"][:, j % 4], w_mod[:, 2 * j:2 * j + 2, cols]).then_inc(sem(f"mod_slot{j % 4}"), 16)

        for j in range(4):
            mod_load(slice(0, MB), j)
        pool_eng.memset(gates[:], 0.0).then_inc(sem("gates_zero"), 1)
        for j in range(4, MOD_UNITS):
            pool_eng.wait_ge(*at("mod_used", j - 3))
            mod_load(slice(0, MB), j)
        with pool_eng.Fori(1, 12) as i:
            for j in range(MOD_UNITS):
                pool_eng.wait_ge(*at("mod_used", i * MOD_UNITS + (j - 3)))
                pool_eng.sem_inc(sem("pool_turn"), 1)
                mod_load(bass.ds(i * MB, MB), j)
        plink = Chain(pool_eng, at, "pool_chain")
        pool_eng.wait_ge(*at("unit_used", SLOTS * BLK["out1"]))
        pu, pw, pw2 = pool["u"], pool["w"], pool["w2"]
        N = T + 16
        for buf in (pu, pw, pw2):
            ins = pool_eng.memset(buf[:, :, 0:16], 0.0)
            plink(ins, "pool_zero")
        g0, n0 = turn_taken(POOL_T + 1)
        pool_eng.wait_ge(g0, n0)
        plink(pool_eng.tensor_tensor(pw[:, :, 1:N], pu[:, :, 1:N], pu[:, :, 0:N - 1], ALU.add))
        plink(pool_eng.tensor_tensor(pw2[:, 1:4, 2:N], pw[:, 1:4, 2:N], pw[:, 1:4, 0:N - 2], ALU.add))
        plink(pool_eng.tensor_tensor(pw[:, 2:4, 4:N], pw2[:, 2:4, 4:N], pw2[:, 2:4, 0:N - 4], ALU.add))
        plink(pool_eng.tensor_tensor(pw2[:, 3:4, 8:N], pw[:, 3:4, 8:N], pw[:, 3:4, 0:N - 8], ALU.add))
        inv = tb("pool_inv").rearrange("p (g n) -> p g n", n=16)
        for g, win in enumerate(WINS):
            src = (pw, pw2)[g % 2]
            plink(pool_eng.tensor_tensor(src[:, g, 16:32], src[:, g, 16:32], inv[:, g, :], ALU.mult))
            plink(pool_eng.tensor_scalar(src[:, g, 32:N], src[:, g, 32:N], 1.0 / win, None, ALU.mult))
            plink(pool_eng.tensor_tensor(src[:, g, 16:N], src[:, g, 16:N], pu[:, g, 16:N], ALU.subtract), "pool_delta")
        for n in range(16):
            g, sblk = n // 8, n % 8
            t0 = 8 * sblk
            d = pair_buf(n).rearrange("p (c s t) -> p c s t", c=4, s=8)
            pool_eng.wait_ge(*at("pair_k", n + 1))
            qv = gla["q"][:, g, :].rearrange("p (c t) -> p c t", c=4)[:, :, t0:CH].unsqueeze(2).to_broadcast([P, 4, 8, CH - t0])
            plink(pool_eng.tensor_tensor(d, d, qv, ALU.mult), "pair_q", wait=False)
        for phase, table in enumerate((a["peer_u_2"], a["peer_v_2"])):
            for t in range(NT):
                pool_eng.wait_ge(*at("experts", t + 1))
                base = PICKS * (NT * phase + t)
                with pool_eng.Fori(0, PICKS // (2 * ROWS)) as i:
                    for half in range(2):
                        pool_eng.wait_ge(*at("row_used", i * (2 * ROWS) + (base + ROWS * half + 1)))
                        pool_eng.tensor_copy(expert_now[:, half, :], expert[:, t, bass.ds(i * (2 * ROWS) + ROWS * half, ROWS)]).then_inc(sem("experts_now"), 1)
                        for s in range(ROWS):
                            if s == 4:
                                pool_eng.wait_ge(*at("unit_used", SLOTS * (BLK["wq"] + 4 * NT)))
                            if s == 0:
                                pool_eng.wait_ge(*at("experts_now", i * 2 + (base // ROWS + half + 1)))
                            pool_eng.wait_ge(*at("row_used", i * (2 * ROWS) + (base + ROWS * half + s + 1)))
                            pool_eng.sem_inc(sem("pool_turn"), 1)
                            pool_eng.indirect_dma_start(row_slots[s], None, table, bass.IndirectOffsetOnAxis(expert_now[:, half, s:s + 1], 0))\
                                    .then_inc(sem(f"row{s}"), 16)

    @block.scalar
    def _(act):
        link = Chain(act, at, "act_chain")
        act.wait_ge(*at("c_in", 16))
        act.activation(c_col[:], c_col[:], ACT.Silu).then_inc(sem("cond"), 1)
        act.wait_ge(*at("vec_T", 1))
        turned = ps[:, 7, :].rearrange("p (a b) -> p a b", b=P)
        act.copy(vcols[:, 0:3, 0:120], turned[:, 0:3, 0:120]).then_inc(sem("vcols"), 1)
        act.copy(vcols[:, 3, 0:32], turned[:, 3, 0:32]).then_inc(sem("vcols"), 1)

        def norm(n, scaled=True):
            for t in range(NT):
                act.activation(xs[:, t], x[:, t], ACT.Square, accum_out=stat[:, t:t + 1]).then_inc(sem("squares"), 1)
            act.wait_ge(*at("mean_sq", n + 1))
            act.activation(stat[:, 4:6], stat[:, 2:4], ACT.Sqrt).then_inc(sem("root"), 1)
            if not scaled:
                return
            act.wait_ge(*at("squares", 2 * n + 2))
            act.wait_ge(*at("rstd", n + 1))
            act.activation(xs[:, 1], x[:, 1], ACT.Copy, scale=stat[:, 7:8]).then_inc(sem("xs_act"), 1)

        def norm_cols(n, scale, shift):
            for g in range(0, 8, 2):
                act.wait_ge(*at("hT_turned", n * 8 + g + 1))
                for k in range(2):
                    f = 2 * g + k
                    ins = act.activation(hT[:, f, :], ps[:, g % 4, T * k:T * (k + 1)], ACT.Identity, scale=scale[:, f:f + 1],
                                         bias=shift[:, f:f + 1] if shift is not None else 0.0)
                ins.then_inc(sem("hT_act"), 1)

        def evac(blk, n, dst, tail, tiles=1):
            def one(turn, cols, b, w):
                act.wait_ge(*at("unit_used", turn + SLOTS * (blk + b + 1)))
                pair = 2 * (b % 2)
                act.copy(dst[:, 0:tiles, cols], ps[:, pair:pair + tiles, 0:w]).then_inc(sem("evac_act"), 1)
            with act.Fori(0, n // 2) as i:
                for b in range(2):
                    one(i * (2 * SLOTS), bass.ds(i * (2 * NB) + b * NB, NB), b, NB)
            if n % 2:
                one(0, slice((n - 1) * NB, n * NB), n - 1, NB)
            if tail:
                one(0, slice(n * NB, n * NB + tail), n, tail)

        act.wait_ge(*at("x_in", 16))
        norm(0)
        act.wait_ge(*at("mod_cols", 1))
        norm_cols(0, mod_col[:, 16:32], mod_col[:, 0:16])
        evac(BLK["in1"], 11, proj, W1 - 11 * NB, tiles=2)
        def taken(g):
            act.wait_ge(*at("turned", g + 1))
            return ps[:, g % 4, :]

        act_turn = lambda ins: ins.then_inc(sem("turn_act"), 1)

        def log1p_exp(n, e, out):
            act.wait_ge(*at("abs_z", n + 1))
            link(act.activation(e, e, ACT.Exp, scale=-1.0), "exp_z")
            link(act.activation(out, e, ACT.Ln, bias=1.0), "ln_z")

        act.wait_ge(*at("mod_used", 12 * MOD_UNITS))
        for j in range(2):
            act_turn(act.activation(fox["q"][:, 2 * j:2 * j + 2, :], taken(FOX_T + j).rearrange("p (h t) -> p h t", h=2), ACT.Copy, scale=HD ** -0.5))
        log1p_exp(0, fox["e"], fox["l"])
        act.wait_ge(*at("fox_max", 1))
        fm, fs = fox["max"][:, 0, :], fox["sum"][:, 0, :]
        for h in range(4):
            for t in range(NT):
                part = fox["logit"][:, h, (0, P)[t]:(P, 3 * P)[t]]
                act.activation(part, part, ACT.Exp, bias=fm[:, 4 * t + h:4 * t + h + 1], accum_out=fs[:, 4 * t + h:4 * t + h + 1])\
                   .then_inc(sem("fox_exp"), 1)
        for h in range(4):
            act.wait_ge(*at("fox_pT", h + 1))
            act.copy(fox["pT"][:, h, :], ps[:, 5 + h % 2, 0:384]).then_inc(sem("fox_pT_out"), 1)
        for g in range(4):
            act.wait_ge(*at("pool_y", 1))
            act.activation(yT[:, 8 + g, :], ps[:, 5 + g // 2, T * (g % 2):T * (g % 2 + 1)], ACT.Copy, scale=vc("pool_scale", g))\
               .then_inc(sem("pool_out"), 1)
        act.wait_ge(*at("fox_out", 4))
        act.wait_ge(*at("fox_pT_out", 4))
        act_turn(act.activation(gla["q"], taken(GLA_T).rearrange("p (h t) -> p h t", h=2), ACT.Copy, scale=DK ** -0.5))
        for j in range(2):
            act_turn(act.activation(gla["gate"][:, 2 * j:2 * j + 2, :], taken(GLA_T + 2 + j).rearrange("p (h t) -> p h t", h=2), ACT.Silu))
        log1p_exp(1, gla["e"], gla["e"])
        act.wait_ge(*at("gla_b", 1))
        act.activation(gla["z"], gla["b"], ACT.Exp).then_inc(sem("gla_eb"), 1)
        act.wait_ge(*at("gla_kd", 1))
        act.activation(gla["e"], gla["e"], ACT.Exp).then_inc(sem("gla_ekd"), 1)
        for b in range(2):
            act.wait_ge(*at("ke_turned", b + 1))
            act.copy(gla["ke_tok"][0:CH, 4 * b:4 * b + 4, :], ps[0:CH, 5 + b, :].rearrange("p (n d) -> p n d", d=P)).then_inc(sem("ke_tok"), 1)
        for n in range(16):
            d = pair_buf(n)
            act.wait_ge(*at("pair_diff", n + 1))
            act.activation(d, d, ACT.Exp).then_inc(sem("pair_exp"), 1)
            if n % 3 == 2 and n < 12:
                act.wait_ge(*at("gate_sum", n // 3 + 1))
                act.copy(gate_pairs[:, n // 3], ps[:, 6:8, :]).then_inc(sem("gate_out"), 1)

        def head_norm(m, sq):
            act.wait_ge(*at("mix_o", m + 1))
            for j in range(2):
                act.activation(sq[:, NB * j:NB * (j + 1)], ps[:, 6 + j, :], ACT.Square).then_inc(sem("o_sq"), 1)
            act.wait_ge(*at("o_mean", m + 1))
            act.activation(sq, sq, ACT.Sqrt).then_inc(sem("o_root"), 1)

        head_norm(0, gla["pair"].rearrange("p a b -> p (a b)")[:, 0:1024])
        act.wait_ge(*at("mix_out", 2))
        gsm = lambda name: gdn[name][:, 0, :]
        by_tile = lambda v: v.rearrange("p (t h) -> p t h", t=NT)
        act.activation(by_tile(gsm("beta")), proj[:, :, GDN_B:GDN_B + 4], ACT.Sigmoid).then_inc(sem("gdn_beta"), 1)
        for j in range(2):
            act_turn(act.activation(gdn["gate"][:, 2 * j:2 * j + 2, :], taken(GDN_T + 6 + j).rearrange("p (h t) -> p h t", h=2), ACT.Silu))
        link(act.activation(gdn["decay"][:, 0, :], small[:, 8:12], ACT.Exp), "gdn_alog")
        log1p_exp(2, gdn["e"], gdn["l"])
        g0, n0 = turn_taken(GDN_T + 5)
        act.wait_ge(g0, n0)
        for i in range(12):
            ins = act.activation(gdn["conv"][:, i, :], gdn["in"][:, i, 1:T + 1], ACT.Copy, scale=vc("gdn_conv", i))
        link(ins, "conv0")
        act.wait_ge(*at("conv_sum", 1))
        link(act.activation(gdn["conv"], gdn["conv"], ACT.Silu), "conv_silu")
        act.activation(gdn["sq"], gdn["conv"][:, 0:8, :], ACT.Square).then_inc(sem("qk_sq"), 1)
        act.wait_ge(*at("qk_eps", 1))
        act.activation(gdn["sq"], gdn["sq"], ACT.Sqrt).then_inc(sem("qk_root"), 1)
        act.wait_ge(*at("gdn_cum_out", 1))
        act.activation(gdn["ecum"], gdn["cum"], ACT.Exp).then_inc(sem("gdn_ecum"), 1)
        act.wait_ge(*at("gdn_rows_out", 1))
        act.activation(gdn["erows"], gdn["rows"], ACT.Exp).then_inc(sem("gdn_erows"), 1)
        act.wait_ge(*at("gdn_diff", 1))
        act.activation(gdn["dT"], gdn["dT"], ACT.Exp).then_inc(sem("gdn_dT"), 1)
        for c2 in range(2):
            r = slice(CH * c2, CH * (c2 + 1))
            ins = act.activation(gdn["fac"][r, c2, :], gdn["fac"][r, c2, :], ACT.Exp)
        link(ins, "gdn_fac")
        act.wait_ge(*at("k_turned", 1))
        act.wait_ge(*at("gdn_bg", 1))
        for n in range(8):
            src = ps[:, n // 4, P * (n % 4):P * (n % 4 + 1)]
            for c2 in range(2):
                act.activation(gdn["k_end"][:, c2, n, :], src, ACT.Copy, scale=gdn["fac"][:, c2, n:n + 1])
            ins = act.activation(gdn["k_w"][:, n, :], src, ACT.Copy, scale=gsm("u1")[:, n:n + 1])
        ins.then_inc(sem("k_scaled"), 1)
        flat = lambda name: gdn[name].rearrange("p n c -> p (n c)")
        act.wait_ge(*at("inv_turned", 1))
        act.copy(flat("inv")[:, 0:NB], ps[:, 4, :])
        act.copy(flat("inv")[:, NB:2 * NB], ps[:, 5, :]).then_inc(sem("inv_out"), 1)
        for lv in range(1, len(LEVELS)):
            act.wait_ge(*at("inv_x", lv))
            act.copy(flat("X")[:, 0:NB], ps[:, 4, :])
            act.copy(flat("X")[:, NB:2 * NB], ps[:, 5, :]).then_inc(sem("inv_x_out"), 1)
        act.wait_ge(*at("gdn_w", 1))
        act.copy(flat("wT")[:, 0:NB], ps[:, 6, :])
        act.copy(flat("wT")[:, NB:2 * NB], ps[:, 7, :]).then_inc(sem("gdn_w_out"), 1)
        head_norm(1, gdn["sq"].rearrange("p a b -> p (a b)")[:, 0:1024])
        def residual_evac(blk, ev):
            for i in range(4):
                act.wait_ge(*at("unit_used", SLOTS * (blk + i + 1)))
                if i or ev > 12:
                    act.wait_ge(*at("added", ev // 23 * 4 + i))
                act.copy(ffn["y"][:, 0, :], ps[:, 2 * (i % 2), :]).then_inc(sem("evac_act"), 1)

        act.wait_ge(*at("mix_out", 4))
        residual_evac(BLK["out1"], EVB["out1"])
        act.wait_ge(*at("x_done", 1))
        norm(1)
        norm_cols(1, mod_col[:, 48:64], mod_col[:, 32:48])
        act.wait_ge(*at("ffn_credit", 1))
        with act.Fori(0, 11) as i:
            act.wait_ge(*at("unit_used", i * 8 + SLOTS * (BLK["up"] + 1)))
            act.wait_ge(*at("up_free", i + 1))
            for f in range(4):
                act.activation(ffn["gate"][:, f, :], ps[:, f, 0:T], ACT.Identity, scale=vcols[:, 2, bass.ds(i * 4 + f, 1)],
                               bias=vcols[:, 2, bass.ds(i * 4 + (44 + f), 1)]).then_inc(sem("conv_tap2"), 1)
            act.wait_ge(*at("gate_free", i + 2))
            act.activation(ffn["gate"], ffn["gate"], ACT.Silu).then_inc(sem("gate_silu"), 1)
        act.wait_ge(*at("up_free", 12))
        for j in range(2):
            act.copy(ffn["act"][:, j], act_store[:, 4 * j:4 * j + 4, :]).then_inc(sem("staged"), 1)
        with act.Fori(2, DOWN - 1, 2) as i:
            for par in range(2):
                act.wait_ge(*at("unit_used", i * SLOTS + SLOTS * (BLK["down"] - 1 + par)))
                act.copy(ffn["act"][:, par], act_store[:, bass.ds(i * 4 + 4 * par, 4), :]).then_inc(sem("staged"), 1)
        act.wait_ge(*at("unit_used", SLOTS * (BLK["down"] + DOWN - 2)))
        act.copy(ffn["act"][:, 0], act_store[:, 4 * (DOWN - 1):4 * DOWN, :]).then_inc(sem("staged"), 1)
        act.wait_ge(*at("x_done", 2))
        norm(2, scaled=False)
        act.wait_ge(*at("x_done", 3))
        norm(3)
        norm_cols(2, vc("attn_norm", 0, 16), None)
        evac(BLK["in2"], 6, p2, W2 - 6 * NB)
        act.wait_ge(*at("evac_vec", EVB["out2"] + 2))
        act.wait_ge(*at("evac_act", EVB["out2"] + 2))
        for t in range(NT):
            act.activation(hst["gate"][:, 3 * t:3 * t + 3, :], p2[:, t, GATE:GATE + 48].rearrange("p (h b) -> p b h", b=3), ACT.Sigmoid)\
               .then_inc(sem("gate_sig"), 1)
        for m in range(2):
            act.wait_ge(*at("cmp_hid", m + 1))
            act.wait_ge(*at("cmp_hb", m + 1))
            act.activation(hyb["hid"][:, m, :], ps[:, 2 + m, 0:30], ACT.Gelu_apprx_tanh, bias=hst["hb"][:, 0, m:m + 1]).then_inc(sem("cmp_gelu"), 1)

        def softmax_exp(i, g, u):
            t, br = UNITS[u % NU]
            n = {"cmp": (7, 15)[t]}.get(br, P * (t + 1))
            act.wait_ge(*at("att_max", i * NU + (4 * NU * g + u + 1)))
            act.wait_ge(*at("att_turned", i * NU + (4 * NU * g + max(u - 1, 0) + 1)))
            if br == "ban":
                act.activation(hst["esink"][:, u % NU, :], hst["sink"][:, u % NU, :], ACT.Exp)
            for h in range(2):
                ins = act.activation(hyb["p"][:, u % 2, h, 0:n], ps[:, u % 4, T * h:T * h + n], ACT.Exp, bias=hst["max"][:, u % NU, h:h + 1],
                                     accum_out=hst["sum"][:, u % NU, h:h + 1])
            ins.then_inc(sem("att_exp"), 1)

        def turned_out(i, g, u):
            t, br = UNITS[u % NU]
            act.wait_ge(*at("att_turned", i * NU + (4 * NU * g + u + 2)))
            act.wait_ge(*at("att_pv", i * NU + (4 * NU * g + max(u - 1, 0) + 1)))
            r, n = {"cmp": ((7, 15)[t], 2)}.get(br, (P, 2 * (t + 1)))
            act.copy(hyb["pT"][0:r, u % 2, 0:n, :], ps[0:r, 4 + u % 2, 0:P * n].rearrange("p (a b) -> p a b", b=P)).then_inc(sem("att_pT"), 1)

        act.wait_ge(*at("q_zero", 1))
        def q_out(i, g):
            act.wait_ge(*at("q_turned", i + (4 * g + 1)))
            for h in range(2):
                r = slice(DK * h, DK * (h + 1))
                ins = act.activation(hyb["q"][r, :, h, :], ps[r, 0, :].rearrange("p (k t) -> p k t", k=2), ACT.Copy, scale=DK ** -0.5)
            ins.then_inc(sem("q_out"), 1)

        def head_pair(i, g, more):
            for u in range(NU):
                if u + 1 < NU or more:
                    softmax_exp(i, g, u + 1)
                if u == 5 and more:
                    q_out(i + 1, g)
                turned_out(i, g, u)

        for g in range(2):
            q_out(0, g)
            softmax_exp(0, g, 0)
            with act.Fori(0, 3) as i:
                head_pair(i, g, True)
            head_pair(3, g, False)
        residual_evac(BLK["out2"], EVB["out2"])
        act.wait_ge(*at("x_done", 4))
        act.dma_start(peer["keys"], a["peer_subkeys_2"].rearrange("s n d -> n s d")).then_inc(sem("keys_in"), 16)
        norm(4)
        norm_cols(3, vc("ffn_norm2", 0, 16), None)
        for t in range(NT):
            with act.Fori(0, 4) as i:
                act.wait_ge(*at("unit_used", i * SLOTS + SLOTS * (BLK["wq"] + 4 * t + 1)))
                act.copy(peer["q"][:, bass.ds(i * 4, 4), P * t:P * (t + 1)], ps[:, 0:4, 0:P]).then_inc(sem("wq_out"), 1)
            for b in range(4):
                act.wait_ge(*at("keys_scored", t * 4 + b + 1))
                act.copy(peer["score"][:, t, 4 * b:4 * b + 4, :], ps[:, 4 + b, :].rearrange("p (a b) -> p a b", b=P)).then_inc(sem("score_out"), 1)
        for t in range(NT):
            act.wait_ge(*at("best_shift", t + 1))
            best = peer["best"][:, HEADS * t:HEADS * (t + 1), :]
            act.activation(best, best, ACT.Exp).then_inc(sem("best_exp"), 1)
        for t in range(NT):
            act.wait_ge(*at("h_done", t + 1))
            act.activation(peer["h"][:, t, :], peer["h"][:, t, :], ACT.Gelu_apprx_tanh).then_inc(sem("h_gelu"), 1)
        act.wait_ge(*at("x_done", 5))
        norm(5, scaled=False)

    @block.tensor
    def _(pe):
        pe.wait_ge(*at("tab_in", 32))
        pe.wait_ge(*at("rows_in", 16 * len(VEC)))
        for j, n in enumerate(VROWS):
            ins = pe.transpose(ps[:, 7, P * j:P * j + n], vrows[0:n, j, :], ident[0:n, 0:n])
        ins.then_inc(sem("vec_T"), 1)

        pe.matmul(ps[0:32, 6, 0:384], rel[:], tb("bucket")[0:32, :], start=True, stop=True).then_inc(sem("bias_rows_ps"), 1)
        def mod_sums(n):
            pe.wait_ge(*at("mod_used", (4, 12)[n] * MOD_UNITS))
            bank = MOD_BANK[n]
            for j in range(32):
                ins = pe.matmul(ps[:, bank, j:j + 1], mod["acc"].rearrange("p a b -> p (a b)")[:, P * j:P * (j + 1)], ones[:, 0:1], start=True, stop=True)
            ins.then_inc(sem("mod_sum"), 1)

        pe.wait_ge(*at("vcols", 2))
        mod_sums(0)

        def norm_turn(n):
            pe.wait_ge(*at("xs_vec", n + 1))
            pe.wait_ge(*at("xs_act", n + 1))
            for g in range(8):
                if g >= 4:
                    pe.wait_ge(sem("hT_vec" if g % 2 else "hT_act"), n * 4 + (g - 4) // 2 + 1)
                for k in range(2):
                    for t in range(NT):
                        f = 2 * g + k
                        ins = pe.transpose(ps[:, g % 4, (NT * k + t) * P:(NT * k + t + 1) * P], xs[:, t, P * f:P * (f + 1)], ident)
                ins.then_inc(sem("hT_turned"), 1)
            pe.wait_ge(*at("hT_act", n * 4 + 4))
            pe.wait_ge(*at("hT_vec", n * 4 + 4))

        def project(lhs, blk, ev, n, tail, by_vec=True):
            def one(i, step, b, w):
                pe.wait_ge(*at("evac_act", i * step + (ev + b + 1)))
                if by_vec:
                    pe.wait_ge(*at("evac_vec", i * step + (ev + b + 1)))
                for s in range(SLOTS):
                    pe.wait_ge(sem(f"slot{s}"), i * (16 * step) + 16 * (blk + b + 1))
                    for k in range(KS):
                        for t in range(NT):
                            ins = pe.matmul(ps[:, 2 * (b % 2) + t, 0:w], lhs[:, KS * s + k, P * t:P * (t + 1)], ring[:, s, k, 0:w],
                                            start=(s == 0 and k == 0), stop=(s == SLOTS - 1 and k == KS - 1))
                    ins.then_inc(sem("unit_used"), 1)
            with pe.Fori(0, n // 2) as i:
                one(i, 2, 0, NB)
                one(i, 2, 1, NB)
            if n % 2:
                one(0, 0, n - 1, NB)
            if tail:
                one(0, 0, n, tail)

        norm_turn(0)
        project(hT, BLK["in1"], EVB["in1"], 11, W1 - 11 * NB, by_vec=False)
        def turn(g):
            col, w, tiles, _ = TURNS[g]
            if g >= 4:
                pe.wait_ge(*turn_taken(g - 4))
            for k in range(tiles):
                for t in range(NT):
                    ins = pe.transpose(ps[0:w, g % 4, (NT * k + t) * P:(NT * k + t + 1) * P],
                                       proj[:, t, col + w * k:col + w * (k + 1)], ident)
            ins.then_inc(sem("turned"), 1)

        pe.wait_ge(*at("evac_act", EVB["out1"] + 2))
        pe.wait_ge(*at("evac_vec", EVB["out1"] + 2))
        for g in range(FOX_T, GLA_T):
            turn(g)
        pe.wait_ge(*at("fox_lf", 1))
        lf = fox["z"][:, 0, :]
        pe.matmul(ps[:, 4, 0:8], tb("tri"), lf, start=True, stop=False, skip_group_check=True)
        pe.matmul(ps[:, 4, 4:8], ones, lf[:, 0:4], start=False, stop=True, skip_group_check=True).then_inc(sem("fox_cum"), 1)
        pe.wait_ge(*at("fox_cum_out", 1))
        for h in range(4):
            for t in range(NT):
                ins = pe.transpose(ps[:, 5 + h // 2, (NT * (h % 2) + t) * P:(NT * (h % 2) + t + 1) * P],
                                   fox["cum"][:, 0, 4 * t + h:4 * t + h + 1].to_broadcast([P, P]), ident)
        ins.then_inc(sem("fox_rows"), 1)
        for g in range(FOX_T, POOL_T):
            pe.wait_ge(*turn_taken(g))
        for h in range(4):
            bank = (4, 7)[h % 2]
            if h >= 2:
                pe.wait_ge(*at("fox_logit", h - 1))
            pe.matmul(ps[:, bank, 0:P], fox["q"][:, h, 0:P], fox["k"][:, h, 0:P], start=True, stop=True)
            pe.matmul(ps[:, bank, P:3 * P], fox["q"][:, h, P:T], fox["k"][:, h, :], start=True, stop=True).then_inc(sem("fox_score"), 1)
        mod_sums(1)

        def fox_values(h):
            bank = (4, 7)[h % 2]
            pe.wait_ge(*at("fox_pT_out", h + 1))
            if h >= 2:
                pe.wait_ge(*at("fox_out", h - 1))
            v = [proj[:, t, FOX_V + P * h:FOX_V + P * (h + 1)] for t in range(NT)]
            pT = fox["pT"][:, h, :]
            pe.matmul(ps[:, bank, 0:P], v[0], pT[:, 0:P], start=True, stop=True)
            pe.matmul(ps[:, bank, P:T], v[0], pT[:, P:2 * P], start=True, stop=False)
            pe.matmul(ps[:, bank, P:T], v[1], pT[:, 2 * P:3 * P], start=False, stop=True).then_inc(sem("fox_o"), 1)

        pe.wait_ge(*at("fox_p", 2))
        for h in range(4):
            if h >= 2:
                pe.wait_ge(*at("fox_pT_out", h - 1))
            for j in range(3):
                ins = pe.transpose(ps[:, 5 + h % 2, P * j:P * (j + 1)], fox["logit"][:, h, P * j:P * (j + 1)], ident)
            ins.then_inc(sem("fox_pT"), 1)
            if h >= 1:
                fox_values(h - 1)
        fox_values(3)
        pe.wait_ge(*at("pool_delta", 4))
        pe.wait_ge(*at("mixer_w_in", 32))
        pe.wait_ge(*at("fox_pT_out", 4))
        for g in range(4):
            src = (pool["w"], pool["w2"])[g % 2]
            ins = pe.matmul(ps[:, 5 + g // 2, T * (g % 2):T * (g % 2 + 1)], pool["pw"][:, g, :], src[:, g, 16:T + 16], start=True, stop=True)
        ins.then_inc(sem("pool_y"), 1)
        pe.wait_ge(*at("mod_cols", 2))
        for g in range(GLA_T, GDN_T):
            turn(g)
        pe.wait_ge(*turn_taken(GLA_T + 4))
        pe.wait_ge(*at("mixer_w_in", 32))
        pe.wait_ge(*at("fox_out", 4))
        for g in range(2):
            ins = pe.matmul(ps[:, 4, T * g:T * (g + 1)], w_lr[:, P * g:P * (g + 1)], gla["lr"][0:16, 0, :], start=True, stop=True)
        ins.then_inc(sem("gla_z"), 1)
        pe.wait_ge(*at("gla_ke", 1))
        pe.wait_ge(*at("pool_out", 4))
        for c in range(4):
            for g in range(2):
                ins = pe.transpose(ps[0:CH, 5 + c // 2, P * (2 * (c % 2) + g):P * (2 * (c % 2) + g + 1)], gla["ke"][:, g, CH * c:CH * (c + 1)], ident)
            if c % 2:
                ins.then_inc(sem("ke_turned"), 1)
        pe.wait_ge(*at("gla_z_out", 1))
        pe.wait_ge(*at("ke_tok", 2))
        for n in range(16):
            g, sblk = n // 8, n % 8
            t0 = 8 * sblk
            d = pair_buf(n).rearrange("p (c s t) -> p c s t", c=4, s=8)
            dst = ps[:, 4 + g, 0:T].rearrange("p (c t) -> p c t", c=4)[:, :, t0:CH]
            pe.wait_ge(*at("pair_q", n + 1))
            for s in range(8):
                key = 8 * sblk + s
                ins = pe.matmul(dst, tb("pick")[:, CH - 1 - key:CH - 1 - key + P], d[:, :, s, :],
                                start=(key == 0), stop=(key == CH - 1), skip_group_check=True)
            ins.then_inc(sem("pair_used"), 1)
            if n % 3 == 1 and n < 12:
                if n // 3:
                    pe.wait_ge(*at("gate_out", n // 3))
                for j in range(2):
                    ins = pe.matmul(ps[:, 6 + j, :], ones, gate_pairs[:, n // 3, j], start=True, stop=True)
                ins.then_inc(sem("gate_sum"), 1)
        pe.wait_ge(*at("gate_out", 4))
        pe.wait_ge(*at("gla_att", 2))
        pe.wait_ge(*at("gla_v_in", 16 * 8))
        pe.wait_ge(*at("fox_out", 4))
        for c in range(4):
            for h in range(4):
                g, r = h // 2, slice(CH * (h % 2), CH * (h % 2) + CH)
                dst = ps[:, 6 + h % 2, T * g + CH * c:T * g + CH * (c + 1)]
                ins = pe.matmul(dst, gla["v"][r, c, P * h:P * (h + 1)], gla["att"][r, g, CH * c:CH * (c + 1)],
                                start=True, stop=(c == 0), skip_group_check=True)
                if c > 0:
                    if h == 0:
                        pe.wait_ge(*at("gla_state", c))
                    ins = pe.matmul(dst, gla["state"][r, g, :], gla["qe"][r, g, CH * c:CH * (c + 1)],
                                    start=False, stop=True, skip_group_check=True)
            if c < 3:
                for g in range(2):
                    ins2 = pe.matmul(ps[:, 4, T * g:T * (g + 1)], gla["ke_tok"][0:CH, 2 * c + g, :], gla["v"][0:CH, c, T * g:T * (g + 1)],
                                     start=True, stop=True)
                ins2.then_inc(sem("gla_dstate"), 1)
        ins.then_inc(sem("mix_o"), 1)

        def head_norm(m, sq):
            pe.wait_ge(*at("o_sq", 2 * m + 2))
            for j in range(2):
                ins = pe.matmul(ps[:, 4 + j, :], ones, sq[:, NB * j:NB * (j + 1)], start=True, stop=True)
            ins.then_inc(sem("o_sum"), 1)

        head_norm(0, gla["pair"].rearrange("p a b -> p (a b)")[:, 0:1024])
        for g in range(GDN_T, len(TURNS)):
            turn(g)
        gsm = lambda name: gdn[name][:, 0, :]
        tok = lambda n: slice(P * (n // 4), P * (n // 4 + 1))
        pe.wait_ge(*at("qk_sq", 1))
        pe.wait_ge(*at("mix_out", 2))
        for j in range(4):
            ins = pe.matmul(ps[:, 4 + j, :], ones, gdn["sq"][:, 2 * j:2 * j + 2, :], start=True, stop=True)
        ins.then_inc(sem("qk_sum"), 1)
        pe.wait_ge(*at("gdn_g", 1))
        for g in (len(TURNS) - 4, len(TURNS) - 3, len(TURNS) - 2, len(TURNS) - 1):
            pe.wait_ge(*turn_taken(g))
        pe.matmul(ps[:, 0, 0:8], tb("tri_chunk"), gsm("g"), start=True, stop=True).then_inc(sem("gdn_cum"), 1)
        pe.wait_ge(*at("gdn_cum_out", 1))
        pe.wait_ge(*at("gdn_beta", 1))
        pe.wait_ge(*at("qk_eps", 1))
        for i, name in enumerate(("cum", "beta")):
            for n in range(8):
                ins = pe.transpose(ps[:, 2 + 2 * i + n // 4, P * (n % 4):P * (n % 4 + 1)], gsm(name)[:, n:n + 1].to_broadcast([P, P]), ident)
        ins.then_inc(sem("gdn_rows"), 1)
        pe.wait_ge(*at("kb_out", 2))
        pe.wait_ge(*at("qk_norm", 2))
        pe.wait_ge(*at("gdn_rows_out", 1))
        for n in range(8):
            h, t = n % 4, tok(n)
            pe.matmul(ps[:, 4 + n // 4, P * h:P * (h + 1)], gdn["conv"][:, 4 + h, t], gdn["kb"][:, h, t], start=True, stop=True)
            ins = pe.matmul(ps[:, 6 + n // 4, P * h:P * (h + 1)], gdn["conv"][:, 4 + h, t], gdn["conv"][:, h, t], start=True, stop=True)
        ins.then_inc(sem("gdn_kk"), 1)
        for n in range(8):
            ins = pe.transpose(ps[:, n // 4, P * (n % 4):P * (n % 4 + 1)], gdn["conv"][:, 4 + n % 4, tok(n)], ident)
        ins.then_inc(sem("k_turned"), 1)
        for n in range(8):
            ins = pe.transpose(ps[:, 2 + n // 4, P * (n % 4):P * (n % 4 + 1)], gdn["conv"][:, 8 + n % 4, tok(n)], ident)
        ins.then_inc(sem("v_turned"), 1)
        pe.wait_ge(*at("invT_out", 1))
        for n in range(8):
            ins = pe.transpose(ps[:, 4 + n // 4, P * (n % 4):P * (n % 4 + 1)], gdn["invT"][:, n, :], ident)
        ins.then_inc(sem("inv_turned"), 1)
        for lv in range(1, len(LEVELS)):
            last = lv == len(LEVELS) - 1
            pe.wait_ge(*at("inv_off", lv))
            if lv == 1:
                pe.wait_ge(*at("inv_out", 1))
                pe.wait_ge(*at("k_scaled", 1))
                pe.wait_ge(*at("v_scaled", 1))
                pe.wait_ge(*at("attn_out", 1))
            else:
                pe.wait_ge(*at("inv_new", lv - 1))
                pe.wait_ge(*at("invT_out", lv))
            for n in range(8):
                ins = pe.matmul(ps[:, 4 + n // 4, P * (n % 4):P * (n % 4 + 1)], gdn["off"][:, n, :], gdn["inv"][:, n, :], start=True, stop=True)
            ins.then_inc(sem("inv_x"), 1)
            pe.wait_ge(*at("inv_x_out", lv))
            for n in range(8):
                ins = pe.matmul(ps[:, n // 4, P * (n % 4):P * (n % 4 + 1)], gdn["X"][:, n, :], gdn["invT"][:, n, :], start=True, stop=True)
            ins.then_inc(sem("invT_delta"), 1)
            if not last:
                for n in range(8):
                    ins = pe.matmul(ps[:, 6 + n // 4, P * (n % 4):P * (n % 4 + 1)], gdn["invT"][:, n, :], gdn["X"][:, n, :], start=True, stop=True)
                ins.then_inc(sem("inv_delta"), 1)
        pe.wait_ge(*at("invT_out", len(LEVELS)))
        for n in range(8):
            dst = slice(P * (n % 4), P * (n % 4 + 1))
            pe.matmul(ps[:, 4 + n // 4, dst], gdn["invT"][:, n, :], gdn["v_b"][:, n, :], start=True, stop=True)
            ins = pe.matmul(ps[:, 6 + n // 4, dst], gdn["k_w"][:, n, :], gdn["invT"][:, n, :], start=True, stop=True)
        ins.then_inc(sem("gdn_w"), 1)
        pe.wait_ge(*at("gdn_u_out", 1))
        pe.wait_ge(*at("gdn_w_out", 1))
        pe.wait_ge(*at("q_decayed", 2))
        for c in range(4):
            t, c2 = c // 2, c % 2
            if c > 0:
                pe.wait_ge(*at("gdn_state", c))
                for h in range(4):
                    ins = pe.matmul(ps[:, 4, P * h:P * (h + 1)], gdn["wT"][:, 4 * t + h, :], gdn["state"][:, h, :], start=True, stop=True)
                ins.then_inc(sem("gdn_ws"), 1)
                pe.wait_ge(*at("gdn_new", c))
            new = gdn["u"] if c == 0 else gdn["new"]
            if c < 3:
                for h in range(4):
                    ins = pe.matmul(ps[:, 5, P * h:P * (h + 1)], gdn["k_end"][:, c2, 4 * t + h, :], new[:, h, :], start=True, stop=True)
                ins.then_inc(sem("gdn_dstate"), 1)
            for h in range(4):
                dst = ps[:, 6 + h % 2, T * (h // 2) + CH * c:T * (h // 2) + CH * (c + 1)]
                ins = pe.matmul(dst, new[:, h, :], gdn["attnT"][:, 4 * t + h, CH * c2:CH * (c2 + 1)], start=True, stop=(c == 0), skip_group_check=True)
                if c > 0:
                    ins = pe.matmul(dst, gdn["state"][:, h, :], gdn["conv"][:, h, CH * c:CH * (c + 1)], start=False, stop=True, skip_group_check=True)
            if c < 3:
                ins.then_inc(sem("gdn_o"), 1)
        ins.then_inc(sem("mix_o"), 1)
        head_norm(1, gdn["sq"].rearrange("p a b -> p (a b)")[:, 0:1024])
        pe.wait_ge(*at("mix_out", 4))
        project(yT, BLK["out1"], EVB["out1"], 4, 0)
        norm_turn(1)
        pe.wait_ge(*at("ffn_credit", 1))
        with pe.Fori(0, 11) as i:
            for m, free in enumerate(("gate_free", "up_free")):
                pe.wait_ge(sem(free), i + 1)
                for s in range(SLOTS):
                    pe.wait_ge(sem(f"slot{s}"), i * 32 + 16 * (BLK["up"] + m + 1))
                    for k in range(KS):
                        for f in range(4):
                            ins = pe.matmul(ps[:, 4 * m + f, 0:T], ring[:, s, k, P * f:P * (f + 1)], hT[:, KS * s + k, :],
                                            start=(s == 0 and k == 0), stop=(s == SLOTS - 1 and k == KS - 1))
                    ins.then_inc(sem("unit_used"), 1)
        pe.wait_ge(*at("gate_free", 12))
        pe.wait_ge(*at("up_free", 12))

        def down_group(i, j, par, start, stop):
            pe.wait_ge(*at("staged", i + (j + 1)))
            for s in range(SLOTS):
                pe.wait_ge(sem(f"slot{s}"), i * 16 + 16 * (BLK["down"] + j + 1))
                for t in range(NT):
                    for n in range(4):
                        ins = pe.matmul(ps[:, 2 * n + t, :], ffn["act"][:, par, s, P * t:P * (t + 1)], ring[:, s, n, :],
                                        start=(start and s == 0), stop=(stop and s == SLOTS - 1))
                ins.then_inc(sem("unit_used"), 1)

        down_group(0, 0, 0, True, False)
        with pe.Fori(1, DOWN - 2, 2) as i:
            down_group(i, 0, 1, False, False)
            down_group(i, 1, 0, False, False)
        down_group(0, DOWN - 2, 1, False, False)
        down_group(0, DOWN - 1, 0, False, True)
        pe.wait_ge(*at("x_done", 2))
        norm_turn(2)
        project(hT, BLK["in2"], EVB["in2"], 6, W2 - 6 * NB)
        pe.wait_ge(*at("evac_act", EVB["out2"] + 2))
        pe.wait_ge(*at("evac_vec", EVB["out2"] + 2))

        pe.wait_ge(*at("kv_twice", 1))
        for i, bank in enumerate((0, 1, 4, 5, 6)):
            for g in range(2):
                for t in range(NT):
                    ins = pe.transpose(ps[:, bank, T * g + P * t:T * g + P * (t + 1)], kv_twice[:, 4 * i + 2 * t + g, :], ident)
            ins.then_inc(sem("kv_turned"), 1)
        pe.wait_ge(*at("cmp_w_in", 16 * 6))
        for m in range(2):
            pe.wait_ge(*at("xk", 2 * m + 2))
            for j in range(16):
                pe.matmul(ps[:, 2 + m, 0:30], hyb["w1"][:, m, j, :], hyb["xk"][:, 2 * m:2 * m + 2, 2 * j:2 * j + 225:16], start=(j == 0), stop=(j == 15))
            for j in range(16):
                ins = pe.matmul(ps[:, 7, m:m + 1], hyb["w1"][:, m, j, :], vc(("pos_k", "pos_v")[m], j), start=(j == 0), stop=(j == 15), skip_group_check=True)
            ins.then_inc(sem("cmp_hid"), 1)
            pe.wait_ge(*at("cmp_hb", m + 1))
        pe.wait_ge(*at("cmp_gelu", 2))
        pe.matmul(ps[:, 0, 0:30], hst["w2"][:, 0, :], hyb["hid"][:, 0, :], start=True, stop=True)
        for g in range(2):
            ins = pe.matmul(ps[0:NCMP, 1, DK * g:DK * (g + 1)], hyb["hid"][:, 1, NCMP * g:NCMP * (g + 1)], hst["w2"][:, 1, 0:DK], start=True, stop=True)
        ins.then_inc(sem("cmp_kv"), 1)
        pe.wait_ge(*at("kv_out", 1))
        pe.wait_ge(*at("bias_in", 16))

        def score(i, g, u):
            t, br = UNITS[u % NU]
            pe.wait_ge(*at("att_exp", i * NU + (4 * NU * g + max(u - 3, 0) + 1)))
            if u % NU == 0:
                pe.wait_ge(*at("q_out", i + (4 * g + u // NU + 1)))
            off = P * (1 - t)
            for h in range(2):
                head = bass.ds(i * 2 + (2 * (u // NU) + 8 * g + h + (16 if br == "ban" else 0)), 1)
                if br == "cmp":
                    n = (7, 15)[t]
                    keys, cols = hyb["kc"][:, g, 0:n], slice(off + 31, T, 16)
                else:
                    n = P * (t + 1)
                    keys, cols = hyb["kT"][:, 2 * ("slc", "win", "ban").index(br) + g, 0:n], slice(off, off + n)
                dst = ps[:, u % 4, T * h:T * h + n]
                pe.matmul(dst, hyb["q"][:, int(br == "ban"), h, P * t:P * (t + 1)], keys, start=True, stop=False)
                ins = pe.matmul(dst, tb("anti"), hyb["bias"][:, head, cols], start=False, stop=True)
            ins.then_inc(sem("att_score"), 1)

        def turn_p(i, g, u):
            t, br = UNITS[u % NU]
            pe.wait_ge(*at("att_p", i * NU + (4 * NU * g + u + 1)))
            pe.wait_ge(*at("att_pT", i * NU + (4 * NU * g + max(u - 1, 0) + 1)))
            for h in range(2):
                for k in range(1 if br == "cmp" else t + 1):
                    n = (7, 15)[t] if br == "cmp" else P
                    q = h if br == "cmp" else (t + 1) * h + k
                    ins = pe.transpose(ps[0:n, 4 + u % 2, P * q:P * (q + 1)], hyb["p"][:, u % 2, h, P * k:P * k + n], ident)
            ins.then_inc(sem("att_turned"), 1)

        def values(i, g, u):
            t, br = UNITS[u % NU]
            pe.wait_ge(*at("att_pT", i * NU + (4 * NU * g + u + 2)))
            if u == 0:
                pe.wait_ge(*at("att_out", i * 2 + (8 * g + 1)))
            dst = ps[:, 7 if br == "ban" else 6, P * t:P * (t + 1)]
            for h in range(2):
                cols = slice(DK * (1 - h), DK * (1 - h) + P)
                for k in range(1 if br == "cmp" else t + 1):
                    first = br in ("slc", "ban") and h == 0 and k == 0
                    if br == "cmp":
                        n = (7, 15)[t]
                        v, w = hyb["v_cmp"][0:n, g, cols], hyb["pT"][0:n, u % 2, h, :]
                    else:
                        v, w = hyb["v"][:, ("slc", "win", "ban").index(br), 2 * k + g, cols], hyb["pT"][:, u % 2, (t + 1) * h + k, :]
                    ins = pe.matmul(dst, v, w, start=first, stop=(br in ("cmp", "ban") and h == 1 and (br == "cmp" or k == t)))
            ins.then_inc(sem("att_pv"), 1)

        def turn_q(i, g):
            pe.wait_ge(*at("q_in", i + (4 * g + 1)))
            for k in range(2):
                for t in range(NT):
                    ins = pe.transpose(ps[:, 0, T * k + P * t:T * k + P * (t + 1)], hyb["q_in"][:, k, t, :], ident)
            ins.then_inc(sem("q_turned"), 1)

        def head_pair(i, g, more):
            for u in range(NU):
                turn_p(i, g, u)
                if u + 3 < NU or more:
                    score(i, g, u + 3)
                if u == 4 and more:
                    turn_q(i + 1, g)
                if u:
                    values(i, g, u - 1)
            values(i, g, NU - 1)

        for g in range(2):
            turn_q(0, g)
            for u in range(3):
                score(0, g, u)
            with pe.Fori(0, 3) as i:
                head_pair(i, g, True)
            head_pair(3, g, False)
        pe.wait_ge(*at("att_out", 17))
        project(yT, BLK["out2"], EVB["out2"], 4, 0)
        pe.wait_ge(*at("x_done", 4))
        norm_turn(3)
        pe.wait_ge(*at("keys_in", 16))
        for s in range(2):
            ins = pe.transpose(ps[:, 4, P * s:P * (s + 1)], peer["keys"][:, s, :], ident)
        ins.then_inc(sem("keys_turned"), 1)
        for t in range(NT):
            with pe.Fori(0, 4) as i:
                pe.wait_ge(*at("wq_out", i + (4 * t + 1)))
                for s in range(SLOTS):
                    pe.wait_ge(sem(f"slot{s}"), i * 16 + 16 * (BLK["wq"] + 4 * t + 1))
                    for k in range(KS):
                        for f in range(4):
                            ins = pe.matmul(ps[:, f, 0:P], ring[:, s, k, P * f:P * (f + 1)], hT[:, KS * s + k, P * t:P * (t + 1)],
                                            start=(s == 0 and k == 0), stop=(s == SLOTS - 1 and k == KS - 1))
                    ins.then_inc(sem("unit_used"), 1)
            pe.wait_ge(*at("wq_out", 4 * t + 5))
            if t == 0:
                pe.wait_ge(*at("keys_out", 1))
            else:
                pe.wait_ge(*at("score_out", 4))
            for c in range(SIDES):
                ins = pe.matmul(ps[:, 4 + c // 4, P * (c % 4):P * (c % 4 + 1)], peer["q"][:, c, P * t:P * (t + 1)], peer["keysT"][:, c % 2, :],
                                start=True, stop=True)
                if c % 4 == 3:
                    ins.then_inc(sem("keys_scored"), 1)

    @block.vector
    def _(vec):
        link = Chain(vec, at, "vec_chain")
        vec.memset(stat[:, 14:15], 0.0).then_inc(sem("evac_vec"), 2 + EVB["out1"])
        vec.memset(stat[:, 15:16], 0.0).then_inc(sem("evac_act"), 2)

        def norm(n, scaled=True):
            vec.wait_ge(*at("squares", 2 * n + 2))
            vec.tensor_scalar(stat[:, 2:4], stat[:, 0:2], 1.0 / D, EPS, ALU.mult, ALU.add).then_inc(sem("mean_sq"), 1)
            vec.wait_ge(*at("root", n + 1))
            vec.reciprocal(stat[:, 6:8], stat[:, 4:6]).then_inc(sem("rstd"), 1)
            vec.wait_ge(*at("rstd", n + 1))
            if scaled:
                vec.tensor_scalar(xs[:, 0], x[:, 0], stat[:, 6:7], None, ALU.mult).then_inc(sem("xs_vec"), 1)

        def norm_cols(n, scale, shift):
            for g in range(1, 8, 2):
                vec.wait_ge(*at("hT_turned", n * 8 + g + 1))
                for k in range(2):
                    f = 2 * g + k
                    bank = ps[:, g % 4, T * k:T * (k + 1)]
                    if shift is not None:
                        ins = vec.tensor_scalar(hT[:, f, :], bank, scale[:, f:f + 1], shift[:, f:f + 1], ALU.mult, ALU.add)
                    else:
                        ins = vec.tensor_scalar(hT[:, f, :], bank, scale[:, f:f + 1], None, ALU.mult)
                ins.then_inc(sem("hT_vec"), 1)

        def evac(blk, n, dst, tail):
            def one(turn, cols, b, w):
                vec.wait_ge(*at("unit_used", turn + SLOTS * (blk + b + 1)))
                vec.tensor_copy(dst[:, 1, cols], ps[:, 2 * (b % 2) + 1, 0:w]).then_inc(sem("evac_vec"), 1)
            with vec.Fori(0, n // 2) as i:
                for b in range(2):
                    one(i * (2 * SLOTS), bass.ds(i * (2 * NB) + b * NB, NB), b, NB)
            if n % 2:
                one(0, slice((n - 1) * NB, n * NB), n - 1, NB)
            if tail:
                one(0, slice(n * NB, n * NB + tail), n, tail)

        acc = mod["acc"].rearrange("p a b -> p (a b)")
        flat_gates = gates[:].rearrange("p g n -> p (g n)")
        vec.wait_ge(*at("cond", 1))

        def mod_blocks(first, n, dst, off, fresh):
            with vec.Fori(0, n) as i:
                link.begin(i, vec_chain=MOD_UNITS, mod_used=MOD_UNITS)
                to = dst[:, bass.ds(i * MB + off, MB)]
                for j in range(MOD_UNITS):
                    vec.wait_ge(*at(f"mod_slot{j % 4}", i * 32 + 16 * (2 * first + j // 4 + 1)))
                    for r in range(2):
                        w, c = mod["ring"][:, j % 4, r], c_col[:, 2 * j + r:2 * j + r + 1]
                        if fresh and j == r == 0:
                            ins = vec.tensor_scalar(to, w, c, None, ALU.mult)
                        else:
                            ins = vec.scalar_tensor_tensor(out=to, in0=w, scalar=c, in1=to, op0=ALU.mult, op1=ALU.add)
                        link(ins, "mod_used" if r else None)
            link.end(n)

        def mod_finish(n, bias, weight):
            vec.wait_ge(*at("mod_sum", n + 1))
            link(vec.tensor_tensor(mod_col[:, 32 * n:32 * n + 32], ps[:, MOD_BANK[n], 0:32], bias, ALU.add))
            scale = mod_col[:, 32 * n + 16:32 * n + 32]
            link(vec.scalar_tensor_tensor(out=scale, in0=scale, scalar=1.0, in1=weight, op0=ALU.add, op1=ALU.mult), "mod_cols")

        mod_blocks(0, 2, acc, 0, True)
        vec.wait_ge(*at("bias_rows_ps", 1))
        link(vec.tensor_tensor(bias_rows, ps[0:32, 6, 0:384], tb("bias_neg")[0:32, :], ALU.add), "bias_rows")
        norm(0)
        mod_blocks(2, 2, acc, 2 * MB, True)
        vec.wait_ge(*at("vcols", 2))
        mod_finish(0, vc("b_mod1", 0, 32), vc("norm_mix", 0, 16))
        norm_cols(0, mod_col[:, 16:32], mod_col[:, 0:16])
        vec.wait_ge(*at("gate_bias_in", 32))
        mod_blocks(4, 2, flat_gates, 0, False)
        mod_blocks(6, 4, acc, 0, True)
        mod_blocks(10, 2, flat_gates, D, False)
        vec.wait_ge(*at("small_in", 64))
        vec.wait_ge(*at("evac_act", EVB["out1"] + 2))

        def taken(g):
            vec.wait_ge(*at("turned", g + 1))
            return ps[:, g % 4, :]

        vec_turn = lambda ins, wait=False: link(ins, "turn_vec", wait)
        z2 = fox["z"][:, 0, :].rearrange("p (t h) -> p t h", t=NT)
        link(vec.tensor_tensor(z2, proj[:, :, FOX_F:FOX_F + 4], small[:, 0:4].unsqueeze(1).to_broadcast([P, NT, 4]), ALU.add))
        link(vec.scalar_tensor_tensor(out=fox["e"], in0=fox["z"], scalar=-1.0, in1=fox["z"], op0=ALU.mult, op1=ALU.max), "abs_z")
        for j in range(2):
            vec_turn(vec.tensor_copy(fox["k"][:, 2 * j:2 * j + 2, :], taken(FOX_T + 2 + j).rearrange("p (h t) -> p h t", h=2)))
        vec.wait_ge(*at("pool_zero", 3))
        for j in range(2):
            vec_turn(vec.tensor_copy(pool["u"][:, 2 * j:2 * j + 2, 16:T + 16], taken(POOL_T + j).rearrange("p (h t) -> p h t", h=2)))
        vec.wait_ge(*at("ln_z", 1))
        link(vec.scalar_tensor_tensor(out=fox["z"], in0=fox["z"], scalar=0.0, in1=fox["l"], op0=ALU.min, op1=ALU.subtract), "fox_lf")
        vec.wait_ge(*at("fox_cum", 1))
        link(vec.tensor_copy(fox["cum"][:, 0, :], ps[:, 4, 0:8]), "fox_cum_out")
        vec.wait_ge(*at("fox_rows", 1))
        neg2 = tb("neg_tri").unsqueeze(1).to_broadcast([P, 2, P])
        for b in range(2):
            rows = ps[:, 5 + b, :].rearrange("p (h t k) -> p h t k", h=2, t=2)
            hh = slice(2 * b, 2 * b + 2)
            vec.tensor_tensor(fox["decay"][:, hh, 0:P], rows[:, :, 0, :], neg2, ALU.add)
            vec.tensor_copy(fox["decay"][:, hh, P:2 * P], rows[:, :, 0, :])
            link(vec.tensor_tensor(fox["decay"][:, hh, 2 * P:3 * P], rows[:, :, 1, :], neg2, ALU.add))
        for h in range(4):
            bank = (4, 7)[h % 2]
            vec.wait_ge(*at("fox_score", h + 1))
            for t in range(NT):
                r = slice((0, P)[t], (P, 3 * P)[t])
                ins = vec.scalar_tensor_tensor(out=fox["logit"][:, h, r], in0=ps[:, bank, r], scalar=fox["cum"][:, 0, 4 * t + h:4 * t + h + 1],
                                               in1=fox["decay"][:, h, r], op0=ALU.add, op1=ALU.subtract)
            link(ins, "fox_logit")
        fm = fox["max"][:, 0, :]
        vec.tensor_reduce(fm[:, 0:4], fox["logit"][:, :, 0:P], X_AXIS, ALU.max)
        link(vec.tensor_reduce(fm[:, 4:8], fox["logit"][:, :, P:3 * P], X_AXIS, ALU.max))
        link(vec.tensor_scalar(fm, fm, -1.0, None, ALU.mult), "fox_max")
        mod_finish(1, vc("b_mod2", 0, 32), vc("norm_ffn", 0, 16))
        vec.wait_ge(*at("fox_exp", 8))
        link(vec.reciprocal(fox["rec"], fox["sum"]))
        for t in range(NT):
            r = slice((0, P)[t], (P, 3 * P)[t])
            rec = fox["rec"][:, 0, 4 * t:4 * t + 4].unsqueeze(2).to_broadcast([P, 4, P * (t + 1)])
            link(vec.tensor_tensor(fox["logit"][:, :, r], fox["logit"][:, :, r], rec, ALU.mult), "fox_p")
        for h in range(4):
            vec.wait_ge(*at("fox_o", h + 1))
            link(vec.tensor_copy(yT[:, 12 + h, :], ps[:, (4, 7)[h % 2], 0:T]), "fox_out")
        gv = lambda name: gla[name].rearrange("p a b -> p (a b)")
        vec.wait_ge(*at("fox_pT_out", 4))
        vec_turn(vec.tensor_copy(gla["k"], taken(GLA_T + 1).rearrange("p (h t) -> p h t", h=2)))
        vec_turn(vec.tensor_copy(gla["lr"][0:16, 0, :], taken(GLA_T + 4)[0:16, 0:T]), True)
        vec.wait_ge(*at("gla_z", 1))
        for g in range(2):
            ins = vec.tensor_scalar(gla["z"][:, g, :], ps[:, 4, T * g:T * (g + 1)], vc("gla_b", g), None, ALU.add)
        link(ins, "gla_z_out")
        link(vec.scalar_tensor_tensor(out=gla["e"], in0=gla["z"], scalar=-1.0, in1=gla["z"], op0=ALU.mult, op1=ALU.max), "abs_z")
        vec.wait_ge(*at("ln_z", 2))
        link(vec.scalar_tensor_tensor(out=gla["z"], in0=gla["z"], scalar=0.0, in1=gla["e"], op0=ALU.min, op1=ALU.subtract))
        for g in range(2):
            ins = vec.tensor_tensor_scan(gla["b"][:, g, :], tb("scan_reset"), gla["z"][:, g, :], 0.0, ALU.mult, ALU.add)
        link(ins)
        link(vec.tensor_scalar(gla["b"], gla["b"], 1.0 / 16.0, None, ALU.mult), "gla_b")
        bc = gv("b").rearrange("p (n t) -> p n t", t=CH)
        link(vec.tensor_tensor(gv("e").rearrange("p (n t) -> p n t", t=CH), bc[:, :, CH - 1:CH].to_broadcast([P, 8, CH]), bc, ALU.subtract), "gla_kd")
        vec.wait_ge(*at("gla_eb", 1))
        vec.wait_ge(turn_taken(GLA_T)[0], turn_taken(GLA_T)[1])
        link(vec.tensor_tensor(gla["qe"], gla["q"], gla["z"], ALU.mult))
        vec.wait_ge(*at("gla_ekd", 1))
        link(vec.tensor_tensor(gla["ke"], gla["k"], gla["e"], ALU.mult), "gla_ke")

        def pair(n):
            g, t0 = n // 8, 8 * (n % 8)
            d = pair_buf(n).rearrange("p (c s t) -> p c s t", c=4, s=8)
            chunks = lambda v: gla[v][:, g, :].rearrange("p (c t) -> p c t", c=4)
            shape = [P, 4, 8, CH - t0]
            return d, chunks("b")[:, :, t0:CH].unsqueeze(2).to_broadcast(shape), \
                chunks("b")[:, :, t0:t0 + 8].unsqueeze(3).to_broadcast(shape), chunks("k")[:, :, t0:t0 + 8].unsqueeze(3).to_broadcast(shape)

        def pair_diff(n):
            d, bt, bs, _ = pair(n)
            if n >= 3:
                vec.wait_ge(*at("pair_used", n - 2))
            link(vec.tensor_tensor(d, bt, bs, ALU.subtract))
            near = d[:, :, :, 0:8]
            vec.tensor_scalar(near, near, 0.0, None, ALU.min).then_inc(sem("pair_diff"), 1)

        vec.wait_ge(*at("pool_out", 4))
        pair_diff(0)
        pair_diff(1)
        for n in range(16):
            d, _, _, kb = pair(n)
            vec.wait_ge(*at("pair_exp", n + 1))
            vec.tensor_tensor(d, d, kb, ALU.mult).then_inc(sem("pair_k"), 1)
            if n < 14:
                pair_diff(n + 2)
        mask = tb("gla_mask").unsqueeze(1).to_broadcast([P, 4, CH])
        vec.wait_ge(*at("pair_used", 16))
        for g in range(2):
            link(vec.tensor_tensor(gla["att"][:, g, :].rearrange("p (c t) -> p c t", c=4), ps[:, 4 + g, 0:T].rearrange("p (c t) -> p c t", c=4), mask, ALU.mult), "gla_att")
        for c in range(3):
            vec.wait_ge(*at("gla_dstate", c + 1))
            for h in range(4):
                g, r = h // 2, slice(CH * (h % 2), CH * (h % 2) + CH)
                st, ds = gla["state"][r, g, :], ps[r, 4, T * g + P * (h % 2):T * g + P * (h % 2 + 1)]
                if c == 0:
                    ins = vec.tensor_copy(st, ds)
                else:
                    last = CH * c + CH - 1
                    ins = vec.scalar_tensor_tensor(out=st, in0=st, scalar=gla["z"][r, g, last:last + 1], in1=ds, op0=ALU.mult, op1=ALU.add)
            link(ins, "gla_state")

        def head_norm(m, sq, gate, norm, y0):
            vec.wait_ge(*at("o_sum", m + 1))
            for j in range(2):
                ins = vec.tensor_scalar(sq[:, NB * j:NB * (j + 1)], ps[:, 4 + j, :], 1.0 / HD, EPS, ALU.mult, ALU.add)
            link(ins, "o_mean")
            vec.wait_ge(*at("o_root", m + 1))
            link(vec.reciprocal(sq, sq))
            for j in range(2):
                y, two = yT[:, y0 + j:y0 + j + 3:2, :], lambda v: v.rearrange("p (h t) -> p h t", h=2)
                link(vec.scalar_tensor_tensor(out=y, in0=two(ps[:, 6 + j, :]), scalar=vc(norm), in1=two(sq[:, NB * j:NB * (j + 1)]), op0=ALU.mult, op1=ALU.mult))
                link(vec.tensor_tensor(y, y, gate[:, j:j + 3:2, :], ALU.mult), "mix_out")

        vec.wait_ge(turn_taken(GLA_T + 3)[0], turn_taken(GLA_T + 3)[1])
        head_norm(0, gla["pair"].rearrange("p a b -> p (a b)")[:, 0:1024], gla["gate"], "gla_norm", 0)
        gsm = lambda name: gdn[name][:, 0, :]
        flat = lambda name: gdn[name].rearrange("p n c -> p (n c)")
        by_tile = lambda v: v.rearrange("p (t h) -> p t h", t=NT)
        link(vec.memset(gdn["in"][:, :, 0:4], 0.0))
        link(vec.memset(gdn["fac"], 0.0))
        link(vec.tensor_tensor(by_tile(gsm("z")), proj[:, :, GDN_A:GDN_A + 4], small[:, 4:8].unsqueeze(1).to_broadcast([P, NT, 4]), ALU.add))
        link(vec.scalar_tensor_tensor(out=gdn["e"], in0=gdn["z"], scalar=-1.0, in1=gdn["z"], op0=ALU.mult, op1=ALU.max), "abs_z")
        for j in range(6):
            vec_turn(vec.tensor_copy(gdn["in"][:, 2 * j:2 * j + 2, 4:T + 4], taken(GDN_T + j).rearrange("p (h t) -> p h t", h=2)), j == 5)
        vec.wait_ge(*at("ln_z", 3))
        link(vec.tensor_scalar(gdn["u1"], gdn["e"], 1.0, None, ALU.add))
        link(vec.tensor_scalar(gdn["g"], gdn["u1"], -1.0, None, ALU.add))
        link(vec.tensor_tensor(gdn["g"], gdn["e"], gdn["g"], ALU.subtract))
        link(vec.reciprocal(gdn["u1"], gdn["u1"]))
        link(vec.tensor_tensor(gdn["g"], gdn["g"], gdn["u1"], ALU.mult))
        link(vec.tensor_tensor(gdn["g"], gdn["g"], gdn["l"], ALU.add))
        link(vec.scalar_tensor_tensor(out=gdn["z"], in0=gdn["z"], scalar=0.0, in1=gdn["g"], op0=ALU.max, op1=ALU.add))
        vec.wait_ge(*at("gdn_alog", 1))
        link(vec.scalar_tensor_tensor(out=by_tile(gsm("g")), in0=by_tile(gsm("z")), scalar=-1.0,
                                      in1=gdn["decay"].to_broadcast([P, NT, 4]), op0=ALU.mult, op1=ALU.mult), "gdn_g")
        vec.wait_ge(*at("conv0", 1))
        for j in range(1, 4):
            for i in range(12):
                ins = vec.scalar_tensor_tensor(out=gdn["conv"][:, i, :], in0=gdn["in"][:, i, 1 + j:T + 1 + j], scalar=vc("gdn_conv", 12 * j + i),
                                               in1=gdn["conv"][:, i, :], op0=ALU.mult, op1=ALU.add)
            link(ins, "conv_sum" if j == 3 else None)
        vec.wait_ge(*at("qk_sum", 1))
        for j in range(4):
            ins = vec.tensor_scalar(gdn["sq"][:, 2 * j:2 * j + 2, :], ps[:, 4 + j, :].rearrange("p (h t) -> p h t", h=2), EPS, None, ALU.add)
        link(ins, "qk_eps")
        vec.wait_ge(*at("gdn_cum", 1))
        link(vec.tensor_copy(gsm("cum"), ps[:, 0, 0:8]), "gdn_cum_out")
        vec.wait_ge(*at("qk_root", 1))
        link(vec.reciprocal(gdn["sq"], gdn["sq"]))
        q4, k4 = gdn["conv"][:, 0:4, :], gdn["conv"][:, 4:8, :]
        link(vec.scalar_tensor_tensor(out=q4, in0=q4, scalar=HD ** -0.5, in1=gdn["sq"][:, 0:4, :], op0=ALU.mult, op1=ALU.mult), "qk_norm")
        link(vec.tensor_tensor(k4, k4, gdn["sq"][:, 4:8, :], ALU.mult), "qk_norm")
        vec.wait_ge(*at("gdn_rows", 1))
        vec.wait_ge(*at("turn_act", turn_taken(len(TURNS) - 1)[1]))
        for j in range(2):
            ins = vec.tensor_copy(flat("rows")[:, NB * j:NB * (j + 1)], ps[:, 2 + j, :])
        link(ins, "gdn_rows_out")
        for t in range(2):
            link(vec.tensor_tensor(gdn["kb"][:, :, P * t:P * (t + 1)], gdn["conv"][:, 4:8, P * t:P * (t + 1)],
                                   ps[:, 4 + t, :].rearrange("p (h t) -> p h t", h=4), ALU.mult), "kb_out")
        for n in range(8):
            ins = vec.tensor_scalar(gdn["dT"][:, n, :], gdn["rows"][:, n, :], gsm("cum")[:, n:n + 1], 0.0, ALU.subtract, ALU.min)
        for c2 in range(2):
            r = slice(CH * c2, CH * (c2 + 1))
            ins = vec.tensor_tensor(gdn["fac"][r, c2, :], gdn["rows"][r, :, CH * c2 + CH - 1], gsm("cum")[r, :], ALU.subtract)
        link(ins, "gdn_diff")
        vec.wait_ge(*at("gdn_ecum", 1))
        link(vec.tensor_tensor(gdn["u1"], gdn["beta"], gdn["ecum"], ALU.mult), "gdn_bg")
        vec.wait_ge(*at("gdn_dT", 1))
        wide = lambda name: tb(name).unsqueeze(1).to_broadcast([P, 8, P])
        link(vec.tensor_tensor(gdn["dT"], gdn["dT"], wide("tri_chunk"), ALU.mult))
        vec.wait_ge(*at("gdn_kk", 1))
        for j in range(2):
            r = slice(NB * j, NB * (j + 1))
            vec.tensor_tensor(flat("attnT")[:, r], ps[:, 6 + j, :], flat("dT")[:, r], ALU.mult)
            ins = vec.tensor_tensor(flat("LT")[:, r], ps[:, 4 + j, :], flat("dT")[:, r], ALU.mult)
        link(ins, "attn_out")
        link(vec.tensor_tensor(gdn["LT"], gdn["LT"], wide("strict_chunk"), ALU.mult))
        link(vec.tensor_tensor(gdn["off"], gdn["LT"], wide("level1"), ALU.mult))
        link(vec.tensor_tensor(gdn["invT"], wide("ident"), gdn["off"], ALU.subtract), "invT_out")
        vec.wait_ge(*at("v_turned", 1))
        for n in range(8):
            ins = vec.tensor_scalar(gdn["v_b"][:, n, :], ps[:, 2 + n // 4, P * (n % 4):P * (n % 4 + 1)], gsm("beta")[:, n:n + 1], None, ALU.mult)
        link(ins, "v_scaled")
        vec.wait_ge(*at("gdn_erows", 1))
        for t in range(2):
            r = slice(P * t, P * (t + 1))
            link(vec.tensor_tensor(gdn["conv"][:, 0:4, r], gdn["conv"][:, 0:4, r], gdn["erows"][:, 4 * t:4 * t + 4, :], ALU.mult), "q_decayed")
        for lv in range(1, len(LEVELS)):
            link(vec.tensor_tensor(gdn["off"], gdn["LT"], wide(f"level{LEVELS[lv]}"), ALU.mult), "inv_off")
            if lv < len(LEVELS) - 1:
                vec.wait_ge(*at("inv_delta", lv))
            vec.wait_ge(*at("invT_delta", lv))
            for j in range(2):
                r = slice(NB * j, NB * (j + 1))
                ins = vec.tensor_tensor(flat("invT")[:, r], flat("invT")[:, r], ps[:, j, :], ALU.subtract)
            link(ins, "invT_out")
            if lv < len(LEVELS) - 1:
                for j in range(2):
                    r = slice(NB * j, NB * (j + 1))
                    ins = vec.tensor_tensor(flat("inv")[:, r], flat("inv")[:, r], ps[:, 6 + j, :], ALU.subtract)
                link(ins, "inv_new")
        vec.wait_ge(*at("gdn_w", 1))
        for j in range(2):
            ins = vec.tensor_copy(flat("u")[:, NB * j:NB * (j + 1)], ps[:, 4 + j, :])
        link(ins, "gdn_u_out")
        for c in range(4):
            t, c2 = c // 2, c % 2
            if c > 0:
                vec.wait_ge(*at("gdn_ws", c))
                link(vec.tensor_tensor(flat("new"), flat("u")[:, NB * t:NB * (t + 1)], ps[:, 4, :], ALU.subtract), "gdn_new")
            if c < 3:
                vec.wait_ge(*at("gdn_dstate", c + 1))
                vec.wait_ge(*at("gdn_o", c + 1))
                for h in range(4):
                    st, ds = gdn["state"][:, h, :], ps[:, 5, P * h:P * (h + 1)]
                    if c == 0:
                        ins = vec.tensor_copy(st, ds)
                    else:
                        last = CH * c2 + CH - 1
                        ins = vec.scalar_tensor_tensor(out=st, in0=st, scalar=gdn["erows"][:, 4 * t + h, last:last + 1], in1=ds, op0=ALU.mult, op1=ALU.add)
                link(ins, "gdn_state")
        head_norm(1, gdn["sq"].rearrange("p a b -> p (a b)")[:, 0:1024], gdn["gate"], "gdn_norm", 4)
        vec.memset(stat[:, 13:14], 0.0).then_inc(sem("gate_free"), 1)
        vec.memset(stat[:, 12:13], 0.0).then_inc(sem("up_free"), 1)
        vec.memset(stat[:, 11:12], 0.0).then_inc(sem("ffn_credit"), 1)

        def residual_add(blk, ev, gate):
            for i in range(4):
                r = slice(NB * i, NB * (i + 1))
                vec.wait_ge(*at("unit_used", SLOTS * (blk + i + 1)))
                if gate is not None:
                    link(vec.tensor_tensor(ffn["y2"][:, 1, :], ps[:, 2 * (i % 2) + 1, :], gate[:, r], ALU.mult), "evac_vec")
                    link(vec.tensor_tensor(x[:, 1, r], x[:, 1, r], ffn["y2"][:, 1, :], ALU.add))
                else:
                    link(vec.tensor_tensor(x[:, 1, r], x[:, 1, r], ps[:, 2 * (i % 2) + 1, :], ALU.add), "evac_vec")
                vec.wait_ge(*at("evac_act", ev + i + 3))
                y = ffn["y"][:, 0, :]
                if gate is not None:
                    y = ffn["y2"][:, 0, :]
                    link(vec.tensor_tensor(y, ffn["y"][:, 0, :], gate[:, r], ALU.mult))
                link(vec.tensor_tensor(x[:, 0, r], x[:, 0, r], y, ALU.add), "added")

        link.n["evac_vec"] = EVB["out1"] + 2
        vec.wait_ge(*at("gate_out", 4))
        residual_add(BLK["out1"], EVB["out1"], gates[:, 0, :])
        link(vec.memset(stat[:, 10:11], 0.0), "x_done")
        norm(1)
        norm_cols(1, mod_col[:, 48:64], mod_col[:, 32:48])
        with vec.Fori(0, 11) as i:
            link.begin(i, vec_chain=1, gate_free=1, up_free=1)
            vec.wait_ge(*at("conv_tap2", i * 4 + 4))
            for f in range(4):
                ins = vec.scalar_tensor_tensor(out=ffn["gate"][:, f, 1:T], in0=ps[:, f, 0:T - 1], scalar=vcols[:, 1, bass.ds(i * 4 + (44 + f), 1)],
                                               in1=ffn["gate"][:, f, 1:T], op0=ALU.mult, op1=ALU.add)
            link(ins)
            for f in range(4):
                ins = vec.scalar_tensor_tensor(out=ffn["gate"][:, f, 2:T], in0=ps[:, f, 0:T - 2], scalar=vcols[:, 1, bass.ds(i * 4 + f, 1)],
                                               in1=ffn["gate"][:, f, 2:T], op0=ALU.mult, op1=ALU.add)
            link(ins, "gate_free", wait=False)
            vec.wait_ge(*at("gate_silu", i + 1))
            vec.wait_ge(*at("unit_used", i * 8 + SLOTS * (BLK["up"] + 2)))
            link(vec.tensor_tensor(act_store[:, bass.ds(i * 4, 4), :], ffn["gate"], ps[:, 4:8, 0:T], ALU.mult), "up_free", wait=False)
        link.end(11)
        vec.wait_ge(*at("unit_used", SLOTS * (BLK["down"] + DOWN)))
        for n in range(4):
            r = slice(NB * n, NB * (n + 1))
            for t in range(NT):
                ins = vec.tensor_tensor(ffn["y2"][:, t, :], ps[:, 2 * n + t, :], gates[:, 1, r], ALU.mult)
            link(ins)
            link(vec.tensor_tensor(x[:, :, r], x[:, :, r], ffn["y2"], ALU.add), "x_done" if n == 3 else None)
        norm(2, scaled=False)
        vec.wait_ge(*at("norm_in", 16))
        for t in range(NT):
            ins = vec.scalar_tensor_tensor(out=x[:, t], in0=x[:, t], scalar=stat[:, 6 + t:7 + t], in1=gates[:, 0, :], op0=ALU.mult, op1=ALU.mult)
        link(ins, "x_done")
        norm(3)
        norm_cols(2, vc("attn_norm", 0, 16), None)
        evac(BLK["in2"], 6, p2, W2 - 6 * NB)
        for k, name in enumerate(("att_exp", "att_turned", "att_pT", "att_pv", "att_out")):
            vec.memset(stat[:, 17 + k:18 + k], 0.0).then_inc(sem(name), 1)
        link.n["att_out"] = 1
        vec.wait_ge(*at("evac_act", EVB["out2"] + 2))
        vec.wait_ge(*at("evac_vec", EVB["out2"] + 2))
        for i, col in enumerate(TWICE):
            for t in range(NT):
                src = p2[:, t, col:col + 2 * DK].rearrange("p (g d) -> p g d", g=2).unsqueeze(2).to_broadcast([P, 2, 2, DK])
                ins = vec.tensor_copy(kv_twice[:, 4 * i + 2 * t:4 * i + 2 * t + 2, :].rearrange("p g (c d) -> p g c d", c=2), src)
        link(ins, "kv_twice")
        vec.memset(hyb["v"], 0.0)
        vec.memset(hyb["v_cmp"], 0.0)
        link(vec.memset(hyb["q"], 0.0), "q_zero")
        for kind in range(3):
            for t in range(NT):
                ins = vec.tensor_copy(hyb["v"][:, kind, 2 * t:2 * t + 2, DK:2 * DK], p2[:, t, VCOL[kind]:VCOL[kind] + 2 * DK].rearrange("p (g d) -> p g d", g=2))
        link(ins)
        for m in range(2):
            vec.wait_ge(*at("kv_turned", m + 1))
            src = ps[:, m, :].rearrange("p (g t) -> p g t", g=2)
            link(vec.tensor_copy(hyb["xk"][0:DK, 2 * m:2 * m + 2, :], src[0:DK]), "xk")
            link(vec.tensor_copy(hyb["xk"][DK:P, 2 * m:2 * m + 2, 0:T - 1], src[DK:P, :, 1:T]), "xk")
        for kind in range(3):
            vec.wait_ge(*at("kv_turned", kind + 3))
            ins = vec.tensor_copy(hyb["kT"][:, 2 * kind:2 * kind + 2, :], ps[:, 4 + kind, :].rearrange("p (g t) -> p g t", g=2))
        for m in range(2):
            vec.wait_ge(*at("cmp_hid", m + 1))
            link(vec.tensor_copy(hst["hb"][:, 0, m:m + 1], ps[:, 7, m:m + 1]), "cmp_hb")
        vec.wait_ge(*at("cmp_kv", 1))
        vec.tensor_copy(hyb["kc"], ps[:, 0, 0:30].rearrange("p (g c) -> p g c", g=2))
        link(vec.tensor_copy(hyb["v_cmp"][0:NCMP, :, DK:2 * DK], ps[0:NCMP, 1, 0:P].rearrange("p (g d) -> p g d", g=2)), "kv_out")
        vec.wait_ge(*at("gate_sig", 2))
        for t in range(NT):
            link(vec.tensor_scalar(hst["gate"][:, 3 * t, :], hst["gate"][:, 3 * t, :], tb("cmp_valid")[:, t:t + 1], None, ALU.mult))

        def row_max(i, g, u):
            t, br = UNITS[u % NU]
            n = {"cmp": (7, 15)[t]}.get(br, P * (t + 1))
            vec.wait_ge(*at("att_score", i * NU + (4 * NU * g + u + 1)))
            m = hst["max"][:, u % NU, :]
            link(vec.tensor_reduce(m, ps[:, u % 4, :].rearrange("p (h k) -> p h k", h=2)[:, :, 0:n], X_AXIS, ALU.max))
            if br == "ban":
                sink = small[:, bass.ds(i * 2 + (2 * (u // NU) + 12 + 8 * g), 2)]
                link(vec.tensor_tensor(m, m, sink, ALU.max))
                link(vec.tensor_tensor(hst["sink"][:, u % NU, :], sink, m, ALU.subtract))
            link(vec.tensor_scalar(m, m, -1.0, None, ALU.mult), "att_max")

        def weigh(i, g, u):
            t, br = UNITS[u % NU]
            n = {"cmp": (7, 15)[t]}.get(br, P * (t + 1))
            vec.wait_ge(*at("att_exp", i * NU + (4 * NU * g + u + 2)))
            s = hst["sum"][:, u % NU, :]
            if br == "ban":
                link(vec.tensor_tensor(s, s, hst["esink"][:, u % NU, :], ALU.add))
            link(vec.reciprocal(s, s))
            if br != "ban":
                gate = hst["gate"][:, 3 * t + ("cmp", "slc", "win").index(br), bass.ds(i * 2 + 8 * g, 2)]
                link(vec.tensor_tensor(s, s, gate, ALU.mult))
            p = hyb["p"][:, u % 2, :, 0:n]
            link(vec.tensor_tensor(p, p, s.unsqueeze(2).to_broadcast([P, 2, n]), ALU.mult), "att_p", wait=False)

        nb = UNITS.count((0, "ban")) + UNITS.count((1, "ban"))
        def q_in(i, g):
            if g or not isinstance(i, int):
                vec.wait_ge(*at("q_turned", i + 4 * g))
            for k, col in enumerate((QA, QB)):
                ins = vec.tensor_copy(hyb["q_in"][:, k], p2[:, :, bass.ds(i * P + (col + 512 * g), P)])
            link(ins, "q_in")

        def head_pair(i, g, more):
            for u in range(NU):
                weigh(i, g, u)
                if u + 2 < NU or more:
                    row_max(i, g, u + 2)
                if u == 2 and more:
                    q_in(i + 1, g)
            for k, kind in enumerate("ab"):
                vec.wait_ge(*at("att_pv", i * NU + (4 * NU * g + OUT_AT[kind] + 1)))
                link(vec.tensor_copy(yT[:, bass.ds(i + (4 * g + 8 * k), 1), :], ps[:, 6 + k, 0:T].unsqueeze(1)), "att_out")

        for g in range(2):
            q_in(0, g)
            row_max(0, g, 0)
            row_max(0, g, 1)
            with vec.Fori(0, 3) as i:
                link.begin(i, vec_chain=NU + 2 * nb + NU + nb + (NU - nb), att_max=NU, att_p=NU, q_in=1, att_out=2)
                head_pair(i, g, True)
            link.end(3)
            head_pair(3, g, False)
        residual_add(BLK["out2"], EVB["out2"], None)
        link(vec.memset(stat[:, 22:23], 0.0), "x_done")
        link(vec.memset(stat[:, 24:25], 0.0), "wq_out")
        norm(4)
        norm_cols(3, vc("ffn_norm2", 0, 16), None)
        vec.wait_ge(*at("norm_in", 48))
        vec.wait_ge(*at("hT_turned", 32))
        for t in range(NT):
            ins = vec.tensor_tensor(xs[:, t], xs[:, t], gates[:, 0, :], ALU.mult)
        link(ins)
        vec.wait_ge(*at("keys_turned", 1))
        link(vec.tensor_copy(peer["keysT"], ps[:, 4, 0:2 * P].rearrange("p (s n) -> p s n", s=2)), "keys_out")

        def top16(n, scores, values, places):
            for half in range(2):
                r = slice(8 * half, 8 * half + 8)
                for c in range(n):
                    ins = vec.max(out=values(c)[:, r], in_=scores(c))
                link(ins)
                for c in range(n):
                    ins = vec.max_index(out=places(c)[:, r], in_max=values(c)[:, r], in_values=scores(c))
                link(ins)
                if half == 0:
                    for c in range(n):
                        ins = vec.match_replace(out=scores(c), in_to_replace=values(c)[:, r], in_values=scores(c), imm_value=-3.0e38)
                    link(ins)

        side = lambda t, c: SIDES * t + c
        head = lambda t, h: HEADS * t + h

        def choose_sides(t, cs):
            top16(len(cs), lambda n: peer["score"][:, t, cs[n], :], lambda n: choice[t]["val"][:, cs[n], :], lambda n: at_u[:, side(t, cs[n]), :])

        def halves(name, t):
            return choice[t][name].rearrange("p (h s) n -> p h s n", s=2)

        def add_sides(t):
            mine = slice(SIDES * t, SIDES * (t + 1))
            link(vec.tensor_copy(choice[t]["at_f"], at_u[:, mine, :]))
            val = halves("val", t)
            wide = [P, HEADS, TOP, TOP]
            sums = peer["sum"][:, t].rearrange("p h (i j) -> p h i j", i=TOP)
            link(vec.tensor_tensor(sums, val[:, :, 0, :].unsqueeze(3).to_broadcast(wide), val[:, :, 1, :].unsqueeze(2).to_broadcast(wide), ALU.add))

        def choose_sums(t, hs):
            top16(len(hs), lambda n: peer["sum"][:, t, hs[n], :], lambda n: peer["best"][:, head(t, hs[n]), :], lambda n: pick_u[:, head(t, hs[n]), :])

        def name_experts(t):
            mine = choice[t]
            place = halves("at_f", t)
            picks = pick_u[:, HEADS * t:HEADS * (t + 1), :].rearrange("p h k -> p (h k)")
            hot = mine["hot"].rearrange("p (h k) i -> p h k i", h=HEADS)
            for s, (op, arg, f, e) in enumerate(((ALU.logical_shift_right, 4, "hi_f", "e1"), (ALU.bitwise_and, 15, "lo_f", "e2"))):
                link(vec.tensor_scalar(part_u, picks, arg, None, op))
                link(vec.tensor_copy(mine[f][:, 0, :], part_u))
                full = [P, PICKS, TOP]
                link(vec.tensor_tensor(mine["hot"], mine[f][:, 0, :].unsqueeze(2).to_broadcast(full), tb("iota16").unsqueeze(1).to_broadcast(full), ALU.is_equal))
                link(vec.tensor_tensor(hot, hot, place[:, :, s, :].unsqueeze(2).to_broadcast([P, HEADS, TOP, TOP]), ALU.mult))
                link(vec.tensor_reduce(mine[e][:, 0, :], mine["hot"], X_AXIS, ALU.add))
            link(vec.scalar_tensor_tensor(out=mine["e1"][:, 0, :], in0=mine["e1"][:, 0, :], scalar=float(P), in1=mine["e2"][:, 0, :], op0=ALU.mult, op1=ALU.add))
            link(vec.tensor_copy(expert[:, t, :], mine["e1"][:, 0, :]), "experts")

        def pick_weights(t):
            best = peer["best"][:, HEADS * t:HEADS * (t + 1), :]
            weight = peer["weight"][:, t, :].rearrange("p (h k) -> p h k", h=HEADS)
            many = [P, HEADS, TOP]
            link(vec.tensor_tensor(weight, best, best[:, :, 0:1].to_broadcast(many), ALU.subtract))
            link(vec.tensor_copy(best, weight), "best_shift")
            vec.wait_ge(*at("best_exp", t + 1))
            total = peer["total"][:, 0, HEADS * t:HEADS * (t + 1)]
            link(vec.tensor_reduce(total, best, X_AXIS, ALU.add))
            link(vec.reciprocal(total, total))
            link(vec.tensor_tensor(weight, best, total.unsqueeze(2).to_broadcast(many), ALU.mult))

        def arrived(i, base, s):
            vec.wait_ge(*at(f"row{s % ROWS}", i * 32 + 16 * (base // ROWS + s // ROWS + 1)))

        for s in range(ROWS):
            link(vec.memset(stat[:, 25:26], 0.0), "row_used")
        def dot_rows(i, t):
            for s in range(16):
                arrived(i, PICKS * t, s)
                slot = row_slots[s % ROWS]
                link(vec.tensor_tensor_reduce(slot, slot, xs[:, t], 1.0, 0.0, ALU.mult, ALU.add, peer["h16"][:, 0, s:s + 1]), "row_used", wait=(s == 15))
            link(vec.tensor_copy(peer["h"][:, t, bass.ds(i * 16, 16)], peer["h16"][:, 0, :]))

        vec.wait_ge(*at("score_out", 4))
        choose_sides(0, range(SIDES))
        add_sides(0)
        choose_sums(0, range(HEADS))
        name_experts(0)
        pick_weights(0)
        for i in range(PICKS // 16):
            dot_rows(i, 0)
            if i == 0:
                vec.wait_ge(*at("score_out", 8))
            if i < 4:
                choose_sides(1, range(4 * i, 4 * i + 4))
            elif i == 4:
                add_sides(1)
                choose_sums(1, range(0, 4))
            elif i == 5:
                choose_sums(1, range(4, 8))
            elif i == 6:
                name_experts(1)
            else:
                pick_weights(1)
        link(vec.memset(stat[:, 26:27], 0.0), "h_done")
        with vec.Fori(0, PICKS // 16) as i:
            link.begin(i, vec_chain=1, row_used=16)
            dot_rows(i, 1)
        link.end(PICKS // 16)
        link(vec.memset(stat[:, 27:28], 0.0), "h_done")
        for t in range(NT):
            vec.wait_ge(*at("h_gelu", t + 1))
            link(vec.tensor_tensor(peer["weight"][:, t, :], peer["weight"][:, t, :], peer["h"][:, t, :], ALU.mult))
            with vec.Fori(0, PICKS // 16) as i:
                link.begin(i, row_used=16)
                for s in range(16):
                    arrived(i, PICKS * (NT + t), s)
                    link(vec.scalar_tensor_tensor(out=x[:, t], in0=row_slots[s % ROWS], scalar=peer["weight"][:, t, bass.ds(i * 16 + s, 1)], in1=x[:, t],
                                                  op0=ALU.mult, op1=ALU.add), "row_used")
            link.end(PICKS // 16)
        link(vec.memset(stat[:, 28:29], 0.0), "x_done")
        norm(5, scaled=False)
        for t in range(NT):
            link(vec.scalar_tensor_tensor(out=x[:, t], in0=x[:, t], scalar=stat[:, 6 + t:7 + t], in1=gates[:, 1, :], op0=ALU.mult, op1=ALU.mult), "out_row")
    ctx.close()


VECTORS = ("c", "b_mod", "norm_mix", "norm_ffn", "gla_b_lr", "gla_norm", "gdn_conv", "gdn_a_log", "gdn_dt_bias", "gdn_norm", "pool_scale", "fox_f_bias", "ffn_conv_w", "ffn_conv_b", "norm_final", "attn_norm_2",
           "cmp_pos_k_2", "cmp_pos_v_2", "sinks_2", "ffn_norm_2", "final_norm_2")


def kernel(**inputs):
    import concourse.bacc as bacc
    from concourse.bass_utils import run_bass_kernel_spmd

    nc = bacc.Bacc("TRN2", target_bir_lowering=False, num_devices=1)
    arrays, views = {}, {}
    for name, value in inputs.items():
        v = np.ascontiguousarray(value)
        shape = [n for n in v.shape if n != 1]
        if name in VECTORS:
            shape = [int(np.prod(v.shape))]
        arrays[f"in_{name}"] = v.reshape(shape)
    arrays["in_tab"] = TAB
    for name, v in arrays.items():
        views[name[3:]] = nc.dram_tensor(name, v.shape, mybir.dt.from_np(v.dtype), kind="ExternalInput").ap()
    out = nc.dram_tensor("out", (1, T, D), F32, kind="ExternalOutput").ap()
    scratch = nc.dram_tensor("bias_rows", (32, 384), F32, kind="Internal").ap()
    build(nc, views, out, scratch)
    got = run_bass_kernel_spmd(nc, [arrays], core_ids=[0]).results[0]
    return got["out"]
```
